# Optimizing a Trainium2 kernel written in Bass

```python
import math
import jax, jax.numpy as jnp
from jax import lax
import numpy as np

D_MODEL = 1024
BATCH = 1
SEQ = 1024
DEPTH = 1
DEC_BATCH = 8
DEC_SEQ = 4
PAST_LEN = 8192
PAGE_SIZE = 128

DN_HEADS = 4
DN_DK = 128
DN_DV = 128
DN_CONV = 4
DN_CHUNK = 64
GLA_HEADS = 4
GLA_DK = 64
GLA_DV = 128
GLA_GATE_RANK = 16
GLA_TAU = 16.0
GLA_CHUNK = 64
CONF_DIM = 512
CONF_WIDTH = 31
N_EXPERTS = 64
TOP_K = 8
N_GROUPS = 8
TOPK_GROUPS = 4
EXPERT_FF = 256
SHARED_FF = 256
ROUTE_SCALE = 2.5
MOE_BLOCK = 128
N_BRANCH = 3
BRANCH_DIM = 512
EPS = 1e-6

DN_QK = DN_HEADS * DN_DK
DN_V = DN_HEADS * DN_DV
DN_CONV_CH = 2 * DN_QK + DN_V
GLA_QK = GLA_HEADS * GLA_DK
GLA_V = GLA_HEADS * GLA_DV
IN_SIZES = (DN_CONV_CH, DN_V, DN_HEADS, DN_HEADS, GLA_QK, GLA_QK, GLA_V, GLA_V, GLA_GATE_RANK, 2 * CONF_DIM, N_BRANCH * D_MODEL)
IN_TOTAL = DN_CONV_CH + DN_V + 2 * DN_HEADS + 2 * GLA_QK + 2 * GLA_V + GLA_GATE_RANK + 2 * CONF_DIM + N_BRANCH * D_MODEL

kernel_name = "hybrid_deltanet_gla_conformer_moe_step"

F32 = jnp.float32

def rmsnorm(x, w):
    xf = x.astype(F32)
    y = xf * lax.rsqrt(jnp.mean(xf * xf, axis=-1, keepdims=True) + EPS)
    return (y * w.astype(F32)).astype(x.dtype)

def layernorm(x, w, b):
    xf = x.astype(F32)
    mu = jnp.mean(xf, axis=-1, keepdims=True)
    xc = xf - mu
    var = jnp.mean(xc * xc, axis=-1, keepdims=True)
    return (xc * lax.rsqrt(var + EPS) * w.astype(F32) + b.astype(F32)).astype(x.dtype)

def l2norm(x):
    xf = x.astype(F32)
    return xf * lax.rsqrt(jnp.sum(xf * xf, axis=-1, keepdims=True) + EPS)

def gated_rmsnorm(o, w, z):
    B_, L, H, d = o.shape
    zf = z.reshape(B_, L, H, d).astype(F32)
    y = o * lax.rsqrt(jnp.mean(o * o, axis=-1, keepdims=True) + EPS) * w.astype(F32) * jax.nn.silu(zf)
    return y.reshape(B_, L, H * d).astype(z.dtype)

def causal_dwconv(x, prev, w, b=None):
    xx = jnp.concatenate([prev.astype(x.dtype), x], axis=1)
    y = lax.conv_general_dilated(xx, w[:, None, :].astype(x.dtype), window_strides=(1,), padding='VALID',
                                 dimension_numbers=('NWC', 'WIO', 'NWC'), feature_group_count=x.shape[-1])
    if b is not None:
        y = y + b.astype(x.dtype)
    return y, xx[:, -(w.shape[0] - 1):]

def _to_chunks(x, C):
    B_, L = x.shape[:2]
    n = -(-L // C)
    x = jnp.pad(x, [(0, 0), (0, n * C - L)] + [(0, 0)] * (x.ndim - 2))
    x = x.reshape((B_, n, C) + x.shape[2:])
    return x.transpose((1, 0, 3, 2) + tuple(range(4, x.ndim)))

def _from_chunks(o, L):
    n, B_, H, C, d = o.shape
    return o.transpose(1, 0, 3, 2, 4).reshape(B_, n * C, H, d)[:, :L]

def gated_delta_rule(q, k, v, beta, g, S0):
    L = q.shape[1]
    dv = v.shape[-1]
    C = min(DN_CHUNK, L)
    qc, kc, vc = (_to_chunks(t.astype(F32), C) for t in (q, k, v))
    bc, gc = (_to_chunks(t.astype(F32), C) for t in (beta, g))
    G = jnp.cumsum(gc, axis=-1)
    idx = jnp.arange(C)
    incl = idx[:, None] >= idx[None, :]
    strict = idx[:, None] > idx[None, :]
    decay = jnp.exp(jnp.where(incl, G[..., :, None] - G[..., None, :], -jnp.inf))
    kb = kc * bc[..., None]
    M = jnp.einsum('nbhid,nbhjd->nbhij', kb, kc) * decay * strict
    eye = jnp.eye(C, dtype=F32)
    rhs = jnp.concatenate([vc * bc[..., None], kb * jnp.exp(G)[..., None]], axis=-1)
    uw = lax.linalg.triangular_solve(eye + M, rhs, left_side=True, lower=True, unit_diagonal=True)
    u, w = uw[..., :dv], uw[..., dv:]
    a_qk = jnp.einsum('nbhid,nbhjd->nbhij', qc, kc) * decay
    q_dec = qc * jnp.exp(G)[..., None]
    k_dec = kc * jnp.exp(G[..., -1:] - G)[..., None]
    g_last = jnp.exp(G[..., -1])

    def step(S, inp):
        u_i, w_i, a_i, qd_i, kd_i, gl_i = inp
        v_new = u_i - jnp.einsum('bhcd,bhde->bhce', w_i, S)
        o = jnp.einsum('bhcd,bhde->bhce', qd_i, S) + jnp.einsum('bhij,bhje->bhie', a_i, v_new)
        S = S * gl_i[..., None, None] + jnp.einsum('bhcd,bhce->bhde', kd_i, v_new)
        return S, o

    S, o = lax.scan(step, S0.astype(F32), (u, w, a_qk, q_dec, k_dec, g_last))
    return _from_chunks(o, L), S

def gla_recurrence(q, k, v, log_a, S0):
    L = q.shape[1]
    C = min(GLA_CHUNK, L)
    qc, kc, vc, ac = (_to_chunks(t.astype(F32), C) for t in (q, k, v, log_a))
    bcum = jnp.cumsum(ac, axis=-2)
    idx = jnp.arange(C)
    incl = (idx[:, None] >= idx[None, :])[:, :, None]

    def step(S, inp):
        q_i, k_i, v_i, b_i = inp
        dec = jnp.exp(jnp.where(incl, b_i[:, :, :, None, :] - b_i[:, :, None, :, :], -jnp.inf))
        a = jnp.einsum('bhid,bhjd,bhijd->bhij', q_i, k_i, dec)
        b_last = b_i[:, :, -1:, :]
        o = jnp.einsum('bhcd,bhde->bhce', q_i * jnp.exp(b_i), S) + jnp.einsum('bhij,bhje->bhie', a, v_i)
        S = S * jnp.exp(b_last[:, :, 0, :])[..., None] + jnp.einsum('bhcd,bhce->bhde', k_i * jnp.exp(b_last - b_i), v_i)
        return S, o

    S, o = lax.scan(step, S0.astype(F32), (qc, kc, vc, bcum))
    return _from_chunks(o, L), S

def swiglu(x, w_gate, w_up, w_down):
    return (jax.nn.silu(x @ w_gate) * (x @ w_up)) @ w_down

def moe(u, router_w, router_bias, exp_w_gate, exp_w_up, exp_w_down, sh_w_gate, sh_w_up, sh_w_down):
    T, D = u.shape
    s = jax.nn.sigmoid(jnp.dot(u.astype(F32), router_w.astype(F32)))
    sb = s + router_bias.astype(F32)
    grp_score = jnp.sum(lax.top_k(sb.reshape(T, N_GROUPS, N_EXPERTS // N_GROUPS), 2)[0], axis=-1)
    _, gsel = lax.top_k(grp_score, TOPK_GROUPS)
    gmask = jnp.sum(jax.nn.one_hot(gsel, N_GROUPS, dtype=F32), axis=-2) > 0
    emask = jnp.repeat(gmask, N_EXPERTS // N_GROUPS, axis=-1)
    _, eidx = lax.top_k(jnp.where(emask, sb, -jnp.inf), TOP_K)
    gw = jnp.take_along_axis(s, eidx, axis=-1)
    gw = gw / jnp.sum(gw, axis=-1, keepdims=True) * ROUTE_SCALE
    P = T * TOP_K
    NB = -(-P // MOE_BLOCK) + N_EXPERTS
    flat_e = eidx.reshape(-1)
    flat_t = jnp.repeat(jnp.arange(T, dtype=jnp.int32), TOP_K)
    order = jnp.argsort(flat_e)
    se = flat_e[order]
    counts = jnp.bincount(flat_e, length=N_EXPERTS)
    start = jnp.cumsum(counts) - counts
    pcounts = (counts + MOE_BLOCK - 1) // MOE_BLOCK * MOE_BLOCK
    pend = jnp.cumsum(pcounts)
    pstart = pend - pcounts
    dest = pstart[se] + jnp.arange(P) - start[se]
    buf_t = jnp.full((NB * MOE_BLOCK,), T, jnp.int32).at[dest].set(flat_t[order])
    buf_w = jnp.zeros((NB * MOE_BLOCK,), u.dtype).at[dest].set(gw.reshape(-1)[order].astype(u.dtype))
    block_e = jnp.minimum(jnp.searchsorted(pend, jnp.arange(NB) * MOE_BLOCK, side='right'), N_EXPERTS - 1)
    u_pad = jnp.concatenate([u, jnp.zeros((1, D), u.dtype)], axis=0)
    xb = u_pad[buf_t].reshape(NB, MOE_BLOCK, D)

    def expert_block(args):
        xblk, e = args
        return swiglu(xblk, exp_w_gate[e], exp_w_up[e], exp_w_down[e])

    yb = lax.map(expert_block, (xb, block_e)).reshape(NB * MOE_BLOCK, D) * buf_w[:, None]
    routed = jnp.zeros_like(u_pad).at[buf_t].add(yb)[:T]
    return routed + swiglu(u, sh_w_gate, sh_w_up, sh_w_down)

def _layer(x, c, dn_S0, dn_conv0, gla_S0, conf0,
           ada_w, ada_b, norm_mix_w, w_in, dn_conv_w, dn_A_log, dn_dt_bias, dn_norm_w,
           gla_gate_w, gla_gate_b, gla_norm_w, conf_dw_w, conf_dw_b, conf_ln_w, conf_ln_b,
           w_branch, w_out, norm_ffn_w, router_w, router_bias, exp_w_gate, exp_w_up, exp_w_down,
           sh_w_gate, sh_w_up, sh_w_down):
    B_, L, D = x.shape
    mod = jnp.dot(jax.nn.silu(c), ada_w) + ada_b
    sh1, sc1, gt1, sh2, sc2, gt2 = (m[:, None, :] for m in jnp.split(mod, 6, axis=-1))
    h = rmsnorm(x, norm_mix_w) * (1 + sc1) + sh1
    splits = [int(i) for i in np.cumsum(IN_SIZES)[:-1]]
    (dn_qkv, dn_z, dn_b, dn_a, gq, gk, gv, gr, glr, conf_in, br_g) = jnp.split(h @ w_in, splits, axis=-1)

    qkv, dn_conv = causal_dwconv(dn_qkv, dn_conv0, dn_conv_w)
    qkv = jax.nn.silu(qkv)
    q, k, v = jnp.split(qkv, [DN_QK, 2 * DN_QK], axis=-1)
    q = l2norm(q.reshape(B_, L, DN_HEADS, DN_DK)) * (DN_DK ** -0.5)
    k = l2norm(k.reshape(B_, L, DN_HEADS, DN_DK))
    v = v.reshape(B_, L, DN_HEADS, DN_DV)
    beta = jax.nn.sigmoid(dn_b.astype(F32))
    g = -jnp.exp(dn_A_log.astype(F32)) * jax.nn.softplus(dn_a.astype(F32) + dn_dt_bias.astype(F32))
    o_a, dn_S = gated_delta_rule(q, k, v, beta, g, dn_S0)
    o_a = gated_rmsnorm(o_a, dn_norm_w, dn_z)

    log_a = jax.nn.log_sigmoid((glr @ gla_gate_w + gla_gate_b).astype(F32)) / GLA_TAU
    o_b, gla_S = gla_recurrence((gq * (GLA_DK ** -0.5)).reshape(B_, L, GLA_HEADS, GLA_DK),
                                gk.reshape(B_, L, GLA_HEADS, GLA_DK),
                                gv.reshape(B_, L, GLA_HEADS, GLA_DV),
                                log_a.reshape(B_, L, GLA_HEADS, GLA_DK), gla_S0)
    o_b = gated_rmsnorm(o_b, gla_norm_w, gr)

    ca, cg = jnp.split(conf_in, 2, axis=-1)
    cv, conf = causal_dwconv(ca * jax.nn.sigmoid(cg), conf0, conf_dw_w, conf_dw_b)
    o_c = jax.nn.silu(layernorm(cv, conf_ln_w, conf_ln_b))

    branches = jnp.stack([o_a, o_b, o_c], axis=2)
    yb = jnp.einsum('blnc,ncd->blnd', branches, w_branch)
    gates = jax.nn.sigmoid(br_g.reshape(B_, L, N_BRANCH, D))
    merged = jnp.sum(gates * yb, axis=2)
    x = x + gt1 * (merged @ w_out)

    u = rmsnorm(x, norm_ffn_w) * (1 + sc2) + sh2
    y = moe(u.reshape(B_ * L, D), router_w, router_bias, exp_w_gate, exp_w_up, exp_w_down,
            sh_w_gate, sh_w_up, sh_w_down).reshape(B_, L, D)
    x = x + gt2 * y
    return x, dn_S.astype(dn_S0.dtype), dn_conv, gla_S.astype(gla_S0.dtype), conf

def setup_inputs(seed: int = 0) -> dict:
    key = jax.random.key(seed)
    ks = iter(jax.random.split(key, 48))
    D = D_MODEL

    def nrm(shape, scale):
        return jax.random.normal(next(ks), shape, F32) * scale

    def gain(shape):
        return 1.0 + nrm(shape, 0.02)

    dt = jnp.exp(jax.random.uniform(next(ks), (DEPTH, DN_HEADS), F32, math.log(1e-3), math.log(1e-1)))
    return {
        "x_prompt": nrm((BATCH, SEQ, D), 1.0),
        "x_sample": nrm((DEC_BATCH, DEC_SEQ, D), 1.0),
        "state_delta": nrm((DEPTH, DEC_BATCH, DN_HEADS, DN_DK, DN_DV), DN_DK ** -0.5),
        "state_delta_conv": nrm((DEPTH, DEC_BATCH, DN_CONV - 1, DN_CONV_CH), 1.0),
        "state_gla": nrm((DEPTH, DEC_BATCH, GLA_HEADS, GLA_DK, GLA_DV), 0.5),
        "state_conv": nrm((DEPTH, DEC_BATCH, CONF_WIDTH - 1, CONF_DIM), 0.5),
        "c_prompt": nrm((BATCH, D), 1.0),
        "c_sample": nrm((DEC_BATCH, D), 1.0),
        "ada_w": nrm((DEPTH, D, 6 * D), 0.3 * D ** -0.5),
        "ada_b": nrm((DEPTH, 6 * D), 0.02),
        "norm_mix_w": gain((DEPTH, D)),
        "w_in": nrm((DEPTH, D, IN_TOTAL), D ** -0.5),
        "dn_conv_w": nrm((DEPTH, DN_CONV, DN_CONV_CH), DN_CONV ** -0.5),
        "dn_A_log": jnp.log(jax.random.uniform(next(ks), (DEPTH, DN_HEADS), F32, 1.0, 16.0)),
        "dn_dt_bias": dt + jnp.log(-jnp.expm1(-dt)),
        "dn_norm_w": gain((DEPTH, DN_DV)),
        "gla_gate_w": nrm((DEPTH, GLA_GATE_RANK, GLA_QK), GLA_GATE_RANK ** -0.5),
        "gla_gate_b": nrm((DEPTH, GLA_QK), 0.1),
        "gla_norm_w": gain((DEPTH, GLA_DV)),
        "conf_dw_w": nrm((DEPTH, CONF_WIDTH, CONF_DIM), CONF_WIDTH ** -0.5),
        "conf_dw_b": nrm((DEPTH, CONF_DIM), 0.02),
        "conf_ln_w": gain((DEPTH, CONF_DIM)),
        "conf_ln_b": nrm((DEPTH, CONF_DIM), 0.02),
        "w_branch": nrm((DEPTH, N_BRANCH, BRANCH_DIM, D), BRANCH_DIM ** -0.5),
        "w_out": nrm((DEPTH, D, D), D ** -0.5),
        "norm_ffn_w": gain((DEPTH, D)),
        "router_w": nrm((DEPTH, D, N_EXPERTS), D ** -0.5),
        "router_bias": nrm((DEPTH, N_EXPERTS), 0.01),
        "exp_w_gate": nrm((DEPTH, N_EXPERTS, D, EXPERT_FF), D ** -0.5),
        "exp_w_up": nrm((DEPTH, N_EXPERTS, D, EXPERT_FF), D ** -0.5),
        "exp_w_down": nrm((DEPTH, N_EXPERTS, EXPERT_FF, D), EXPERT_FF ** -0.5),
        "sh_w_gate": nrm((DEPTH, D, SHARED_FF), D ** -0.5),
        "sh_w_up": nrm((DEPTH, D, SHARED_FF), D ** -0.5),
        "sh_w_down": nrm((DEPTH, SHARED_FF, D), SHARED_FF ** -0.5),
        "final_norm_w": gain((D,)),
    }

def reference(x_prompt, x_sample, state_delta, state_delta_conv, state_gla, state_conv,
              c_prompt, c_sample, ada_w, ada_b, norm_mix_w, w_in, dn_conv_w, dn_A_log,
              dn_dt_bias, dn_norm_w, gla_gate_w, gla_gate_b, gla_norm_w, conf_dw_w,
              conf_dw_b, conf_ln_w, conf_ln_b, w_branch, w_out, norm_ffn_w, router_w,
              router_bias, exp_w_gate, exp_w_up, exp_w_down, sh_w_gate, sh_w_up, sh_w_down,
              final_norm_w):
    def run(x, c, dn_S0, dn_conv0, gla_S0, conf0):
        new = ([], [], [], [])
        for l in range(DEPTH):
            x, *st = _layer(x, c, dn_S0[l], dn_conv0[l], gla_S0[l], conf0[l],
                            ada_w[l], ada_b[l], norm_mix_w[l], w_in[l], dn_conv_w[l], dn_A_log[l],
                            dn_dt_bias[l], dn_norm_w[l], gla_gate_w[l], gla_gate_b[l], gla_norm_w[l],
                            conf_dw_w[l], conf_dw_b[l], conf_ln_w[l], conf_ln_b[l], w_branch[l],
                            w_out[l], norm_ffn_w[l], router_w[l], router_bias[l], exp_w_gate[l],
                            exp_w_up[l], exp_w_down[l], sh_w_gate[l], sh_w_up[l], sh_w_down[l])
            for lst, s in zip(new, st):
                lst.append(s)
        return rmsnorm(x, final_norm_w), [jnp.stack(s) for s in new]

    bp = x_prompt.shape[0]

    def zeros_like_state(ref):
        return jnp.zeros((DEPTH, bp) + ref.shape[2:], ref.dtype)

    y_prompt, (p_dn_S, p_dn_conv, p_gla_S, p_conf) = run(
        x_prompt, c_prompt, zeros_like_state(state_delta), zeros_like_state(state_delta_conv),
        zeros_like_state(state_gla), zeros_like_state(state_conv))
    y_sample, (s_dn_S, s_dn_conv, s_gla_S, s_conf) = run(
        x_sample, c_sample, state_delta, state_delta_conv, state_gla, state_conv)
    return (y_prompt, y_sample, p_dn_S, p_dn_conv, p_gla_S, p_conf, s_dn_S, s_dn_conv, s_gla_S, s_conf)


_drawn_inputs = setup_inputs


def setup_inputs(seed=0):
    import zlib

    import numpy as np

    out = dict(_drawn_inputs(seed))
    spreads = {}
    factors = {'dn_norm_w': 8.0,
     'gla_norm_w': 8.0,
     'conf_dw_b': 8.0,
     'conf_ln_w': 8.0,
     'conf_ln_b': 8.0,
     'norm_ffn_w': 3.484,
     'final_norm_w': 2.849}
    for name, (base, spread) in spreads.items():
        noise = np.random.default_rng([zlib.crc32(name.encode()), seed]).standard_normal(out[name].shape)
        drawn = base * np.exp(spread * noise) if base else spread * noise
        out[name] = __import__('jax').numpy.asarray(drawn.astype(out[name].dtype))
    for name, factor in factors.items():
        out[name] = (out[name] * factor).astype(out[name].dtype)
    return out
```

```python
from contextlib import ExitStack

import concourse.bass as bass
from concourse import mybir

F32 = mybir.dt.float32
ACT = mybir.ActivationFunctionType
ALU = mybir.AluOpType
AX = mybir.AxisListType

P = 128
D = 1024
KT = D // P
SEQ = 1024
SB, SL = 8, 4
NS = SB * SL
T = SEQ + NS
NCH = 3
CW = T // NCH
C = 128
NC = SEQ // C
H = 4
LEVELS = 7
DNK, DNC = 3, 12
GDK = 64
CFK, CFC = 30, 4
NSEQ = 1 + SB
E_N, FF = 64, 256
EPS = 1e-6
COL = dict(qkv=0, z=1536, ba=2048, gqk=2056, gv=2568, gr=3080, glr=3592, conf=3608, br=4632)
RB, RG, RT, RE = 0, 32, 64, 96

PRM = {}
_at = 0
for _name, _n in (("ada_b", 48), ("norm_mix_w", 8), ("norm_ffn_w", 8), ("final_norm_w", 8), ("conf_dw_b", 4),
                  ("conf_ln_w", 4), ("conf_ln_b", 4), ("dn_norm_w", 1), ("gla_norm_w", 1), ("gla_gate_b", 2)):
    PRM[_name] = _at
    _at += _n
N_PRM = _at


class Area:

    def __init__(self, ap):
        self.ap, self.at, self.size = ap, 0, ap.shape[1]

    def take(self, *shape):
        n = 1
        for s in shape:
            n *= s
        piece = self.ap[:, self.at:self.at + n]
        self.at += n
        assert self.at <= self.size, (self.at, self.size)
        if len(shape) == 1:
            return piece
        names = "abcd"[:len(shape)]
        return piece.rearrange(f"p ({' '.join(names)}) -> p {' '.join(names)}", **dict(zip(names, shape)))


class Steps:

    def __init__(self, eng, sem):
        self.eng, self.sem, self.n, self.base = eng, sem, 0, 0

    def loop(self, i, per):
        self.base, self.first, self.per = self.n + i * per, self.n, per
        self.n = 0

    def end(self, count):
        assert self.n == self.per, (self.n, self.per)
        self.n, self.base = self.first + self.per * count, 0

    def done(self, ins):
        ins.then_inc(self.sem, 1)
        self.n += 1

    def wait(self):
        self.eng.wait_ge(self.sem, self.base + self.n)

    def __call__(self, ins):
        self.done(ins)
        self.wait()


def chunks(ap):
    return ap.rearrange("p (c w) -> p c w", c=NCH)


def wait_before_addressed(eng, sem, value, passed):
    eng.wait_ge(sem, value)
    eng.sem_inc(passed, 1)


def bcast(ap, *shape):
    return ap.to_broadcast([ap.shape[0], *shape])


def samples(ap):
    return ap[:, SEQ:T].rearrange("p (s l) -> p s l", l=SL)


class Core:
    def __init__(self, nc, ctx, a):
        self.nc, self.ctx, self.a = nc, ctx, a
        self.sems = []
        sb = lambda name, *shape: ctx.enter_context(nc.sbuf_tensor(name, [P, *shape], F32))
        self.xT = sb("xT", KT, T)
        self.hT = sb("hT", KT, T)
        self.oT = sb("oT", 12, T)
        self.ident = sb("ident", P)
        self.ones = sb("ones", P)
        self.pair = sb("pair", LEVELS + 1, C)
        self.causal = sb("causal", C)
        self.causal_s = sb("causal_s", NS)
        self.inseq = sb("inseq", SB)
        self.carry = sb("carry", T)
        self.pick = sb("pick", 3 * H, P)
        self.pick8 = sb("pick8", 8, P)
        self.unit8 = sb("unit8", 8, 8)
        self.prm = sb("prm", P)
        self.mod = sb("mod", 6 * KT, NSEQ)
        self.work = sb("work", 17920)
        self.ps = ctx.enter_context(nc.psum_tensor("ps", [P, 8, 512], F32))

    def sem(self, name):
        self.sems.append(self.nc.alloc_semaphore(name))
        return self.sems[-1]

    def fresh_semaphores(self):
        self.nc.all_engine_barrier()
        self.nc.clear_and_free_semaphores(self.sems)
        self.nc.all_engine_barrier()
        self.sems = []

    def column(self, name, n=0):
        return self.prm[:, PRM[name] + n:PRM[name] + n + 1]


def setup(k):
    nc, a, ps = k.nc, k.a, k.ps
    w = Area(k.work[:, :])
    xin = w.take(9, D)
    prm_in = w.take(P)
    cin = w.take(D)
    csl = w.take(D)
    cT = w.take(KT, NSEQ)
    ring = k.oT[:, :, :].rearrange("p a b -> p (a b)")[:, 0:6 * 2048].rearrange("p (s k n) -> p s k n", s=6, k=KT)
    NR = 6
    NB = 6 * D // 256
    x_loaded, prm_loaded, c_loaded = k.sem("x_loaded"), k.sem("prm_loaded"), k.sem("c_loaded")
    ada_loaded = [k.sem(f"ada_loaded{s}") for s in range(NR)]
    consts_done, pool_step = k.sem("consts_done"), k.sem("setup_pool_step")
    ones_done, silu_done = k.sem("ones_done"), k.sem("silu_c_done")
    x_turned, x_copied = k.sem("x_turned"), k.sem("x_copied")
    p_turned, p_copied = k.sem("p_turned"), k.sem("p_copied")
    x_copied_v = k.sem("x_copied_by_vector")
    mod_done, dstep = k.sem("mod_done"), k.sem("setup_dve_step")
    ada = a["ada_w"][0].rearrange("(k p) n -> p k n", p=P)

    with nc.Block() as block:
        @block.sync
        def _(sp):
            for name, n in (("ada_b", 48), ("norm_mix_w", 8), ("norm_ffn_w", 8), ("conf_dw_b", 4), ("conf_ln_w", 4),
                            ("conf_ln_b", 4), ("dn_norm_w", 1), ("gla_norm_w", 1), ("gla_gate_b", 2)):
                src = a[name][0].rearrange("(n p) -> n p", p=P)
                sp.dma_start(prm_in[PRM[name]:PRM[name] + n, :], src).then_inc(prm_loaded, 16)
            r = PRM["final_norm_w"]
            sp.dma_start(prm_in[r:r + 8, :], a["final_norm_w"].rearrange("(n p) -> n p", p=P)).then_inc(prm_loaded, 16)
            sp.dma_start(cin[0:1, :], a["c_prompt"]).then_inc(c_loaded, 16)
            sp.dma_start(cin[1:NSEQ, :], a["c_sample"]).then_inc(c_loaded, 16)
            for s in range(NR):
                sp.dma_start(ring[:, s], ada[:, :, s * 256:(s + 1) * 256]).then_inc(ada_loaded[s], 16)
            sp.dma_start(xin[:, 0:8, :], a["x_prompt"][0].rearrange("(t p) d -> p t d", p=P)).then_inc(x_loaded, 16)
            sp.dma_start(xin[0:NS, 8, :], a["x_sample"].rearrange("s l d -> (s l) d")).then_inc(x_loaded, 16)
            with sp.Fori(0, NB // NR - 1) as i:
                for s in range(NR):
                    sp.wait_ge(mod_done, i * NR + (s + 1))
                    sp.dma_start(ring[:, s], ada[:, :, bass.ds((i + 1) * (NR * 256) + s * 256, 256)])\
                      .then_inc(ada_loaded[s], 16)

        @block.gpsimd
        def _(g):
            st = Steps(g, pool_step)
            g.memset(k.ident[:, :], 0.0)
            g.memset(k.pair[:, :, :], 0.0)
            g.memset(k.causal[:, :], 1.0)
            g.memset(k.causal_s[:, :], 1.0)
            g.memset(k.inseq[:, :], 1.0)
            g.memset(k.unit8[:, :, :], 0.0)
            g.memset(k.carry[:, :], 1.0)
            st(g.memset(k.ones[:, :], 1.0))
            g.affine_select(out=k.ident[:, :], in_=k.ident[:, :], compare_op=ALU.not_equal, fill=1.0,
                            base=0, pattern=[[-1, P]], channel_multiplier=1)
            g.affine_select(out=k.causal[:, :], in_=k.causal[:, :], compare_op=ALU.is_ge, fill=0.0,
                            base=0, pattern=[[1, C]], channel_multiplier=-1)
            for l in range(LEVELS):
                s = 1 << l
                v = k.pair[:, l, :].rearrange("p (b h r) -> p b h r", h=2, r=s)
                g.memset(v[:, :, 1, :], 1.0)
            g.memset(k.unit8[:, :, :].rearrange("p a b -> p (a b)")[:, 0:64:9], 1.0)
            st(g.memset(k.carry[:, 0:SEQ:C], 0.0))
            g.memset(k.carry[:, SEQ:T:SL], 0.0)
            for l in range(LEVELS):
                s = 1 << l
                v = k.pair[:, l, :].rearrange("p (b h r) -> p b h r", h=2, r=s)[:, :, 1, :]
                g.affine_select(out=v, in_=v, compare_op=ALU.is_ge, fill=0.0, base=0,
                                pattern=[[-2 * s, C // (2 * s)], [0, s]], channel_multiplier=1)
            cs = k.causal_s[:, :].rearrange("p (b r) -> p b r", r=SL)
            g.affine_select(out=cs, in_=cs, compare_op=ALU.is_ge, fill=0.0, base=0,
                            pattern=[[SL, SB], [1, SL]], channel_multiplier=-1)
            g.affine_select(out=k.inseq[:, :], in_=k.inseq[:, :], compare_op=ALU.is_ge, fill=0.0, base=0,
                            pattern=[[-SL, SB]], channel_multiplier=1)
            st(g.tensor_copy(k.pair[:, LEVELS, :], k.ident[:, :]))
            for l in range(LEVELS):
                s = 1 << l
                v = k.pair[:, l, :].rearrange("p (b h r) -> p b h r", h=2, r=s)[:, :, 1, :]
                g.affine_select(out=v, in_=v, compare_op=ALU.is_ge, fill=0.0, base=s - 1,
                                pattern=[[2 * s, C // (2 * s)], [0, s]], channel_multiplier=-1)
            g.affine_select(out=cs, in_=cs, compare_op=ALU.is_ge, fill=0.0, base=0,
                            pattern=[[-SL, SB], [0, SL]], channel_multiplier=1)
            g.affine_select(out=k.inseq[:, :], in_=k.inseq[:, :], compare_op=ALU.is_ge, fill=0.0, base=SL - 1,
                            pattern=[[SL, SB]], channel_multiplier=-1)
            for h in range(H):
                for n, r in enumerate((RG + h, RB + h, RE + h)):
                    g.tensor_copy(k.pick[:, 3 * h + n, :], bcast(k.ident[:, r:r + 1], P))
            for j in range(8):
                ins = g.tensor_copy(k.pick8[0:8, j, :], bcast(k.ident[0:8, j:j + 1], P))
            ins.then_inc(consts_done, 1)

        @block.scalar
        def _(act):
            act.wait_ge(c_loaded, 32)
            act.activation(csl[0:NSEQ, :], cin[0:NSEQ, :], ACT.Silu).then_inc(silu_done, 1)
            for t in range(9):
                n = P if t < 8 else NS
                act.wait_ge(x_turned, 2 * t + 2)
                act.activation(k.xT[:, 4:8, t * P:t * P + n], ps[:, 3, :].rearrange("p (k n) -> p k n", k=4)[:, :, 0:n],
                               ACT.Copy).then_inc(x_copied, 1)

        @block.tensor
        def _(pe):
            pe.wait_ge(consts_done, 1)
            pe.wait_ge(prm_loaded, 160)
            pe.transpose(ps[:, 0, 0:N_PRM], prm_in[0:N_PRM, :], k.ident[0:N_PRM, 0:N_PRM]).then_inc(p_turned, 1)
            pe.wait_ge(silu_done, 1)
            for j in range(KT):
                ins = pe.transpose(ps[:, 1, j * NSEQ:(j + 1) * NSEQ], csl[0:NSEQ, j * P:(j + 1) * P],
                                   k.ident[0:NSEQ, 0:NSEQ])
            ins.then_inc(p_turned, 1)
            pe.wait_ge(p_copied, 2)
            with pe.Fori(0, NB // NR) as i:
                for s in range(NR):
                    pe.wait_ge(ada_loaded[s], (i + 1) * 16)
                    for u in range(2):
                        for j in range(KT):
                            ins = pe.matmul(ps[:, 0, bass.ds(i * (2 * NR * NSEQ) + (2 * s + u) * NSEQ, NSEQ)],
                                            ring[:, s, j, u * P:(u + 1) * P], cT[:, j, :],
                                            start=(j == 0), stop=(j == KT - 1))
                    ins.then_inc(mod_done, 1)
            pe.wait_ge(x_loaded, 32)
            for t in range(9):
                n = P if t < 8 else NS
                for half in range(2):
                    if t:
                        pe.wait_ge(x_copied if half else x_copied_v, t)
                    for j in range(4):
                        ins = pe.transpose(ps[:, 2 + half, j * P:j * P + n],
                                           xin[0:n, t, (4 * half + j) * P:(4 * half + j + 1) * P],
                                           k.ident[0:n, 0:n])
                    ins.then_inc(x_turned, 1)

        @block.vector
        def _(v):
            st = Steps(v, dstep)
            v.wait_ge(p_turned, 1)
            v.tensor_copy(k.prm[:, 0:N_PRM], ps[:, 0, 0:N_PRM]).then_inc(p_copied, 1)
            v.wait_ge(p_turned, 2)
            v.tensor_copy(cT[:, :, :].rearrange("p a b -> p (a b)"), ps[:, 1, 0:KT * NSEQ]).then_inc(p_copied, 1)
            v.wait_ge(mod_done, NB)
            v.wait_ge(p_copied, 2)
            st(v.tensor_tensor(k.mod[:, :, :], ps[:, 0, 0:48 * NSEQ].rearrange("p (a b) -> p a b", b=NSEQ),
                               bcast(k.prm[:, 0:48].unsqueeze(2), 48, NSEQ), ALU.add))
            for slot, name in ((1, "norm_mix_w"), (4, "norm_ffn_w")):
                m = k.mod[:, slot * KT:(slot + 1) * KT, :]
                st.done(v.scalar_tensor_tensor(m, m, 1.0, bcast(k.prm[:, PRM[name]:PRM[name] + 8].unsqueeze(2), 8, NSEQ),
                                       ALU.add, ALU.mult))
            for t in range(9):
                n = P if t < 8 else NS
                v.wait_ge(x_turned, 2 * t + 1)
                v.tensor_copy(k.xT[:, 0:4, t * P:t * P + n], ps[:, 2, :].rearrange("p (k n) -> p k n", k=4)[:, :, 0:n])\
                 .then_inc(x_copied_v, 1)


def norm(k, tag, slot):
    nc, ps = k.nc, k.ps
    w = Area(k.work[:, :])
    sq = w.take(2, T)
    rstd = w.take(T)
    squared, summed, rooted = k.sem(tag + "_squared"), k.sem(tag + "_summed"), k.sem(tag + "_rooted")
    scaled, dstep = k.sem(tag + "_mean"), k.sem(tag + "_dve_step")

    with nc.Block() as block:
        @block.scalar
        def _(act):
            for j in range(KT):
                if j >= 2:
                    act.wait_ge(summed, j - 1)
                act.activation(sq[:, j % 2, :], k.xT[:, j, :], ACT.Square).then_inc(squared, 1)
            act.wait_ge(scaled, 1)
            act.activation(rstd[:, :], rstd[:, :], ACT.Sqrt).then_inc(rooted, 1)

        @block.tensor
        def _(pe):
            for j in range(KT):
                pe.wait_ge(squared, j + 1)
                for c in range(NCH):
                    ins = pe.matmul(ps[:, c, 0:CW], k.ones[:, :], sq[:, j % 2, c * CW:(c + 1) * CW],
                                    start=(j == 0), stop=(j == KT - 1))
                ins.then_inc(summed, 1)

        @block.vector
        def _(v):
            st = Steps(v, dstep)
            v.wait_ge(summed, KT)
            v.tensor_scalar(chunks(rstd), ps[:, 0:NCH, 0:CW], 1.0 / D, EPS, ALU.mult, ALU.add).then_inc(scaled, 1)
            v.wait_ge(rooted, 1)
            st(v.reciprocal(rstd[:, :], rstd[:, :]))
            for j in range(KT):
                if slot is None:
                    st.done(v.scalar_tensor_tensor(k.hT[:, j, :], k.xT[:, j, :], k.column("final_norm_w", j), rstd[:, :],
                                           ALU.mult, ALU.mult))
                    continue
                st.done(v.tensor_tensor(k.hT[:, j, :], k.xT[:, j, :], rstd[:, :], ALU.mult))
            if slot is not None:
                st.wait()
                shift = k.mod[:, slot * KT:(slot + 1) * KT, :]
                scale = k.mod[:, (slot + 1) * KT:(slot + 2) * KT, :]
                for j in range(KT):
                    v.tensor_scalar(k.hT[:, j, 0:SEQ], k.hT[:, j, 0:SEQ], scale[:, j, 0:1], shift[:, j, 0:1],
                                    ALU.mult, ALU.add)
                    s = samples(k.hT[:, j, :])
                    st.done(v.tensor_tensor(s, s, bcast(scale[:, j, 1:NSEQ].unsqueeze(2), SB, SL), ALU.mult))
                st.wait()
                for j in range(KT):
                    s = samples(k.hT[:, j, :])
                    st.done(v.tensor_tensor(s, s, bcast(shift[:, j, 1:NSEQ].unsqueeze(2), SB, SL), ALU.add))


def delta_project(k):
    nc, a, ps = k.nc, k.a, k.ps
    w = Area(k.work[:, :])
    k.qkv = w.take(DNC, T)
    k.work_after_qkv = w.at
    acc = w.take(2, T)
    tails = w.take(DNC, DNK * NSEQ)
    spare = Area(k.oT[:, 4:12, :].rearrange("p a b -> p (a b)"))
    ring = spare.take(2, KT, 256)
    cin = spare.take(2, DNK + T)
    cs = spare.take(2, SB, DNK + SL)
    sacc = spare.take(2, SB, SL)
    taps = spare.take((DNK + 1) * DNC)
    before = spare.take(DNC, SB, DNK)
    prev_in = w.take(D + 512)
    taps_in = prev_in[64:64 + 4 * DNC, 0:P]
    tails_rows = acc[:, :, :].rearrange("p a b -> p (a b)")[:, 0:DNC * P]
    win = a["w_in"][0].rearrange("(k p) n -> p k n", p=P)
    w_loaded = [k.sem(f"qkv_w_loaded{s}") for s in range(2)]
    filled = [k.sem(f"qkv_filled{u}") for u in range(2)]
    emptied = [k.sem(f"qkv_emptied{u}") for u in range(2)]
    conv_done = [k.sem(f"qkv_conv_done{u}") for u in range(2)]
    silu_done, dstep, astep = k.sem("qkv_silu_done"), k.sem("qkv_dve_step"), k.sem("qkv_act_step")
    st_loaded, st_turned, st_copied = k.sem("dn_state_loaded"), k.sem("dn_state_turned"), k.sem("dn_state_copied")
    tails_turned, tails_copied = k.sem("dn_tails_turned"), k.sem("dn_tails_copied")
    stored = k.sem("dn_conv_state_stored")
    act_passed = k.sem("qkv_act_passed")
    NBQ, NBZ = DNC // 2, 2

    with nc.Block() as block:
        @block.sync
        def _(sp):
            for s in range(2):
                sp.dma_start(ring[:, s], win[:, :, s * 256:(s + 1) * 256]).then_inc(w_loaded[s], 16)
            sp.dma_start(prev_in[0:SB * DNK, :], a["state_delta_conv"][0].rearrange("b r c -> (b r) c")).then_inc(st_loaded, 16)
            sp.dma_start(taps_in, a["dn_conv_w"][0].rearrange("w (t p) -> (w t) p", p=P)).then_inc(st_loaded, 16)
            with sp.Fori(0, (NBQ + NBZ) // 2 - 1) as i:
                for s in range(2):
                    sp.wait_ge(filled[1], i * 2 + (s + 1))
                    sp.dma_start(ring[:, s], win[:, :, bass.ds(i * 512 + (2 + s) * 256, 256)]).then_inc(w_loaded[s], 16)
            sp.wait_ge(tails_copied, 2)
            sp.dma_start(a["prompt_state_delta_conv"][0, 0], tails_rows[0:DNK, :]).then_inc(stored, 16)
            sp.dma_start(a["sample_state_delta_conv"][0].rearrange("b r c -> (b r) c"),
                         tails_rows[32:32 + SB * DNK, :]).then_inc(stored, 16)
            sp.wait_ge(stored, 32)

        @block.tensor
        def _(pe):
            pe.wait_ge(st_loaded, 32)
            for t in range(DNC):
                pe.transpose(ps[:, 6, t * SB * DNK:(t + 1) * SB * DNK], prev_in[0:SB * DNK, t * P:(t + 1) * P],
                             k.ident[0:SB * DNK, 0:SB * DNK])
            pe.transpose(ps[:, 7, 0:4 * DNC], taps_in, k.ident[64:64 + 4 * DNC, 64:64 + 4 * DNC]).then_inc(st_turned, 1)

            def block_of(i, s, b):
                pe.wait_ge(w_loaded[s], (i + 1) * 16)
                for u in range(2):
                    pe.wait_ge(emptied[u], b + 1)
                    for c in range(NCH):
                        for j in range(KT):
                            ins = pe.matmul(ps[:, 3 * u + c, 0:CW], ring[:, s, j, u * P:(u + 1) * P],
                                            k.hT[:, j, c * CW:(c + 1) * CW], start=(j == 0), stop=(j == KT - 1))
                    ins.then_inc(filled[u], 1)

            with pe.Fori(0, (NBQ + NBZ) // 2) as i:
                for s in range(2):
                    block_of(i, s, i * 2 + s)
            pe.wait_ge(conv_done[0], NBQ + 1)
            pe.wait_ge(conv_done[1], NBQ + 1)
            pe.wait_ge(emptied[0], NBQ + NBZ + 1)
            pe.wait_ge(emptied[1], NBQ + NBZ + 1)
            for t in range(DNC):
                pe.transpose(ps[0:DNK, t // 4, (t % 4) * P:(t % 4 + 1) * P], tails[:, t, 0:DNK], k.ident[:, :])
                ins = pe.transpose(ps[0:SB * DNK, 3 + t // 4, (t % 4) * P:(t % 4 + 1) * P], tails[:, t, DNK:DNK * NSEQ],
                                   k.ident[:, :])
            ins.then_inc(tails_turned, 1)

        @block.scalar
        def _(act):
            st = Steps(act, astep)
            act.sem_inc(silu_done, 2)
            for u in range(2):
                act.activation(cin[:, u, 0:DNK], k.ones[:, 0:DNK], ACT.Copy, scale=0.0).then_inc(emptied[u], 1)
            act.wait_ge(st_copied, 1)

            with act.Fori(0, NBQ) as i:
                for u in range(2):
                    act.wait_ge(filled[u], i + 1)
                    act.wait_ge(conv_done[u], i + 1)
                    act.activation(chunks(cin[:, u, DNK:DNK + T]), ps[:, 3 * u:3 * u + 3, 0:CW], ACT.Copy)
                    act.activation(cs[:, u, :, 0:DNK], before[:, bass.ds(i * 2 + u, 1), :, :].rearrange("p a s r -> p (a s) r"), ACT.Copy)
                    act.activation(cs[:, u, :, DNK:], ps[:, 3 * u + 2, CW - NS:CW].rearrange("p (s l) -> p s l", l=SL),
                                   ACT.Copy).then_inc(emptied[u], 1)
                for u in range(2):
                    wait_before_addressed(act, conv_done[u], i + 2, act_passed)
                    act.activation(k.qkv[:, bass.ds(i * 2 + u, 1), :].rearrange("p a t -> p (a t)"), acc[:, u, :], ACT.Silu)\
                       .then_inc(silu_done, 1)
            for b in range(NBZ):
                for u in range(2):
                    act.wait_ge(filled[u], NBQ + b + 1)
                    act.activation(chunks(k.oT[:, 2 * b + u, :]), ps[:, 3 * u:3 * u + 3, 0:CW], ACT.Silu)\
                       .then_inc(emptied[u], 1)
            act.wait_ge(tails_turned, 1)
            act.activation(tails_rows[0:DNK, :].rearrange("p (b n) -> p b n", n=512), ps[0:DNK, 0:3, :], ACT.Copy)\
               .then_inc(tails_copied, 1)

        @block.vector
        def _(v):
            st = Steps(v, dstep)
            v.wait_ge(st_turned, 1)
            v.tensor_copy(before[:, :, :, :].rearrange("p t s r -> p (t s r)"), ps[:, 6, 0:DNC * SB * DNK]).then_inc(st_copied, 1)
            st(v.tensor_copy(taps[:, :], ps[:, 7, 0:4 * DNC]))
            for u in range(2):
                v.sem_inc(conv_done[u], 1)
            with v.Fori(0, NBQ) as i:
                st.loop(i, 2 * DNK)
                for u in range(2):
                    v.wait_ge(emptied[u], i + 2)
                    v.wait_ge(silu_done, i * 2 + (u + 1))
                    for tap in range(DNK + 1):
                        f = taps[:, bass.ds(i * 2 + (tap * DNC + u), 1)]
                        x, y = cin[:, u, tap:tap + SEQ], acc[:, u, 0:SEQ]
                        xs, ys = cs[:, u, :, tap:tap + SL], samples(acc[:, u, :])
                        if tap == 0:
                            v.tensor_copy(tails[:, bass.ds(i * 2 + u, 1), 0:DNK].rearrange("p a r -> p (a r)"), cin[:, u, SEQ:SEQ + DNK])
                            v.tensor_copy(tails[:, bass.ds(i * 2 + u, 1), DNK:].rearrange("p a (s r) -> p (a s) r", r=DNK), cs[:, u, :, SL:])
                            v.tensor_scalar(y, x, f, None, ALU.mult)
                            st(v.tensor_scalar(ys, xs, f, None, ALU.mult))
                            continue
                        v.scalar_tensor_tensor(y, x, f, y, ALU.mult, ALU.add)
                        ins = v.scalar_tensor_tensor(ys, xs, f, ys, ALU.mult, ALU.add)
                        if tap < DNK:
                            st(ins)
                    ins.then_inc(conv_done[u], 1)
                st.end(NBQ)
            v.wait_ge(tails_turned, 1)
            v.wait_ge(silu_done, 2 * NBQ + 2)
            v.tensor_copy(tails_rows[32:32 + SB * DNK, :].rearrange("p (b n) -> p b n", n=512), ps[0:SB * DNK, 3:6, :])\
             .then_inc(tails_copied, 1)


OUTS = [("y_prompt", (1, SEQ, D)), ("y_sample", (SB, SL, D)),
        ("prompt_state_delta", (1, 1, H, P, P)), ("prompt_state_delta_conv", (1, 1, DNK, DNC * P)),
        ("prompt_state_gla", (1, 1, H, GDK, P)), ("prompt_state_conv", (1, 1, CFK, CFC * P)),
        ("sample_state_delta", (1, SB, H, P, P)), ("sample_state_delta_conv", (1, SB, DNK, DNC * P)),
        ("sample_state_gla", (1, SB, H, GDK, P)), ("sample_state_conv", (1, SB, CFK, CFC * P))]


def delta_rows(k):
    nc, a, ps = k.nc, k.a, k.ps
    w = Area(k.work[:, k.work_after_qkv:])
    k.rows, k.rows8 = w.take(T), w.take(T)
    k.delta_area = w
    t = Area(k.oT[:, 4:12, :].rearrange("p a b -> p (a b)"))
    sq = t.take(2, T)
    wsm = t.take(KT, 80)
    raw, x, e, g = t.take(T), t.take(T), t.take(T), t.take(T)
    head = t.take(4)
    G0, G1 = RG, RG + H
    w_loaded, zeroed = k.sem("rows_w_loaded"), k.sem("rows_zeroed")
    squared, summed, small = k.sem("qk_squared"), k.sem("qk_summed"), k.sem("rows_small_done")
    dve, act_done, dstep, astep = k.sem("rows_by_vector"), k.sem("rows_by_scalar"), k.sem("rows_dve_step"), k.sem("rows_act_step")
    win = a["w_in"][0].rearrange("(k p) n -> p k n", p=P)

    with nc.Block() as block:
        @block.gpsimd
        def _(gp):
            gp.memset(wsm[:, :, :], 0.0)
            gp.memset(k.rows[:, :], 0.0).then_inc(zeroed, 1)

        @block.sync
        def _(sp):
            sp.dma_start(head[G0:G1, 0:1], a["dn_dt_bias"].rearrange("a h -> h a")).then_inc(w_loaded, 16)
            sp.dma_start(head[G0:G1, 1:2], a["dn_A_log"].rearrange("a h -> h a")).then_inc(w_loaded, 16)
            sp.wait_ge(zeroed, 1)
            for at, c0, n in ((RB, COL["ba"], H), (RG, COL["ba"] + H, H), (RT, COL["glr"], 16)):
                sp.dma_start(wsm[:, :, at:at + n], win[:, :, c0:c0 + n]).then_inc(w_loaded, 16)

        @block.tensor
        def _(pe):
            for j in range(2 * H):
                pe.wait_ge(squared, j + 1)
                for c in range(NCH):
                    ins = pe.matmul(ps[0:8, 3 + c, 0:CW], k.unit8[:, j, :], sq[:, j % 2, c * CW:(c + 1) * CW],
                                    start=(j == 0), stop=(j == 2 * H - 1))
                ins.then_inc(summed, 1)
            pe.wait_ge(w_loaded, 80)
            for c in range(NCH):
                for j in range(KT):
                    ins = pe.matmul(ps[0:80, c, 0:CW], wsm[:, j, :], k.hT[:, j, c * CW:(c + 1) * CW],
                                    start=(j == 0), stop=(j == KT - 1))
            ins.then_inc(small, 1)

        @block.scalar
        def _(act):
            st = Steps(act, astep)
            for j in range(2 * H):
                if j >= 2:
                    act.wait_ge(summed, j - 1)
                act.activation(sq[:, j % 2, :], k.qkv[:, j, :], ACT.Square).then_inc(squared, 1)
            act.wait_ge(dve, 1)
            act.activation(k.rows8[0:8, :], k.rows8[0:8, :], ACT.Sqrt).then_inc(act_done, 1)
            act.wait_ge(small, 1)
            st(act.activation(chunks(raw[0:80, :]), ps[0:80, 0:3, 0:CW], ACT.Copy))
            act.wait_ge(zeroed, 1)
            act.activation(k.rows8[64:80, :], raw[64:80, :], ACT.Copy)
            act.activation(k.rows[RB:RB + H, :], raw[0:H, :], ACT.Sigmoid)
            act.activation(head[G0:G1, 2:3], head[G0:G1, 1:2], ACT.Exp).then_inc(act_done, 1)
            act.wait_ge(dve, 2)
            st(act.activation(e[G0:G1, :], e[G0:G1, :], ACT.Exp, scale=-1.0))
            act.activation(e[G0:G1, :], e[G0:G1, :], ACT.Ln, bias=1.0).then_inc(act_done, 1)
            act.wait_ge(dve, 3)
            act.activation(k.rows[RE:RE + H, :], k.rows[G0:G1, :], ACT.Exp).then_inc(act_done, 1)

        @block.vector
        def _(v):
            st = Steps(v, dstep)
            v.wait_ge(summed, 2 * H)
            v.tensor_scalar(chunks(k.rows8[0:8, :]), ps[0:8, 3:6, 0:CW], EPS, None, ALU.add).then_inc(dve, 1)
            v.wait_ge(act_done, 1)
            st(v.reciprocal(k.rows8[0:8, :], k.rows8[0:8, :]))
            v.tensor_scalar(k.rows8[0:H, :], k.rows8[0:H, :], float(P) ** -0.5, None, ALU.mult)
            v.wait_ge(act_done, 2)
            st(v.tensor_scalar(x[G0:G1, :], raw[G0:G1, :], head[G0:G1, 0:1], None, ALU.add))
            v.scalar_tensor_tensor(e[G0:G1, :], x[G0:G1, :], -1.0, x[G0:G1, :], ALU.mult, ALU.max).then_inc(dve, 1)
            v.wait_ge(act_done, 3)
            st(v.scalar_tensor_tensor(g[G0:G1, :], x[G0:G1, :], 0.0, e[G0:G1, :], ALU.max, ALU.add))
            st(v.tensor_scalar(g[G0:G1, :], g[G0:G1, :], head[G0:G1, 2:3], -1.0, ALU.mult, ALU.mult))
            v.tensor_tensor_scan(k.rows[G0:G1, :], k.carry[G0:G1, :], g[G0:G1, :], 0.0, ALU.mult, ALU.add).then_inc(dve, 1)
            v.wait_ge(dve, 3)
            G = k.rows[G0:G1, :]
            for src, dst, n, l in ((G[:, 0:SEQ], k.rows[RT:RT + H, 0:SEQ], NC, C), (G[:, SEQ:T], k.rows[RT:RT + H, SEQ:T], SB, SL)):
                src = src.rearrange("p (c l) -> p c l", l=l)
                dst = dst.rearrange("p (c l) -> p c l", l=l)
                v.tensor_tensor(dst, bcast(src[:, :, l - 1:l], n, l), src, ALU.subtract)


def delta_rule(k):
    nc, a, ps = k.nc, k.a, k.ps
    w = k.delta_area
    t = Area(k.oT[:, 4:12, :].rearrange("p a b -> p (a b)"))

    def take(*s):
        n = 1
        for x in s:
            n *= x
        return (t if t.at + n <= t.size else w).take(*s)

    stage = [take(3, C) for _ in range(H)]
    rb = [take(2, C) for _ in range(H)]
    XY = [take(2, C) for _ in range(H)]
    lv = [take(2, C) for _ in range(H)]
    dec, AT, MT, P1, vb, kbe, kd, nwT, vn, qe, S = ([take(C) for _ in range(H)] for _ in range(11))
    rst, tcol, ecol, bge = take(C), take(C), take(C), take(H)
    v_filled, v_drained, s_filled, s_drained = (k.sem("dr_" + x) for x in
                                                ("v_filled", "v_drained", "s_filled", "s_drained"))
    rows_staged, cols_exp, bge_ready = k.sem("dr_rows_staged"), k.sem("dr_cols_exp"), k.sem("dr_bge_ready")
    decay_ready, level_ready = k.sem("dr_decay_ready"), k.sem("dr_level_ready")
    vexp_ready, dstep, astep = k.sem("dr_vexp_ready"), k.sem("dr_dve_step"), k.sem("dr_act_step")
    s0_loaded = [k.sem(f"dr_s0_loaded{h}") for h in range(H)]
    q_free, s_stored, s_final = k.sem("dr_q_free"), k.sem("dr_state_stored"), k.sem("dr_state_final")
    act_passed, pe_passed = k.sem("dr_act_passed"), k.sem("dr_pe_passed")
    LS = 2
    VE, SE = H * (4 + LEVELS) + 1, H * (4 + LEVELS)

    class At:
        def __init__(self, i):
            self.i = i

        def v(self, e, h):
            return self.i * VE + (1 + H * e + h + 1 if e >= 0 else 1)

        def s(self, e, h):
            return self.i * SE + (H * e + h + 1)
    bankv = lambda h: ps[:, 2 * h, :]
    banks = lambda h: ps[:, 2 * h + 1, :]

    def columns(i):
        return bass.ds(i * C, C) if not isinstance(i, int) or i < NC else slice(SEQ, T)

    with nc.Block() as block:
        def pe_front(pe, i, n, levels):
            at = At(i)
            cols = columns(i)

            def v_free(e, h, wait=None):
                (wait or (lambda s, x: pe.wait_ge(s, x)))(v_drained, at.v(e - 1, h) + H if e > 0 or h == 0 and e == 0 else at.i * VE + (1 + h))

            def s_free(e, h):
                pe.wait_ge(s_drained, at.s(e - 1, h) + H if e > 0 else at.i * SE + (1 + h))

            pe.wait_ge(rows_staged, i + 1)
            pe.wait_ge(v_drained, at.i * VE + 1)
            pe.transpose(ps[0:n, 0, 0:P], rst[:, 0:n], k.ident[:, :]).then_inc(v_filled, 1)
            for h in range(H):
                v_free(0, h, lambda s, x: wait_before_addressed(pe, s, x, pe_passed))
                for m, x in enumerate((h, H + h)):
                    pe.matmul(bankv(h)[:, m * n:(m + 1) * n], k.pick8[0:8, x, :], k.rows8[0:8, cols], start=True, stop=True)
                pe.matmul(bankv(h)[:, 2 * n:3 * n], k.pick[:, 3 * h, :], k.rows[:, cols], start=True, stop=True)\
                  .then_inc(v_filled, 1)
                s_free(0, h)
                for m in range(2):
                    ins = pe.matmul(banks(h)[:, m * n:(m + 1) * n], k.pick[:, 3 * h + 1 + m, :], k.rows[:, cols],
                                    start=True, stop=True)
                ins.then_inc(s_filled, 1)
            for h in range(H):
                v_free(1, h)
                kT = stage[h][:, 1, 0:n]
                pe.matmul(bankv(h)[0:n, 0:n], kT, stage[h][:, 0, 0:n], start=True, stop=True)
                pe.matmul(bankv(h)[0:n, n:2 * n], kT, kT, start=True, stop=True).then_inc(v_filled, 1)
                s_free(1, h)
                pe.transpose(banks(h)[0:n, 0:P], kT, k.ident[:, :])
                pe.transpose(banks(h)[0:n, P:2 * P], stage[h][:, 2, 0:n], k.ident[:, :]).then_inc(s_filled, 1)
            for l in range(levels):
                for h in range(H):
                    pe.wait_ge(level_ready, at.i * (H * LEVELS) + (H * l + h + 1))
                    v_free(2 + l, h)
                    s_free(2 + l, h)
                    pe.matmul(banks(h)[0:n, 0:n], lv[h][0:n, l % 2, 0:n], XY[h][0:n, 0, 0:n], start=True, stop=True)\
                      .then_inc(s_filled, 1)
                for h in range(H):
                    pe.wait_ge(s_drained, at.s(2 + l, h) + H)
                    if l < levels - 1:
                        pe.matmul(bankv(h)[0:n, 0:n], XY[h][0:n, 1, 0:n], P1[h][0:n, 0:n], start=True, stop=True)
                    pe.matmul(bankv(h)[0:n, n:2 * n], P1[h][0:n, 0:n], XY[h][0:n, 1, 0:n], start=True, stop=True)\
                      .then_inc(v_filled, 1)
            e = 2 + levels
            for h in range(H):
                v_free(e, h)
                s_free(e, h)
                pe.matmul(banks(h)[:, 0:n], kbe[h][0:n, :], XY[h][0:n, 1, 0:n], start=True, stop=True).then_inc(s_filled, 1)
            return at, e

        @block.tensor
        def _(pe):
            with pe.Fori(0, NC) as i:
                at, e = pe_front(pe, i, C, LEVELS)
                for h in range(H):
                    pe.wait_ge(s_drained, at.s(e, h) + H)
                    pe.matmul(bankv(h)[:, 0:C], XY[h][:, 1, :], vb[h][:, :], start=True, stop=False)
                    pe.matmul(bankv(h)[:, 0:C], nwT[h][:, :], S[h][:, :], start=False, stop=True).then_inc(v_filled, 1)
                for h in range(H):
                    pe.wait_ge(v_drained, at.v(e, h) + H)
                    pe.matmul(banks(h)[:, 0:C], S[h][:, :], qe[h][:, :], start=True, stop=False)
                    pe.matmul(banks(h)[:, 0:C], vn[h][:, :], AT[h][:, :], start=False, stop=True).then_inc(s_filled, 1)
                    pe.matmul(bankv(h)[:, 0:C], kd[h][:, :], vn[h][:, :], start=True, stop=True).then_inc(v_filled, 1)
            at, e = pe_front(pe, NC, NS, LS)
            for h in range(H):
                pe.wait_ge(s_drained, at.s(e, h) + H)
                pe.wait_ge(s0_loaded[h], 16)
                S0 = k.qkv[:, h, 0:SEQ].rearrange("p (b e) -> p b e", b=SB)
                pe.matmul(bankv(h)[:, 0:NS], vb[h][0:NS, :], XY[h][0:NS, 1, 0:NS], start=True, stop=False)
                for b in range(SB):
                    ins = pe.matmul(bankv(h)[:, b * SL:(b + 1) * SL], S0[:, b, :], nwT[h][:, b * SL:(b + 1) * SL],
                                    start=False, stop=(b == SB - 1))
                ins.then_inc(v_filled, 1)
            for h in range(H):
                pe.wait_ge(v_drained, at.v(e, h) + H)
                pe.transpose(banks(h)[0:NS, 0:P], nwT[h][:, 0:NS], k.ident[:, :]).then_inc(s_filled, 1)
            for h in range(H):
                pe.wait_ge(s_drained, at.s(e + 1, h) + H)
                S0 = k.qkv[:, h, 0:SEQ].rearrange("p (b e) -> p b e", b=SB)
                pe.matmul(bankv(h)[:, 0:NS], vn[h][0:NS, :], AT[h][0:NS, 0:NS], start=True, stop=False)
                for b in range(SB):
                    ins = pe.matmul(bankv(h)[:, b * SL:(b + 1) * SL], S0[:, b, :], qe[h][:, b * SL:(b + 1) * SL],
                                    start=False, stop=(b == SB - 1))
                ins.then_inc(v_filled, 1)
            for half in range(2):
                for h in range(H):
                    pe.wait_ge(vexp_ready, h + 1)
                    pe.wait_ge(v_drained, at.v(e + 1 + half, h) + H)
                    pe.matmul(bankv(h)[:, :], kd[h][0:NS, :], k.qkv[0:NS, H + h, half * 512:(half + 1) * 512],
                              start=True, stop=True).then_inc(v_filled, 1)

        def act_front(act, i, n, levels):
            at = At(i)
            cols = columns(i)
            act.wait_ge(v_drained, at.v(-1, 0) + H)
            act.activation(ecol[0:n, RG:RT + H], tcol[0:n, RG:RT + H], ACT.Exp).then_inc(cols_exp, 1)
            for h in range(H):
                src = k.qkv[:, 2 * H + h, cols]
                act.activation(stage[h][:, 2, 0:n], src, ACT.Copy)
                act.wait_ge(s_filled, at.s(0, h))
                act.activation(rb[h][:, :, 0:n], banks(h)[:, 0:2 * n].rearrange("p (a b) -> p a b", a=2), ACT.Copy)\
                   .then_inc(s_drained, 1)
            for h in range(H):
                act.wait_ge(v_drained, at.v(0, h) + H)
                act.activation(dec[h][0:n, 0:n], dec[h][0:n, 0:n], ACT.Exp).then_inc(decay_ready, 1)
            act.wait_ge(bge_ready, i + 1)
            for h in range(H):
                act.wait_ge(s_filled, at.s(1, h))
                act.activation(vb[h][0:n, :], banks(h)[0:n, P:2 * P], ACT.Copy, scale=tcol[0:n, RB + h:RB + h + 1])
                act.activation(kbe[h][0:n, :], banks(h)[0:n, 0:P], ACT.Copy, scale=bge[0:n, h:h + 1])
                act.activation(kd[h][0:n, :], banks(h)[0:n, 0:P], ACT.Copy, scale=ecol[0:n, RT + h:RT + h + 1])\
                   .then_inc(s_drained, 1)
            for l in range(levels):
                for h in range(H):
                    act.wait_ge(s_filled, at.s(2 + l, h))
                    act.activation(P1[h][0:n, 0:n], banks(h)[0:n, 0:n], ACT.Copy).then_inc(s_drained, 1)
            e = 2 + levels
            for h in range(H):
                act.wait_ge(s_filled, at.s(e, h))
                act.activation(nwT[h][:, 0:n], banks(h)[:, 0:n], ACT.Copy, scale=-1.0).then_inc(s_drained, 1)
            return at, e

        @block.scalar
        def _(act):
            act.sem_inc(s_drained, H)
            with act.Fori(0, NC) as i:
                at, e = act_front(act, i, C, LEVELS)
                for h in range(H):
                    wait_before_addressed(act, s_filled, at.s(e + 1, h), act_passed)
                    act.activation(k.qkv[:, 2 * H + h, columns(i)], banks(h)[:, 0:C], ACT.Copy).then_inc(s_drained, 1)
            at, e = act_front(act, NC, NS, LS)
            for h in range(H):
                act.wait_ge(s_filled, at.s(e + 1, h))
                act.activation(vn[h][0:NS, :], banks(h)[0:NS, 0:P], ACT.Copy).then_inc(s_drained, 1)

        def dve_front(v, st, i, n, levels):
            at = At(i)
            cols = columns(i)
            v.tensor_copy(rst[:, 0:n], k.rows[:, cols]).then_inc(rows_staged, 1)
            v.wait_ge(v_filled, at.v(-1, 0))
            v.tensor_copy(tcol[0:n, :], ps[0:n, 0, 0:P]).then_inc(v_drained, 1)
            v.wait_ge(cols_exp, i + 1)
            v.wait_ge(v_drained, at.v(-1, 0) + H)
            v.tensor_tensor(bge[0:n, :], tcol[0:n, RB:RB + H], ecol[0:n, RG:RG + H], ALU.mult).then_inc(bge_ready, 1)
            for h in range(H):
                v.wait_ge(v_filled, at.v(0, h))
                v.tensor_tensor(stage[h][:, 0:2, 0:n], k.qkv[:, h:h + 5:4, cols],
                                bankv(h)[:, 0:2 * n].rearrange("p (a b) -> p a b", a=2), ALU.mult)
                v.tensor_scalar(dec[h][0:n, 0:n], bankv(h)[0:n, 2 * n:3 * n], tcol[0:n, RG + h:RG + h + 1], 0.0,
                                ALU.subtract, ALU.min).then_inc(v_drained, 1)
            mask = k.causal[:, :] if n == C else k.causal_s[0:n, :]
            for h in range(H):
                v.wait_ge(decay_ready, at.i * H + (h + 1))
                st.done(v.tensor_tensor(dec[h][0:n, 0:n], dec[h][0:n, 0:n], mask, ALU.mult))
            st.wait()
            for h in range(H):
                v.wait_ge(v_filled, at.v(1, h))
                v.tensor_tensor(AT[h][0:n, 0:n], bankv(h)[0:n, 0:n], dec[h][0:n, 0:n], ALU.mult)
                v.tensor_tensor(MT[h][0:n, 0:n], bankv(h)[0:n, n:2 * n], dec[h][0:n, 0:n], ALU.mult).then_inc(v_drained, 1)
            v.wait_ge(v_drained, at.v(1, H - 1) + H)
            v.wait_ge(s_drained, at.s(0, H - 1) + H)
            for h in range(H):
                v.tensor_tensor(qe[h][:, 0:n], stage[h][:, 0, 0:n], rb[h][:, 1, 0:n], ALU.mult)
                v.tensor_copy(XY[h][0:n, 0, 0:n], k.ident[0:n, 0:n])
                v.tensor_copy(XY[h][0:n, 1, 0:n], k.ident[0:n, 0:n])
                st.done(v.tensor_tensor(MT[h][0:n, 0:n], MT[h][0:n, 0:n], rb[h][0:n, 0, 0:n], ALU.mult))
            st.wait()
            for l in range(levels + 1):
                if l < levels:
                    for h in range(H):
                        v.tensor_tensor(lv[h][0:n, l % 2, 0:n], MT[h][0:n, 0:n], k.pair[0:n, l, 0:n], ALU.mult)\
                         .then_inc(level_ready, 1)
                if l:
                    for h in range(H):
                        v.wait_ge(v_filled, at.v(1 + l, h))
                        v.wait_ge(v_drained, at.v(l, h) + H)
                        lo = 0 if l < levels else 1
                        v.tensor_tensor(XY[h][0:n, lo:2, 0:n], XY[h][0:n, lo:2, 0:n],
                                        bankv(h)[0:n, lo * n:2 * n].rearrange("p (a b) -> p a b", b=n), ALU.subtract)\
                         .then_inc(v_drained, 1)
            return at, 2 + levels

        @block.vector
        def _(v):
            st = Steps(v, dstep)
            for h in range(H):
                v.memset(S[h][:, :], 0.0).then_inc(v_drained, 1)
            with v.Fori(0, NC) as i:
                st.loop(i, 2 * H)
                at, e = dve_front(v, st, i, C, LEVELS)
                st.end(NC)
                for h in range(H):
                    v.wait_ge(v_filled, at.v(e, h))
                    v.tensor_copy(vn[h][:, :], bankv(h)[:, 0:C]).then_inc(v_drained, 1)
                for h in range(H):
                    v.wait_ge(v_filled, at.v(e + 1, h))
                    v.scalar_tensor_tensor(S[h][:, :], S[h][:, :], rb[h][:, 1, C - 1:C], bankv(h)[:, 0:C],
                                           ALU.mult, ALU.add).then_inc(v_drained, 1)
            at, e = dve_front(v, st, NC, NS, LS)
            for h in range(H):
                v.wait_ge(v_filled, at.v(e, h))
                v.tensor_copy(nwT[h][:, 0:NS], bankv(h)[:, 0:NS]).then_inc(v_drained, 1)
            for h in range(H):
                v.wait_ge(s_drained, at.s(e + 1, h) + H)
                v.tensor_tensor(k.qkv[0:NS, H + h, 0:SEQ].rearrange("p (b e) -> p b e", b=SB),
                                bcast(vn[h][0:NS, :].unsqueeze(1), SB, P), bcast(k.inseq[0:NS, :].unsqueeze(2), SB, P),
                                ALU.mult).then_inc(vexp_ready, 1)
            for h in range(H):
                v.wait_ge(v_filled, at.v(e + 1, h))
                v.tensor_copy(k.qkv[:, 2 * H + h, SEQ:T], bankv(h)[:, 0:NS]).then_inc(v_drained, 1)
            for half in range(2):
                for h in range(H):
                    v.wait_ge(v_filled, at.v(e + 2 + half, h))
                    for b in range(4):
                        bb = 4 * half + b
                        S0 = k.qkv[:, h, bb * P:(bb + 1) * P]
                        ins = v.scalar_tensor_tensor(S0, S0, rb[h][:, 1, bb * SL + SL - 1:bb * SL + SL],
                                                     bankv(h)[:, b * P:(b + 1) * P], ALU.mult, ALU.add)
                    ins.then_inc(v_drained, 1)

        @block.sync
        def _(sp):
            for h in range(H):
                sp.wait_ge(v_drained, (NC - 1) * VE + (1 + H * 0 + h + 1) + H)
                sp.dma_start(k.qkv[:, h, 0:SEQ].rearrange("p (b e) -> p b e", b=SB),
                             a["state_delta"][0, :, h].rearrange("b d e -> d b e")).then_inc(s0_loaded[h], 16)
            for h in range(H):
                sp.wait_ge(v_drained, NC * VE + H)
                sp.dma_start(a["prompt_state_delta"][0, 0, h], S[h][:, :]).then_inc(s_stored, 16)
            for h in range(H):
                sp.wait_ge(v_drained, At(NC).v(7, h) + H)
                sp.dma_start(a["sample_state_delta"][0, :, h].rearrange("b d e -> d b e"),
                             k.qkv[:, h, 0:SEQ].rearrange("p (b e) -> p b e", b=SB)).then_inc(s_stored, 16)
            sp.wait_ge(s_stored, 16 * 2 * H)


def gated_norm(k, tag, src, dst, weight, area):
    nc, ps = k.nc, k.ps
    sq, fac = area.take(2, T), area.take(T)
    squared, summed, spread = k.sem(tag + "_squared"), k.sem(tag + "_summed"), k.sem(tag + "_spread")
    by_act, by_dve, dstep = k.sem(tag + "_by_act"), k.sem(tag + "_by_dve"), k.sem(tag + "_dve_step")
    drained = k.sem(tag + "_drained")

    with nc.Block() as block:
        @block.scalar
        def _(act):
            for h in range(H):
                if h >= 2:
                    act.wait_ge(summed, h - 1)
                act.activation(sq[:, h % 2, :], src[:, h, :], ACT.Square).then_inc(squared, 1)
            act.wait_ge(by_dve, 1)
            act.activation(fac[0:8, :], fac[0:8, :], ACT.Sqrt).then_inc(by_act, 1)

        @block.tensor
        def _(pe):
            for h in range(H):
                pe.wait_ge(squared, h + 1)
                for c in range(NCH):
                    ins = pe.matmul(ps[0:8, c, 0:CW], k.unit8[:, h, :], sq[:, h % 2, c * CW:(c + 1) * CW],
                                    start=(h == 0), stop=(h == H - 1))
                ins.then_inc(summed, 1)
            pe.wait_ge(by_dve, 2)
            for h in range(H):
                if h >= 2:
                    pe.wait_ge(drained, h - 1)
                for c in range(NCH):
                    ins = pe.matmul(ps[:, 3 * (h % 2) + c, 0:CW], k.pick8[0:8, h, :], fac[0:8, c * CW:(c + 1) * CW],
                                    start=True, stop=True)
                ins.then_inc(spread, 1)

        @block.vector
        def _(v):
            st = Steps(v, dstep)
            v.wait_ge(summed, H)
            v.tensor_scalar(chunks(fac[0:8, :]), ps[0:8, 0:3, 0:CW], 1.0 / P, EPS, ALU.mult, ALU.add).then_inc(by_dve, 1)
            v.wait_ge(by_act, 1)
            v.reciprocal(fac[0:8, :], fac[0:8, :]).then_inc(by_dve, 1)
            for h in range(H):
                v.wait_ge(spread, h + 1)
                v.scalar_tensor_tensor(chunks(src[:, h, :]), chunks(src[:, h, :]), weight,
                                       ps[:, 3 * (h % 2):3 * (h % 2) + 3, 0:CW], ALU.mult, ALU.mult).then_inc(drained, 1)
            v.wait_ge(drained, H)
            for h in range(H):
                v.tensor_tensor(dst[:, h, :], dst[:, h, :], src[:, h, :], ALU.mult)


def gla_project(k):
    nc, a, ps = k.nc, k.a, k.ps
    w = Area(k.work[:, :])
    low = k.rows8
    k.gla = w.take(8, T)
    w.take(k.work_after_qkv + 2 * T - w.at)
    k.bcum = k.oT[:, 8:10, :]
    lg, ab = w.take(T), w.take(T)
    ring = Area(k.work[:, 8 * T:k.work_after_qkv]).take(2, KT, 256)
    gw = w.take(256)
    win = a["w_in"][0].rearrange("(k p) n -> p k n", p=P)
    w_loaded = [k.sem(f"gla_w_loaded{s}") for s in range(2)]
    filled, drained = k.sem("gla_filled"), k.sem("gla_drained")
    gw_loaded, lg_done, by_dve, dstep, astep = (k.sem("gla_" + x) for x in ("gw_loaded", "lg_done", "by_dve", "dstep", "astep"))
    NB = 6

    with nc.Block() as block:
        @block.sync
        def _(sp):
            sp.dma_start(gw[64:80, :], a["gla_gate_w"][0]).then_inc(gw_loaded, 16)
            for b in range(NB):
                if b >= 2:
                    sp.wait_ge(filled, 2 * (b - 1))
                c0 = COL["gqk"] + b * 256
                sp.dma_start(ring[:, b % 2], win[:, :, c0:c0 + 256]).then_inc(w_loaded[b % 2], 16)

        @block.tensor
        def _(pe):
            for b in range(NB):
                pe.wait_ge(w_loaded[b % 2], 16 * (b // 2 + 1))
                for u in range(2):
                    f = 2 * b + u
                    if f >= 2:
                        pe.wait_ge(drained, f - 1)
                    for c in range(NCH):
                        for j in range(KT):
                            ins = pe.matmul(ps[:, 3 * u + c, 0:CW], ring[:, b % 2, j, u * P:(u + 1) * P],
                                            k.hT[:, j, c * CW:(c + 1) * CW], start=(j == 0), stop=(j == KT - 1))
                    ins.then_inc(filled, 1)
            pe.wait_ge(gw_loaded, 16)
            for u in range(2):
                f = 2 * NB + u
                pe.wait_ge(drained, f - 1)
                for c in range(NCH):
                    ins = pe.matmul(ps[:, 3 * u + c, 0:CW], gw[64:80, u * P:(u + 1) * P], low[64:80, c * CW:(c + 1) * CW],
                                    start=True, stop=True)
                ins.then_inc(filled, 1)

        @block.scalar
        def _(act):
            st = Steps(act, astep)
            for f in range(2 * NB):
                act.wait_ge(filled, f + 1)
                src = ps[:, 3 * (f % 2):3 * (f % 2) + 3, 0:CW]
                if f < 8:
                    act.activation(chunks(k.gla[:, f, :]), src, ACT.Copy, scale=GDK ** -0.5 if f < 2 else 1.0).then_inc(drained, 1)
                else:
                    act.activation(chunks(k.oT[:, f - 4, :]), src, ACT.Silu).then_inc(drained, 1)
            for u in range(2):
                act.wait_ge(filled, 2 * NB + u + 1)
                if u:
                    act.wait_ge(by_dve, 2)
                act.activation(chunks(lg), ps[:, 3 * u:3 * u + 3, 0:CW], ACT.Identity, bias=k.column("gla_gate_b", u))\
                   .then_inc(drained, 1)
                act.wait_ge(by_dve, 2 * u + 1)
                st(act.activation(ab[:, :], ab[:, :], ACT.Exp, scale=-1.0))
                act.activation(ab[:, :], ab[:, :], ACT.Ln, bias=1.0).then_inc(lg_done, 1)

        @block.vector
        def _(v):
            st = Steps(v, dstep)
            for u in range(2):
                v.wait_ge(drained, 2 * NB + u + 1)
                if u:
                    v.wait_ge(by_dve, 2)
                v.scalar_tensor_tensor(ab[:, :], lg[:, :], -1.0, lg[:, :], ALU.mult, ALU.max).then_inc(by_dve, 1)
                v.wait_ge(lg_done, u + 1)
                st(v.scalar_tensor_tensor(ab[:, :], lg[:, :], 0.0, ab[:, :], ALU.min, ALU.subtract))
                st(v.tensor_scalar(ab[:, :], ab[:, :], 1.0 / 16.0, None, ALU.mult))
                v.tensor_tensor_scan(k.bcum[:, u, :], k.carry[:, :], ab[:, :], 0.0, ALU.mult, ALU.add).then_inc(by_dve, 1)


def gla_rule(k):
    nc, a, ps = k.nc, k.a, k.ps
    w = Area(k.work[:, 8 * T:])
    t = Area(k.oT[:, 10:12, :].rearrange("p a b -> p (a b)"))
    E = [w.take(LEVELS + 2, C) for _ in range(2)]
    Kf = [w.take(LEVELS + 1, C) for _ in range(2)]
    Qf = [w.take(LEVELS + 1, C) for _ in range(2)]
    raw = [w.take(2, C) for _ in range(2)]
    vst = [w.take(2, C) for _ in range(2)]
    kdv = [w.take(3, P) for _ in range(2)]
    S = [w.take(2, P) for _ in range(2)]
    head_q, head_f = w.take(H, NS), w.take(H, NS)
    prod = [t.take(LEVELS + 1, C) for _ in range(2)]
    AT = [w.take(C) for _ in range(H)]
    L_filled, L_drained, T_filled, T_drained, O_filled, O_drained, S_filled, S_drained = (
        k.sem("gr_" + x) for x in ("levels_filled", "levels_drained", "turned_filled", "turned_drained",
                                   "out_filled", "out_drained", "state_filled", "state_drained"))
    diff_ready, exp_ready, kq_ready, staged, at_ready, vexp_ready = (
        k.sem("gr_" + x) for x in ("diff_ready", "exp_ready", "kq_ready", "staged", "at_ready", "vexp_ready"))
    dstep, astep, stored = k.sem("gr_dve_step"), k.sem("gr_act_step"), k.sem("gr_state_stored")
    s0_loaded = [k.sem(f"gr_s0_loaded{h}") for h in range(H)]
    shifted, act_passed = k.sem("gr_head_rows_shifted"), k.sem("gr_act_passed")
    S0 = [k.gla[0:GDK, h, 0:SEQ].rearrange("p (b e) -> p b e", b=SB) for h in range(H)]
    vexp = [x.rearrange("p a b -> p (a b)") for x in (Kf[0], Qf[0], Kf[1], Qf[1])]

    def columns(i):
        return bass.ds(i * C, C) if not isinstance(i, int) or i < NC else slice(SEQ, T)

    def level_bank(h, n):
        return ps[0:n, 2 * (h % 2):2 * (h % 2) + 2, :].rearrange("p a b -> p (a b)")

    with nc.Block() as block:
        def pe_front(pe, i, n, levels):
            for p in range(2):
                pe.wait_ge(kq_ready, 2 * i + p + 1)
                pe.wait_ge(staged, 2 * i + p + 1)
                for hh in range(2):
                    h, r = 2 * p + hh, slice(64 * hh, 64 * hh + 64)
                    pe.wait_ge(L_drained, 4 * i + h + 1)
                    out = level_bank(h, n)
                    for l in range(levels):
                        pe.matmul(out[:, l * n:(l + 1) * n], Kf[p][r, l, 0:n], Qf[p][r, l, 0:n], start=True, stop=True)
                    pe.matmul(out[:, levels * n:(levels + 1) * n], raw[p][r, 1, 0:n], raw[p][r, 0, 0:n],
                              start=True, stop=True).then_inc(L_filled, 1)
                pe.wait_ge(T_drained, 2 * i + p + 1)
                pe.transpose(ps[0:n, 4 + p, 0:P], Kf[p][:, LEVELS, 0:n], k.ident[:, :])
                for hh in range(2):
                    ins = pe.transpose(ps[0:n, 4 + p, (1 + hh) * P:(2 + hh) * P], vst[p][:, hh, 0:n], k.ident[:, :])
                ins.then_inc(T_filled, 1)
            pe.wait_ge(O_drained, i + 1)
            for p in range(2):
                pe.wait_ge(T_drained, 2 * i + p + 3)

        @block.tensor
        def _(pe):
            with pe.Fori(0, NC) as i:
                pe_front(pe, i, C, LEVELS)
                pe.wait_ge(S_drained, i + 1)
                for h in range(H):
                    p, hh = divmod(h, 2)
                    pe.wait_ge(at_ready, 4 * i + h + 1)
                    pe.matmul(ps[:, 7, h * C:(h + 1) * C], S[p][:, hh, :], Qf[p][:, LEVELS, :], start=True, stop=False)
                    ins = pe.matmul(ps[:, 7, h * C:(h + 1) * C], kdv[p][:, 1 + hh, :], AT[h][:, :], start=False, stop=True)
                ins.then_inc(O_filled, 1)
                for p in range(2):
                    ins = pe.matmul(ps[:, 6, p * 256:(p + 1) * 256], kdv[p][:, 0, :],
                                    kdv[p][:, 1:3, :].rearrange("p a b -> p (a b)"), start=True, stop=True)
                ins.then_inc(S_filled, 1)
            pe_front(pe, NC, NS, 2)
            pe.wait_ge(shifted, 1)
            for h in range(H):
                p, hh = divmod(h, 2)
                pe.wait_ge(s0_loaded[h], 16)
                pe.wait_ge(at_ready, 4 * NC + h + 1)
                out = ps[:, 7, h * NS:(h + 1) * NS]
                pe.matmul(out, kdv[p][0:NS, 1 + hh, :], AT[h][0:NS, 0:NS], start=True, stop=False)
                for b in range(SB):
                    ins = pe.matmul(out[:, b * SL:(b + 1) * SL], S0[h][:, b, :], head_q[0:GDK, h, b * SL:(b + 1) * SL],
                                    start=False, stop=(b == SB - 1))
            ins.then_inc(O_filled, 1)
            for n in range(2 * H):
                h, half = divmod(n, 2)
                p, hh = divmod(h, 2)
                pe.wait_ge(S_drained, NC + n + 1)
                pe.wait_ge(vexp_ready, h + 1)
                pe.matmul(ps[0:GDK, 6, :], kdv[p][0:NS, 0, GDK * hh:GDK * hh + GDK],
                          vexp[h][0:NS, half * 512:(half + 1) * 512], start=True, stop=True).then_inc(S_filled, 1)

        def act_front(act, i, n):
            for p in range(2):
                for m in range(2):
                    act.activation(raw[p][:, m, 0:n], k.gla[:, 2 * m + p, columns(i)], ACT.Copy)
                    ins = act.activation(vst[p][:, m, 0:n], k.gla[:, 4 + 2 * p + m, columns(i)], ACT.Copy)
                ins.then_inc(staged, 1)
            for p in range(2):
                act.wait_ge(diff_ready, 2 * i + p + 1)
                act.activation(E[p][:, :, 0:n], E[p][:, :, 0:n], ACT.Exp, scale=-1.0).then_inc(exp_ready, 1)
            for p in range(2):
                act.wait_ge(T_filled, 2 * i + p + 1)
                act.activation(kdv[p][0:n, :, :].rearrange("p a b -> p (a b)"), ps[0:n, 4 + p, 0:3 * P], ACT.Copy)\
                   .then_inc(T_drained, 1)

        @block.scalar
        def _(act):
            act.sem_inc(T_drained, 2)
            act.sem_inc(O_drained, 1)
            with act.Fori(0, NC) as i:
                act_front(act, i, C)
                wait_before_addressed(act, O_filled, i + 1, act_passed)
                act.activation(k.gla[:, 4:8, columns(i)], ps[:, 7, :].rearrange("p (h n) -> p h n", h=H), ACT.Copy)\
                   .then_inc(O_drained, 1)
            act_front(act, NC, NS)
            for p in range(2):
                act.wait_ge(kq_ready, 2 * NC + p + 1)
                for hh in range(2):
                    act.activation(head_q[0:GDK, 2 * p + hh, :], Qf[p][64 * hh:64 * hh + 64, LEVELS, 0:NS], ACT.Copy)
                    ins = act.activation(head_f[0:GDK, 2 * p + hh, :], E[p][64 * hh:64 * hh + 64, LEVELS + 1, 0:NS], ACT.Copy)
            ins.then_inc(shifted, 1)
            act.wait_ge(O_filled, NC + 1)
            act.activation(k.gla[:, 4:8, SEQ:T], ps[:, 7, 0:H * NS].rearrange("p (h n) -> p h n", h=H), ACT.Copy)\
               .then_inc(O_drained, 1)

        def dve_front(v, st, i, n, levels, length):
            for p in range(2):
                b = k.bcum[:, p, columns(i)]
                for l in range(levels):
                    s = 1 << l
                    bb = b.rearrange("p (m r) -> p m r", r=2 * s)
                    v.tensor_tensor(E[p][:, l, 0:n].rearrange("p (m r) -> p m r", r=2 * s), bb,
                                    bcast(bb[:, :, s - 1:s], n // (2 * s), 2 * s), ALU.subtract)
                for l in range(levels, LEVELS):
                    if n < C:
                        v.memset(E[p][:, l, 0:n], 0.0)
                bb = b.rearrange("p (m r) -> p m r", r=length)
                v.tensor_copy(E[p][:, LEVELS + 1, 0:n], b)
                st.done(v.tensor_tensor(E[p][:, LEVELS, 0:n].rearrange("p (m r) -> p m r", r=length),
                                        bcast(bb[:, :, length - 1:length], n // length, length), bb, ALU.subtract))
                st.wait()
                v.scalar_tensor_tensor(E[p][:, :, 0:n], E[p][:, :, 0:n], -1.0, E[p][:, :, 0:n], ALU.mult, ALU.max)\
                 .then_inc(diff_ready, 1)
            for p in range(2):
                v.wait_ge(exp_ready, 2 * i + p + 1)
                q, kk = k.gla[:, p, columns(i)], k.gla[:, 2 + p, columns(i)]
                v.tensor_tensor(Kf[p][:, :, 0:n], bcast(kk.unsqueeze(1), LEVELS + 1, n), E[p][:, 0:LEVELS + 1, 0:n], ALU.mult)
                v.tensor_tensor(Qf[p][:, LEVELS, 0:n], q, E[p][:, LEVELS + 1, 0:n], ALU.mult)
                v.tensor_tensor(Qf[p][:, 0:LEVELS, 0:n], bcast(q.unsqueeze(1), LEVELS, n), E[p][:, 0:LEVELS, 0:n], ALU.mult)\
                 .then_inc(kq_ready, 1)
            for h in range(H):
                v.wait_ge(L_filled, 4 * i + h + 1)
                out = level_bank(h, n)
                pr = prod[h % 2].rearrange("p a b -> p (a b)")[:, 0:(levels + 1) * n].rearrange("p (l n) -> p l n", n=n)
                o3 = out[:, 0:(levels + 1) * n].rearrange("p (l n) -> p l n", n=n)
                if levels == LEVELS:
                    v.tensor_tensor(pr[0:n], o3, k.pair[0:n, :, 0:n], ALU.mult).then_inc(L_drained, 1)
                else:
                    v.tensor_tensor(pr[0:n, 0:levels], o3[:, 0:levels], k.pair[0:n, 0:levels, 0:n], ALU.mult)
                    v.tensor_tensor(pr[0:n, levels], o3[:, levels], k.pair[0:n, LEVELS, 0:n], ALU.mult).then_inc(L_drained, 1)
                v.wait_ge(L_drained, 4 * i + h + 3)
                v.tensor_reduce(AT[h][0:n, 0:n], pr[0:n].rearrange("p l n -> p n l"), AX.X, ALU.add).then_inc(at_ready, 1)

        @block.vector
        def _(v):
            st = Steps(v, dstep)
            v.sem_inc(L_drained, 2)
            v.memset(S[0][:, :, :], 0.0)
            v.memset(S[1][:, :, :], 0.0).then_inc(S_drained, 1)
            with v.Fori(0, NC) as i:
                st.loop(i, 2)
                dve_front(v, st, i, C, LEVELS, C)
                st.end(NC)
                v.wait_ge(S_filled, i + 1)
                for p in range(2):
                    for hh in range(2):
                        r = slice(64 * hh, 64 * hh + 64)
                        ins = v.scalar_tensor_tensor(S[p][r, hh, :], S[p][r, hh, :], E[p][r, LEVELS + 1, C - 1:C],
                                                     ps[r, 6, p * 256 + hh * P:p * 256 + (hh + 1) * P], ALU.mult, ALU.add)
                ins.then_inc(S_drained, 1)
                v.wait_ge(S_drained, i + 2)
            dve_front(v, st, NC, NS, 2, SL)
            for h in range(H):
                p, hh = divmod(h, 2)
                if h == 0:
                    v.wait_ge(shifted, 1)
                v.wait_ge(T_drained, 2 * NC + p + 3)
                v.tensor_tensor(vexp[h][0:NS, :].rearrange("p (b e) -> p b e", b=SB),
                                bcast(kdv[p][0:NS, 1 + hh, :].unsqueeze(1), SB, P),
                                bcast(k.inseq[0:NS, :].unsqueeze(2), SB, P), ALU.mult).then_inc(vexp_ready, 1)
            for n in range(2 * H):
                h, half = divmod(n, 2)
                v.wait_ge(S_filled, NC + n + 1)
                for b in range(4):
                    bb = 4 * half + b
                    ins = v.scalar_tensor_tensor(S0[h][:, bb, :], S0[h][:, bb, :],
                                                 head_f[0:GDK, h, bb * SL + SL - 1:bb * SL + SL],
                                                 ps[0:GDK, 6, b * P:(b + 1) * P], ALU.mult, ALU.add)
                ins.then_inc(S_drained, 1)

        @block.sync
        def _(sp):
            sp.wait_ge(L_filled, 4 * NC)
            for h in range(H):
                sp.dma_start(S0[h], a["state_gla"][0, :, h].rearrange("b d e -> d b e")).then_inc(s0_loaded[h], 16)
            sp.wait_ge(S_drained, NC + 1)
            for h in range(H):
                r = slice(64 * (h % 2), 64 * (h % 2) + 64)
                sp.dma_start(a["prompt_state_gla"][0, 0, h], S[h // 2][r, h % 2, :]).then_inc(stored, 16)
            sp.wait_ge(S_drained, NC + 1 + 2 * H)
            for h in range(H):
                sp.dma_start(a["sample_state_gla"][0, :, h].rearrange("b d e -> d b e"), S0[h]).then_inc(stored, 16)
            sp.wait_ge(stored, 16 * 2 * H)


def conformer(k):
    nc, a, ps = k.nc, k.a, k.ps
    w = Area(k.work[:, :])
    ring = w.take(2, KT, 2, P)
    sg, cin, cs = w.take(T), w.take(2, CFK + T), w.take(2, SB, CFK + SL)
    before, taps = w.take(CFC, SB * CFK), w.take(CFK + 1, CFC)
    prev_in, taps_in = w.take(2, CFC * P), w.take(P)
    last = w.take(2, CFC * P)
    tails = w.take(CFC, CFK + NS)
    sq, mean, rstd = w.take(2, T), w.take(T), w.take(T)
    HR = SB // 2 * CFK
    y = k.oT[:, 8:12, :]
    win = a["w_in"][0].rearrange("(k p) n -> p k n", p=P)
    w_loaded = [k.sem(f"cf_w_loaded{s}") for s in range(2)]
    st_loaded, st_turned, st_copied = k.sem("cf_state_loaded"), k.sem("cf_state_turned"), k.sem("cf_state_copied")
    a_filled, g_filled, glu_done, sig_done, conv_done = (k.sem("cf_" + x) for x in
                                                         ("a_filled", "g_filled", "glu_done", "sig_done", "conv_done"))
    tails_turned, tails_copied, summed, squared = (k.sem("cf_" + x) for x in ("tails_turned", "tails_copied", "summed", "squared"))
    by_dve, by_act, dstep, stored = (k.sem("cf_" + x) for x in ("by_dve", "by_act", "dve_step", "stored"))

    with nc.Block() as block:
        @block.sync
        def _(sp):
            def load(j):
                for m in range(2):
                    c0 = COL["conf"] + m * CFC * P + j * P
                    sp.dma_start(ring[:, j % 2, :, m, :], win[:, :, c0:c0 + P]).then_inc(w_loaded[j % 2], 16)
            load(0)
            load(1)
            rows = a["state_conv"][0].rearrange("b r c -> (b r) c")
            for m in range(2):
                sp.dma_start(prev_in[0:HR, m, :], rows[m * HR:(m + 1) * HR]).then_inc(st_loaded, 16)
            sp.dma_start(taps_in[0:(CFK + 1) * CFC, :], a["conf_dw_w"][0].rearrange("w (t p) -> (w t) p", p=P)).then_inc(st_loaded, 16)
            for j in range(2, CFC):
                sp.wait_ge(g_filled, j - 1)
                load(j)
            sp.dma_start(a["sample_state_conv"][0, :, 0:CFK - SL, :], a["state_conv"][0, :, SL:CFK, :]).then_inc(stored, 16)
            sp.wait_ge(tails_copied, 2)
            sp.dma_start(a["prompt_state_conv"][0, 0], last[0:CFK, 0, :]).then_inc(stored, 16)
            for b in range(SB):
                sp.dma_start(a["sample_state_conv"][0, b, CFK - SL:CFK, :], last[b * SL:(b + 1) * SL, 1, :]).then_inc(stored, 16)
            sp.wait_ge(stored, 16 * (2 + SB))

        @block.tensor
        def _(pe):
            pe.wait_ge(st_loaded, 48)
            for m in range(2):
                for t in range(CFC):
                    pe.transpose(ps[:, 6 + m, t * HR:(t + 1) * HR], prev_in[0:HR, m, t * P:(t + 1) * P], k.ident[0:HR, 0:HR])
            n = (CFK + 1) * CFC
            pe.transpose(ps[:, 0, 0:n], taps_in[0:n, :], k.ident[0:n, 0:n]).then_inc(st_turned, 1)
            pe.wait_ge(st_copied, 1)
            for j in range(CFC):
                pe.wait_ge(w_loaded[j % 2], 32 * (j // 2 + 1))
                for m, (filled, free) in enumerate(((a_filled, glu_done), (g_filled, sig_done))):
                    if j:
                        pe.wait_ge(free, j)
                    for c in range(NCH):
                        for q in range(KT):
                            ins = pe.matmul(ps[:, 3 * m + c, 0:CW], ring[:, j % 2, q, m, :], k.hT[:, q, c * CW:(c + 1) * CW],
                                            start=(q == 0), stop=(q == KT - 1))
                    ins.then_inc(filled, 1)
            pe.wait_ge(glu_done, CFC)
            pe.wait_ge(sig_done, CFC)
            for t in range(CFC):
                pe.wait_ge(conv_done, t + 1)
                for c in range(NCH):
                    ins = pe.matmul(ps[:, c, 0:CW], k.ones[:, :], y[:, t, c * CW:(c + 1) * CW], start=(t == 0), stop=(t == CFC - 1))
            ins.then_inc(summed, 1)
            for t in range(CFC):
                pe.transpose(ps[0:CFK, 6, t * P:(t + 1) * P], tails[:, t, 0:CFK], k.ident[:, :])
                ins = pe.transpose(ps[0:NS, 7, t * P:(t + 1) * P], tails[:, t, CFK:], k.ident[:, :])
            ins.then_inc(tails_turned, 1)
            for t in range(CFC):
                pe.wait_ge(squared, t + 1)
                for c in range(NCH):
                    ins = pe.matmul(ps[:, 3 + c, 0:CW], k.ones[:, :], sq[:, t % 2, c * CW:(c + 1) * CW], start=(t == 0), stop=(t == CFC - 1))
                ins.then_inc(summed, 1)

        @block.scalar
        def _(act):
            for j in range(CFC):
                act.wait_ge(g_filled, j + 1)
                if j:
                    act.wait_ge(glu_done, j)
                act.activation(chunks(sg), ps[:, 3:6, 0:CW], ACT.Sigmoid).then_inc(sig_done, 1)
            act.wait_ge(tails_turned, 1)
            act.activation(last[0:CFK, 0, :], ps[0:CFK, 6, :], ACT.Copy).then_inc(tails_copied, 1)
            act.activation(last[0:NS, 1, :], ps[0:NS, 7, :], ACT.Copy).then_inc(tails_copied, 1)
            for t in range(CFC):
                act.wait_ge(by_dve, 1 + t + 1)
                if t >= 2:
                    act.wait_ge(summed, 1 + t - 1)
                act.activation(sq[:, t % 2, :], y[:, t, :], ACT.Square).then_inc(squared, 1)
            act.wait_ge(by_dve, 2 + CFC)
            act.activation(rstd[:, :], rstd[:, :], ACT.Sqrt).then_inc(by_act, 1)
            for t in range(CFC):
                act.wait_ge(by_dve, 3 + CFC + t)
                act.activation(y[:, t, :], y[:, t, :], ACT.Silu, bias=k.column("conf_ln_b", t), scale=k.column("conf_ln_w", t))

        @block.vector
        def _(v):
            st = Steps(v, dstep)
            v.wait_ge(st_turned, 1)
            for m in range(2):
                v.tensor_copy(before[:, :, m * HR:(m + 1) * HR], ps[:, 6 + m, 0:CFC * HR].rearrange("p (t r) -> p t r", t=CFC))
            v.tensor_copy(taps[:, :, :].rearrange("p a b -> p (a b)"), ps[:, 0, 0:(CFK + 1) * CFC]).then_inc(st_copied, 1)
            st(v.memset(cin[:, :, 0:CFK], 0.0))
            v.wait_ge(st_copied, 1)
            for j in range(CFC):
                u = j % 2
                v.wait_ge(a_filled, j + 1)
                v.wait_ge(sig_done, j + 1)
                v.tensor_tensor(chunks(cin[:, u, CFK:]), ps[:, 0:3, 0:CW], chunks(sg), ALU.mult).then_inc(glu_done, 1)
                v.wait_ge(glu_done, j + 1)
                v.tensor_copy(cs[:, u, :, 0:CFK], before[:, j, :].rearrange("p (b r) -> p b r", b=SB))
                v.tensor_copy(tails[:, j, 0:CFK], cin[:, u, SEQ:SEQ + CFK])
                v.tensor_copy(tails[:, j, CFK:], cin[:, u, CFK + SEQ:CFK + T])
                st(v.tensor_copy(cs[:, u, :, CFK:], cin[:, u, CFK + SEQ:CFK + T].rearrange("p (b r) -> p b r", b=SB)))
                for tap in range(CFK + 1):
                    f = taps[:, tap, j:j + 1]
                    x, o = cin[:, u, tap:tap + SEQ], y[:, j, 0:SEQ]
                    xs, os = cs[:, u, :, tap:tap + SL], samples(y[:, j, :])
                    if tap == 0:
                        v.tensor_scalar(o, x, f, k.column("conf_dw_b", j), ALU.mult, ALU.add)
                        ins = v.tensor_scalar(os, xs, f, k.column("conf_dw_b", j), ALU.mult, ALU.add)
                    else:
                        v.scalar_tensor_tensor(o, x, f, o, ALU.mult, ALU.add)
                        ins = v.scalar_tensor_tensor(os, xs, f, os, ALU.mult, ALU.add)
                    if tap < CFK:
                        st(ins)
                ins.then_inc(conv_done, 1)
            v.wait_ge(conv_done, CFC)
            v.wait_ge(summed, 1)
            v.tensor_scalar(chunks(mean), ps[:, 0:3, 0:CW], 1.0 / (CFC * P), None, ALU.mult).then_inc(by_dve, 1)
            v.wait_ge(by_dve, 1)
            for t in range(CFC):
                v.tensor_tensor(y[:, t, :], y[:, t, :], mean[:, :], ALU.subtract).then_inc(by_dve, 1)
            v.wait_ge(summed, 1 + CFC)
            v.tensor_scalar(chunks(rstd), ps[:, 3:6, 0:CW], 1.0 / (CFC * P), EPS, ALU.mult, ALU.add).then_inc(by_dve, 1)
            v.wait_ge(by_act, 1)
            st(v.reciprocal(rstd[:, :], rstd[:, :]))
            v.wait_ge(by_dve, 2 + CFC)
            for t in range(CFC):
                v.tensor_tensor(y[:, t, :], y[:, t, :], rstd[:, :], ALU.mult).then_inc(by_dve, 1)


def merge(k):
    nc, a, ps = k.nc, k.a, k.ps
    w = Area(k.work[:, :])
    k.merged = w.take(KT, T)
    ring_g, ring_b, sig = w.take(3, KT, P), w.take(3, 4, P), w.take(3, T)
    win = a["w_in"][0].rearrange("(k p) n -> p k n", p=P)
    wb = a["w_branch"][0].rearrange("n (k p) c -> n p k c", p=P)
    w_loaded = [k.sem(f"mg_w_loaded{n}") for n in range(3)]
    g_filled, y_filled, sig_done, y_drained, step_merged = (
        k.sem("mg_" + x) for x in ("g_filled", "y_filled", "sig_done", "y_drained", "step_merged"))

    with nc.Block() as block:
        @block.sync
        def _(sp):
            def load(m, n):
                sp.dma_start(ring_g[:, n], win[:, :, bass.ds(m * P + (COL["br"] + n * D), P)]).then_inc(w_loaded[n], 16)
                sp.dma_start(ring_b[:, n], wb[n][:, :, bass.ds(m * P, P)]).then_inc(w_loaded[n], 16)
            for n in range(3):
                load(0, n)
            with sp.Fori(0, KT - 1) as m:
                for n in range(3):
                    sp.wait_ge(y_filled, m * 3 + (n + 1))
                    load(m + 1, n)

        @block.tensor
        def _(pe):
            with pe.Fori(0, KT) as m:
                for n in range(3):
                    pe.wait_ge(w_loaded[n], (m + 1) * 32)
                    pe.wait_ge(sig_done, m * 3 + (n + 1))
                    for c in range(NCH):
                        for j in range(KT):
                            ins = pe.matmul(ps[:, c, 0:CW], ring_g[:, n, j, :], k.hT[:, j, c * CW:(c + 1) * CW],
                                            start=(j == 0), stop=(j == KT - 1))
                    ins.then_inc(g_filled, 1)
                    pe.wait_ge(y_drained, m * 3 + (n + 1))
                    for c in range(NCH):
                        for j in range(4):
                            ins = pe.matmul(ps[:, 3 + c, 0:CW], ring_b[:, n, j, :], k.oT[:, 4 * n + j, c * CW:(c + 1) * CW],
                                            start=(j == 0), stop=(j == 3))
                    ins.then_inc(y_filled, 1)

        @block.scalar
        def _(act):
            act.sem_inc(sig_done, 1)
            with act.Fori(0, KT) as m:
                for n in range(3):
                    act.wait_ge(g_filled, m * 3 + (n + 1))
                    act.wait_ge(step_merged, m * 3 + (n + 1))
                    act.activation(chunks(sig[:, n, :]), ps[:, 0:3, 0:CW], ACT.Sigmoid).then_inc(sig_done, 1)

        @block.vector
        def _(v):
            v.sem_inc(y_drained, 1)
            v.sem_inc(step_merged, 3)
            with v.Fori(0, KT) as m:
                out = k.merged[:, bass.ds(m, 1), :].rearrange("p a t -> p (a t)")
                for n in range(3):
                    v.wait_ge(y_filled, m * 3 + (n + 1))
                    v.wait_ge(sig_done, m * 3 + (n + 2))
                    v.tensor_tensor(chunks(sig[:, n, :]), ps[:, 3:6, 0:CW], chunks(sig[:, n, :]), ALU.mult).then_inc(y_drained, 1)
                    v.wait_ge(y_drained, m * 3 + (n + 2))
                    if n == 0:
                        v.tensor_copy(out, sig[:, n, :]).then_inc(step_merged, 1)
                        continue
                    v.wait_ge(step_merged, m * 3 + (n + 3))
                    v.tensor_tensor(out, out, sig[:, n, :], ALU.add).then_inc(step_merged, 1)


def add_gated(v, k, st, m, slot, src):
    gate = k.mod[:, slot * KT + m, :]
    x = k.xT[:, m, :]
    tmp = k.gate_tmp
    n = SEQ - 2 * CW
    v.scalar_tensor_tensor(x[:, 0:2 * CW].rearrange("p (c w) -> p c w", c=2), src[:, 0:2, 0:CW], gate[:, 0:1],
                           x[:, 0:2 * CW].rearrange("p (c w) -> p c w", c=2), ALU.mult, ALU.add)
    v.scalar_tensor_tensor(x[:, 2 * CW:SEQ], src[:, 2, 0:n], gate[:, 0:1], x[:, 2 * CW:SEQ], ALU.mult, ALU.add)
    return v.tensor_tensor(tmp[:, m, :, :], src[:, 2, n:CW].rearrange("p (s l) -> p s l", l=SL),
                           bcast(gate[:, 1:NSEQ].unsqueeze(2), SB, SL), ALU.mult)


def project_out(k):
    nc, a, ps = k.nc, k.a, k.ps
    w = Area(k.work[:, KT * T:])
    ring = w.take(2, KT, 256)
    k.gate_tmp = w.take(KT, SB, SL)
    wo = a["w_out"][0].rearrange("(k p) n -> p k n", p=P)
    w_loaded = [k.sem(f"po_w_loaded{s}") for s in range(2)]
    filled, drained, dstep = k.sem("po_filled"), k.sem("po_drained"), k.sem("po_dve_step")
    with nc.Block() as block:
        @block.sync
        def _(sp):
            for b in range(4):
                if b >= 2:
                    sp.wait_ge(filled, 2 * (b - 1))
                sp.dma_start(ring[:, b % 2], wo[:, :, b * 256:(b + 1) * 256]).then_inc(w_loaded[b % 2], 16)

        @block.tensor
        def _(pe):
            for m in range(KT):
                b, u = divmod(m, 2)
                pe.wait_ge(w_loaded[b % 2], 16 * (b // 2 + 1))
                if m >= 2:
                    pe.wait_ge(drained, m - 1)
                for c in range(NCH):
                    for j in range(KT):
                        ins = pe.matmul(ps[:, 3 * u + c, 0:CW], ring[:, b % 2, j, u * P:(u + 1) * P],
                                        k.merged[:, j, c * CW:(c + 1) * CW], start=(j == 0), stop=(j == KT - 1))
                ins.then_inc(filled, 1)

        @block.vector
        def _(v):
            for m in range(KT):
                v.wait_ge(filled, m + 1)
                add_gated(v, k, None, m, 2, ps[:, 3 * (m % 2):3 * (m % 2) + 3, :]).then_inc(drained, 1)
            v.wait_ge(drained, KT)
            for m in range(KT):
                s = samples(k.xT[:, m, :])
                v.tensor_tensor(s, s, k.gate_tmp[:, m], ALU.add)


NT = 9
NG, TOPG, EG = 8, 4, 8


def router(k):
    nc, a, ps = k.nc, k.a, k.ps
    w = Area(k.work[:, :])
    k.gates = w.take(NT, E_N)
    k.work_after_gates = w.at
    rw, bias, brow = w.take(KT, E_N), w.take(E_N), w.take(E_N)
    s, sb, msk, rep = w.take(NT, E_N), w.take(NT, E_N), w.take(NT, E_N), w.take(NT, E_N)
    top2, grp = w.take(NT * NG, 8), w.take(NT, NG)
    gt, eq, before = w.take(NT, NG, NG), w.take(NT, NG, NG), w.take(NG, NG)
    rank, pen, top8, total = w.take(NT, NG), w.take(NT, NG), w.take(NT, 8), w.take(NT)
    loaded, filled, scored, bias_ready, dstep = (k.sem("rt_" + x) for x in ("loaded", "filled", "scored", "bias_ready", "dve_step"))

    with nc.Block() as block:
        @block.sync
        def _(sp):
            sp.dma_start(rw[:, :, :], a["router_w"][0].rearrange("(k p) e -> p k e", p=P)).then_inc(loaded, 16)
            sp.dma_start(brow[0:1, :], a["router_bias"]).then_inc(loaded, 16)

        @block.tensor
        def _(pe):
            pe.wait_ge(loaded, 32)
            for t in range(NT):
                n = P if t < 8 else NS
                out = ps[0:n, 0, t * E_N:(t + 1) * E_N] if t < 8 else ps[0:n, 1, 0:E_N]
                for j in range(KT):
                    pe.matmul(out, k.hT[:, j, t * P:t * P + n], rw[:, j, :], start=(j == 0), stop=(j == KT - 1))
            pe.matmul(ps[:, 2, 0:E_N], k.ones[0:1, :], brow[0:1, :], start=True, stop=True).then_inc(filled, 1)

        @block.scalar
        def _(act):
            act.wait_ge(bias_ready, 1)
            act.wait_ge(filled, 1)
            act.activation(s[:, 0:8, :].rearrange("p t e -> p (t e)"), ps[:, 0, :], ACT.Sigmoid)
            act.activation(s[0:NS, 8, :], ps[0:NS, 1, 0:E_N], ACT.Sigmoid).then_inc(scored, 1)

        @block.vector
        def _(v):
            st = Steps(v, dstep)
            st(v.memset(s[:, 8, :], 0.5))
            st(v.memset(before[:, :, :], 0.0))
            for i in range(1, NG):
                v.memset(before[:, i, 0:i], 1.0)
            v.wait_ge(filled, 1)
            v.tensor_copy(bias[:, :], ps[:, 2, 0:E_N]).then_inc(bias_ready, 1)
            v.wait_ge(bias_ready, 1)
            v.wait_ge(scored, 1)
            st(v.tensor_tensor(sb[:, :, :], s[:, :, :], bcast(bias.unsqueeze(1), NT, E_N), ALU.add))
            for t in range(NT):
                for g in range(NG):
                    ins = v.max(top2[:, t * NG + g, :], sb[:, t, g * EG:(g + 1) * EG])
            st(ins)
            pair = top2.rearrange("p (t g) e -> p t g e", g=NG)
            st(v.tensor_tensor(grp[:, :, :], pair[:, :, :, 0], pair[:, :, :, 1], ALU.add))
            mine, other = bcast(grp.unsqueeze(3), NT, NG, NG), bcast(grp.unsqueeze(2), NT, NG, NG)
            v.tensor_tensor(gt[:, :, :, :], other, mine, ALU.is_gt)
            st(v.tensor_tensor(eq[:, :, :, :], other, mine, ALU.is_equal))
            st(v.tensor_tensor(eq[:, :, :, :], eq[:, :, :, :], bcast(before.unsqueeze(1), NT, NG, NG), ALU.mult))
            st(v.tensor_tensor(gt[:, :, :, :], gt[:, :, :, :], eq[:, :, :, :], ALU.add))
            st(v.tensor_reduce(rank[:, :, :], gt[:, :, :, :], AX.X, ALU.add))
            st(v.tensor_scalar(pen[:, :, :], rank[:, :, :], float(TOPG) - 0.5, -1e30, ALU.is_gt, ALU.mult))
            st(v.tensor_tensor(msk.rearrange("p t (g e) -> p t g e", g=NG), sb.rearrange("p t (g e) -> p t g e", g=NG),
                               bcast(pen.unsqueeze(3), NT, NG, EG), ALU.add))
            for t in range(NT):
                ins = v.max(top8[:, t, :], msk[:, t, :])
            st(ins)
            for t in range(NT):
                ins = v.match_replace(out=rep[:, t, :], in_to_replace=top8[:, t, :], in_values=msk[:, t, :], imm_value=-3e38)
            st(ins)
            st(v.tensor_tensor(rep[:, :, :], rep[:, :, :], msk[:, :, :], ALU.not_equal))
            k.sel = rep
            st(v.tensor_tensor(k.gates[:, :, :], s[:, :, :], rep[:, :, :], ALU.mult))
            st(v.tensor_reduce(total[:, :], k.gates[:, :, :], AX.X, ALU.add))
            st(v.reciprocal(total[:, :], total[:, :]))
            st(v.tensor_scalar(total[:, :], total[:, :], 2.5, None, ALU.mult))
            st(v.tensor_tensor(k.gates[:, :, :], k.gates[:, :, :], bcast(total.unsqueeze(2), NT, E_N), ALU.mult))


def experts(k):
    nc, a, ps = k.nc, k.a, k.ps
    w = Area(k.work[:, k.work_after_gates:])
    k.y = w.take(KT, T)
    gT, sele = w.take(T), w.take(2, P)
    gb, sg, hid = w.take(T), w.take(T), w.take(2, T)
    ow = Area(k.oT[:, :, :].rearrange("p a b -> p (a b)"))
    wg, wu, wd = ow.take(2, KT, FF), ow.take(2, KT, FF), ow.take(2, 2, D)
    w_loaded = [k.sem(f"ex_w_loaded{s}") for s in range(2)]
    filled, adrained, vdrained, sel_ready, gT_ready, hid_ready, dstep = (
        k.sem("ex_" + x) for x in ("filled", "act_drained", "dve_drained", "sel_ready", "gT_ready", "hid_ready", "dstep"))
    ITEMS = [x for s in range(2) for x in [("gb", s, 0)] + [(n, s, f) for f in range(2) for n in "gu"] + [("d", s, m) for m in range(KT)]]
    NI = len(ITEMS)
    NA = sum(n in ("gb", "g") for n, _, _ in ITEMS)
    NV = NI - NA

    def drains(q):
        na = sum(n in ("gb", "g") for n, _, _ in ITEMS[:q + 1])
        return na, q + 1 - na

    with nc.Block() as block:
        def shared_items():
            return [(n, 0, f) for f in range(2) for n in "gu"] + [("d", 0, m) for m in range(KT)]
        SH = shared_items()

        @block.sync
        def _(sp):
            sp.dma_start(wg[:, 0], a["sh_w_gate"][0].rearrange("(k p) f -> p k f", p=P)).then_inc(w_loaded[0], 16)
            sp.dma_start(wu[:, 0], a["sh_w_up"][0].rearrange("(k p) f -> p k f", p=P)).then_inc(w_loaded[0], 16)
            sp.dma_start(wd[:, 0], a["sh_w_down"][0].rearrange("(k p) d -> p k d", p=P)).then_inc(w_loaded[0], 16)

            def load(e, s):
                sp.dma_start(wg[:, s], a["exp_w_gate"][0, bass.ds(e, 1)].rearrange("e (k p) f -> p (e k) f", p=P)).then_inc(w_loaded[s], 16)
                sp.dma_start(wu[:, s], a["exp_w_up"][0, bass.ds(e, 1)].rearrange("e (k p) f -> p (e k) f", p=P)).then_inc(w_loaded[s], 16)
                sp.dma_start(wd[:, s], a["exp_w_down"][0, bass.ds(e, 1)].rearrange("e (k p) d -> p (e k) d", p=P)).then_inc(w_loaded[s], 16)
            load(1, 1)
            sp.wait_ge(filled, len(SH))
            load(0, 0)
            with sp.Fori(0, E_N // 2 - 1) as i:
                for s in range(2):
                    sp.wait_ge(filled, i * NI + (len(SH) + 1 + (s + 1) * (NI // 2)))
                    load(i * 2 + (2 + s), s)

        @block.tensor
        def _(pe):
            def item(q, kind, s, x):
                out = ps[:, 3 * (q % 2):3 * (q % 2) + 3, 0:CW]
                for c in range(NCH):
                    cc = slice(c * CW, (c + 1) * CW)
                    if kind == "gb":
                        ins = pe.matmul(out[:, c, :], sele[0:E_N, s, :], gT[0:E_N, cc], start=True, stop=True)
                    elif kind in "gu":
                        ww = wg if kind == "g" else wu
                        for j in range(KT):
                            ins = pe.matmul(out[:, c, :], ww[:, s, j, x * P:(x + 1) * P], k.hT[:, j, cc], start=(j == 0), stop=(j == KT - 1))
                    else:
                        for j in range(2):
                            ins = pe.matmul(out[:, c, :], wd[:, s, j, x * P:(x + 1) * P], hid[:, j, cc], start=(j == 0), stop=(j == 1))
                ins.then_inc(filled, 1)
            pe.wait_ge(w_loaded[0], 48)
            na = nv = 0
            for q, (kind, s, x) in enumerate(SH):
                if q >= 2:
                    na, nv = sum(n == "g" for n, _, _ in SH[:q - 1]), sum(n != "g" for n, _, _ in SH[:q - 1])
                    pe.wait_ge(adrained, na)
                    if nv:
                        pe.wait_ge(vdrained, nv)
                if kind == "d" and x == 0:
                    pe.wait_ge(hid_ready, 1)
                item(q, kind, s, x)
            SA, SV = sum(n == "g" for n, _, _ in SH), sum(n != "g" for n, _, _ in SH)
            pe.wait_ge(vdrained, SV)
            for t in range(NT):
                n = P if t < 8 else NS
                bank, c0 = (3 if t < 4 else 4 if t < 8 else 5), (t % 4) * P
                ins = pe.transpose(ps[0:E_N, bank, c0:c0 + n], k.gates[0:n, t, :], k.ident[0:n, 0:n])
            ins.then_inc(filled, 1)
            with pe.Fori(0, E_N // 2) as i:
                for q, (kind, s, x) in enumerate(ITEMS):
                    if kind == "gb":
                        pe.wait_ge(sel_ready, i * 2 + (s + 1))
                        pe.wait_ge(gT_ready, 1)
                    if kind == "g" and x == 0:
                        pe.wait_ge(w_loaded[s], (i + (2 - s)) * 48)
                    if kind == "d" and x == 0:
                        pe.wait_ge(hid_ready, i * 2 + (s + 2))
                    na, nv = drains(q - 2) if q >= 2 else tuple(x - y for x, y in zip(drains(NI - 2 + q), (NA, NV)))
                    pe.wait_ge(adrained, i * NA + (SA + na))
                    pe.wait_ge(vdrained, i * NV + (SV + nv))
                    item(q, kind, s, x)

        @block.scalar
        def _(act):

            for q, (kind, s, x) in enumerate(SH):
                if kind == "g":
                    act.wait_ge(filled, q + 1)
                    if x == 1:
                        act.wait_ge(vdrained, 1)
                    act.activation(chunks(sg), ps[:, 3 * (q % 2):3 * (q % 2) + 3, 0:CW], ACT.Silu).then_inc(adrained, 1)
            SA = 2
            with act.Fori(0, E_N // 2) as i:
                for q, (kind, s, x) in enumerate(ITEMS):
                    if kind not in ("gb", "g"):
                        continue
                    act.wait_ge(filled, i * NI + (len(SH) + 1 + q + 1))
                    src = ps[:, 3 * (q % 2):3 * (q % 2) + 3, 0:CW]
                    nv = drains(q)[1] if q else 0
                    if kind == "g":
                        act.wait_ge(vdrained, i * NV + (len(SH) - 2 + nv))
                        act.activation(chunks(sg), src, ACT.Silu).then_inc(adrained, 1)
                    else:
                        act.wait_ge(hid_ready, i * 2 + (s + 1))
                        act.activation(chunks(gb), src, ACT.Copy).then_inc(adrained, 1)

        @block.vector
        def _(v):
            st = Steps(v, dstep)

            nv = 0
            for q, (kind, s, x) in enumerate(SH):
                src = ps[:, 3 * (q % 2):3 * (q % 2) + 3, 0:CW]
                if kind == "u":
                    v.wait_ge(filled, q + 1)
                    v.wait_ge(adrained, x + 1)
                    v.tensor_tensor(chunks(hid[:, x, :]), src, chunks(sg), ALU.mult).then_inc(vdrained, 1)
                    nv += 1
                    if x == 1:
                        v.wait_ge(vdrained, 2)
                        v.sem_inc(hid_ready, 1)
                elif kind == "d":
                    v.wait_ge(filled, q + 1)
                    v.tensor_copy(chunks(k.y[:, x, :]), src).then_inc(vdrained, 1)
                    nv += 1
            v.wait_ge(filled, len(SH) + 1)
            v.tensor_copy(gT[0:E_N, 0:1024].rearrange("p (a b) -> p a b", a=2), ps[0:E_N, 3:5, :])
            v.tensor_copy(gT[0:E_N, SEQ:T], ps[0:E_N, 5, 0:NS]).then_inc(gT_ready, 1)
            SV = len(SH) - 2
            with v.Fori(0, E_N // 2) as i:
                st.loop(i, 4)
                for q, (kind, s, x) in enumerate(ITEMS):
                    src = ps[:, 3 * (q % 2):3 * (q % 2) + 3, 0:CW]
                    if kind == "gb":
                        v.tensor_copy(sele[0:E_N, s, :], bcast(k.ident[0:E_N, bass.ds(i * 2 + s, 1)], P)).then_inc(sel_ready, 1)
                    elif kind == "u":
                        na, nvv = drains(q)
                        v.wait_ge(adrained, i * NA + (2 + na))
                        st(v.tensor_tensor(sg[:, :], sg[:, :], gb[:, :], ALU.mult))
                        v.wait_ge(filled, i * NI + (len(SH) + 1 + q + 1))
                        v.tensor_tensor(chunks(hid[:, x, :]), src, chunks(sg), ALU.mult).then_inc(vdrained, 1)
                        if x == 1:
                            v.wait_ge(vdrained, i * NV + (SV + nvv))
                            v.sem_inc(hid_ready, 1)
                    elif kind == "d":
                        na, nvv = drains(q)
                        v.wait_ge(filled, i * NI + (len(SH) + 1 + q + 1))
                        if x == 0:
                            v.wait_ge(vdrained, i * NV + (SV + nvv - 1))
                        v.tensor_tensor(chunks(k.y[:, x, :]), src, chunks(k.y[:, x, :]), ALU.add).then_inc(vdrained, 1)
                st.end(E_N // 2)


def add_moe(k):
    nc = k.nc
    dstep = k.sem("am_step")
    with nc.Block() as block:
        @block.vector
        def _(v):
            st = Steps(v, dstep)
            for m in range(KT):
                gate = k.mod[:, 5 * KT + m, :]
                x = k.xT[:, m, :]
                v.scalar_tensor_tensor(x[:, 0:SEQ], k.y[:, m, 0:SEQ], gate[:, 0:1], x[:, 0:SEQ], ALU.mult, ALU.add)
                ys = samples(k.y[:, m, :])
                st.done(v.tensor_tensor(ys, ys, bcast(gate[:, 1:NSEQ].unsqueeze(2), SB, SL), ALU.mult))
            st.wait()
            for m in range(KT):
                s = samples(k.xT[:, m, :])
                v.tensor_tensor(s, s, samples(k.y[:, m, :]), ALU.add)


def store_y(k):
    nc, a, ps = k.nc, k.a, k.ps
    rows = Area(k.oT[:, :, :].rearrange("p a b -> p (a b)")).take(9, D)
    filled, drained_a, drained_v, stored = k.sem("sy_filled"), k.sem("sy_by_act"), k.sem("sy_by_dve"), k.sem("sy_stored")
    with nc.Block() as block:
        @block.tensor
        def _(pe):
            for t in range(NT):
                n = P if t < 8 else NS
                for half in range(2):
                    if t >= 2:
                        pe.wait_ge(drained_v if half else drained_a, t - 1)
                    for j in range(4):
                        ins = pe.transpose(ps[0:n, 2 * (t % 2) + half, j * P:(j + 1) * P], k.hT[:, 4 * half + j, t * P:t * P + n], k.ident[:, :])
                    ins.then_inc(filled, 1)

        @block.scalar
        def _(act):
            for t in range(NT):
                n = P if t < 8 else NS
                act.wait_ge(filled, 2 * t + 1)
                act.activation(rows[0:n, t, 0:512], ps[0:n, 2 * (t % 2), :], ACT.Copy).then_inc(drained_a, 1)

        @block.vector
        def _(v):
            for t in range(NT):
                n = P if t < 8 else NS
                v.wait_ge(filled, 2 * t + 2)
                v.tensor_copy(rows[0:n, t, 512:D], ps[0:n, 2 * (t % 2) + 1, :]).then_inc(drained_v, 1)

        @block.sync
        def _(sp):
            for t in range(NT):
                sp.wait_ge(drained_a, t + 1)
                sp.wait_ge(drained_v, t + 1)
                if t < 8:
                    sp.dma_start(a["y_prompt"][0, t * P:(t + 1) * P, :], rows[:, t, :]).then_inc(stored, 16)
                else:
                    sp.dma_start(a["y_sample"].rearrange("s l d -> (s l) d"), rows[0:NS, t, :]).then_inc(stored, 16)
            sp.wait_ge(stored, 16 * NT)


def step_program(nc, a):
    with ExitStack() as ctx:
        k = Core(nc, ctx, a)
        setup(k)
        norm(k, "mix", 0)
        delta_project(k)
        delta_rows(k)
        delta_rule(k)
        gated_norm(k, "dn", k.qkv[:, 2 * H:3 * H, :], k.oT[:, 0:H, :], k.column("dn_norm_w"), Area(k.work[:, 0:2 * H * T]))
        gla_project(k)
        gla_rule(k)
        gated_norm(k, "gn", k.gla[:, 4:8, :], k.oT[:, 4:8, :], k.column("gla_norm_w"), Area(k.work[:, 0:4 * T]))
        k.fresh_semaphores()
        conformer(k)
        merge(k)
        project_out(k)
        norm(k, "ffn", 3)
        router(k)
        experts(k)
        add_moe(k)
        norm(k, "final", None)
        store_y(k)
        k.fresh_semaphores()


INS = ["x_prompt", "x_sample", "state_delta", "state_delta_conv", "state_gla", "state_conv", "c_prompt", "c_sample",
       "ada_w", "ada_b", "norm_mix_w", "w_in", "dn_conv_w", "dn_A_log", "dn_dt_bias", "dn_norm_w", "gla_gate_w",
       "gla_gate_b", "gla_norm_w", "conf_dw_w", "conf_dw_b", "conf_ln_w", "conf_ln_b", "w_branch", "w_out",
       "norm_ffn_w", "router_w", "router_bias", "exp_w_gate", "exp_w_up", "exp_w_down", "sh_w_gate", "sh_w_up",
       "sh_w_down", "final_norm_w"]


def kernel(**inputs):
    import numpy as np
    import concourse.bacc as bacc
    from concourse.bass_utils import run_bass_kernel_spmd

    nc = bacc.Bacc("TRN2", target_bir_lowering=False, num_devices=1)
    arrays, a = {}, {}
    for name in INS:
        x = np.ascontiguousarray(inputs[name])
        arrays[f"in_{name}"] = x
        a[name] = nc.dram_tensor(f"in_{name}", x.shape, mybir.dt.from_np(x.dtype), kind="ExternalInput").ap()
    for name, shape in OUTS:
        a[name] = nc.dram_tensor(f"out_{name}", shape, F32, kind="ExternalOutput").ap()
    step_program(nc, a)
    r = run_bass_kernel_spmd(nc, [arrays], core_ids=[0])
    return tuple(r.results[0][f"out_{name}"] for name, _ in OUTS)
```

```python
from contextlib import ExitStack

import concourse.bass as bass
from concourse import mybir

F32 = mybir.dt.float32
ACT = mybir.ActivationFunctionType
ALU = mybir.AluOpType
AX = mybir.AxisListType

P = 128
D = 1024
KT = D // P
SEQ = 1024
SB, SL = 8, 4
NS = SB * SL
T = SEQ + NS
NCH = 3
CW = T // NCH
C = 128
NC = SEQ // C
H = 4
LEVELS = 7
DNK, DNC = 3, 12
GDK = 64
CFK, CFC = 30, 4
NSEQ = 1 + SB
E_N, FF = 64, 256
EPS = 1e-6
COL = dict(qkv=0, z=1536, ba=2048, gqk=2056, gv=2568, gr=3080, glr=3592, conf=3608, br=4632)
RB, RG, RT, RE = 0, 32, 64, 96

PRM = {}
_at = 0
for _name, _n in (("ada_b", 48), ("norm_mix_w", 8), ("norm_ffn_w", 8), ("final_norm_w", 8), ("conf_dw_b", 4),
                  ("conf_ln_w", 4), ("conf_ln_b", 4), ("dn_norm_w", 1), ("gla_norm_w", 1), ("gla_gate_b", 2)):
    PRM[_name] = _at
    _at += _n
N_PRM = _at
WORK = 17920


class Area:

    def __init__(self, ap):
        self.ap, self.at, self.size = ap, 0, ap.shape[1]

    def take(self, *shape):
        n = 1
        for s in shape:
            n *= s
        piece = self.ap[:, self.at:self.at + n]
        self.at += n
        assert self.at <= self.size, (self.at, self.size)
        if len(shape) == 1:
            return piece
        names = "abcd"[:len(shape)]
        return piece.rearrange(f"p ({' '.join(names)}) -> p {' '.join(names)}", **dict(zip(names, shape)))


class Steps:

    def __init__(self, eng, sem):
        self.eng, self.sem, self.n, self.base = eng, sem, 0, 0

    def loop(self, i, per):
        self.base, self.first, self.per = self.n + i * per, self.n, per
        self.n = 0

    def end(self, count):
        assert self.n == self.per, (self.n, self.per)
        self.n, self.base = self.first + self.per * count, 0

    def done(self, ins):
        ins.then_inc(self.sem, 1)
        self.n += 1

    def wait(self):
        self.eng.wait_ge(self.sem, self.base + self.n)

    def __call__(self, ins):
        self.done(ins)
        self.wait()


def chunks(ap):
    return ap.rearrange("p (c w) -> p c w", c=NCH)


def wait_before_addressed(eng, sem, value, passed):
    eng.wait_ge(sem, value)
    eng.sem_inc(passed, 1)


def bcast(ap, *shape):
    return ap.to_broadcast([ap.shape[0], *shape])


def samples(ap):
    return ap[:, SEQ:T].rearrange("p (s l) -> p s l", l=SL)


class Core:
    def __init__(self, nc, ctx, a):
        self.nc, self.ctx, self.a = nc, ctx, a
        self.sems = []
        sb = lambda name, *shape: ctx.enter_context(nc.sbuf_tensor(name, [P, *shape], F32))
        self.xT = sb("xT", KT, T)
        self.hT = sb("hT", KT, T)
        self.big = sb("big", 12 * T + WORK)
        self.oT = self.big[:, 0:12 * T].rearrange("p (a b) -> p a b", b=T)
        self.work = self.big[:, 12 * T:]
        self.ident = sb("ident", P)
        self.ones = sb("ones", P)
        self.pair = sb("pair", LEVELS + 1, C)
        self.causal = sb("causal", C)
        self.causal_s = sb("causal_s", NS)
        self.inseq = sb("inseq", SB)
        self.carry = sb("carry", T)
        self.pick = sb("pick", 3 * H, P)
        self.pick8 = sb("pick8", 8, P)
        self.unit8 = sb("unit8", 8, 8)
        self.prm = sb("prm", P)
        self.mod = sb("mod", 6 * KT, NSEQ)
        self.ps = ctx.enter_context(nc.psum_tensor("ps", [P, 8, 512], F32))

    def sem(self, name):
        self.sems.append(self.nc.alloc_semaphore(name))
        return self.sems[-1]

    def fresh_semaphores(self):
        self.nc.all_engine_barrier()
        self.nc.clear_and_free_semaphores(self.sems)
        self.nc.all_engine_barrier()
        self.sems = []

    def column(self, name, n=0):
        return self.prm[:, PRM[name] + n:PRM[name] + n + 1]


def setup(k):
    nc, a, ps = k.nc, k.a, k.ps
    w = Area(k.work[:, :])
    xin = w.take(9, D)
    prm_in = w.take(P)
    cin = w.take(D)
    csl = w.take(D)
    cT = w.take(KT, NSEQ)
    ring = k.oT[:, :, :].rearrange("p a b -> p (a b)")[:, 0:6 * 2048].rearrange("p (s k n) -> p s k n", s=6, k=KT)
    NR = 6
    NB = 6 * D // 256
    x_loaded, prm_loaded, c_loaded = k.sem("x_loaded"), k.sem("prm_loaded"), k.sem("c_loaded")
    ada_loaded = [k.sem(f"ada_loaded{s}") for s in range(NR)]
    consts_done, pool_step = k.sem("consts_done"), k.sem("setup_pool_step")
    ones_done, silu_done = k.sem("ones_done"), k.sem("silu_c_done")
    x_turned, x_copied = k.sem("x_turned"), k.sem("x_copied")
    p_turned, p_copied = k.sem("p_turned"), k.sem("p_copied")
    x_copied_v = k.sem("x_copied_by_vector")
    mod_done, dstep = k.sem("mod_done"), k.sem("setup_dve_step")
    ada = a["ada_w"][0].rearrange("(k p) n -> p k n", p=P)

    with nc.Block() as block:
        @block.sync
        def _(sp):
            for name, n in (("ada_b", 48), ("norm_mix_w", 8), ("norm_ffn_w", 8), ("conf_dw_b", 4), ("conf_ln_w", 4),
                            ("conf_ln_b", 4), ("dn_norm_w", 1), ("gla_norm_w", 1), ("gla_gate_b", 2)):
                src = a[name][0].rearrange("(n p) -> n p", p=P)
                sp.dma_start(prm_in[PRM[name]:PRM[name] + n, :], src).then_inc(prm_loaded, 16)
            r = PRM["final_norm_w"]
            sp.dma_start(prm_in[r:r + 8, :], a["final_norm_w"].rearrange("(n p) -> n p", p=P)).then_inc(prm_loaded, 16)
            sp.dma_start(cin[0:1, :], a["c_prompt"]).then_inc(c_loaded, 16)
            sp.dma_start(cin[1:NSEQ, :], a["c_sample"]).then_inc(c_loaded, 16)
            for s in range(NR):
                sp.dma_start(ring[:, s], ada[:, :, s * 256:(s + 1) * 256]).then_inc(ada_loaded[s], 16)
            sp.dma_start(xin[:, 0:8, :], a["x_prompt"][0].rearrange("(t p) d -> p t d", p=P)).then_inc(x_loaded, 16)
            sp.dma_start(xin[0:NS, 8, :], a["x_sample"].rearrange("s l d -> (s l) d")).then_inc(x_loaded, 16)
            with sp.Fori(0, NB // NR - 1) as i:
                for s in range(NR):
                    sp.wait_ge(mod_done, i * NR + (s + 1))
                    sp.dma_start(ring[:, s], ada[:, :, bass.ds((i + 1) * (NR * 256) + s * 256, 256)])\
                      .then_inc(ada_loaded[s], 16)

        @block.gpsimd
        def _(g):
            st = Steps(g, pool_step)
            g.memset(k.ident[:, :], 0.0)
            g.memset(k.pair[:, :, :], 0.0)
            g.memset(k.causal[:, :], 1.0)
            g.memset(k.causal_s[:, :], 1.0)
            g.memset(k.inseq[:, :], 1.0)
            g.memset(k.unit8[:, :, :], 0.0)
            g.memset(k.carry[:, :], 1.0)
            st(g.memset(k.ones[:, :], 1.0))
            g.affine_select(out=k.ident[:, :], in_=k.ident[:, :], compare_op=ALU.not_equal, fill=1.0,
                            base=0, pattern=[[-1, P]], channel_multiplier=1)
            g.affine_select(out=k.causal[:, :], in_=k.causal[:, :], compare_op=ALU.is_ge, fill=0.0,
                            base=0, pattern=[[1, C]], channel_multiplier=-1)
            for l in range(LEVELS):
                s = 1 << l
                v = k.pair[:, l, :].rearrange("p (b h r) -> p b h r", h=2, r=s)
                g.memset(v[:, :, 1, :], 1.0)
            g.memset(k.unit8[:, :, :].rearrange("p a b -> p (a b)")[:, 0:64:9], 1.0)
            st(g.memset(k.carry[:, 0:SEQ:C], 0.0))
            g.memset(k.carry[:, SEQ:T:SL], 0.0)
            for l in range(LEVELS):
                s = 1 << l
                v = k.pair[:, l, :].rearrange("p (b h r) -> p b h r", h=2, r=s)[:, :, 1, :]
                g.affine_select(out=v, in_=v, compare_op=ALU.is_ge, fill=0.0, base=0,
                                pattern=[[-2 * s, C // (2 * s)], [0, s]], channel_multiplier=1)
            cs = k.causal_s[:, :].rearrange("p (b r) -> p b r", r=SL)
            g.affine_select(out=cs, in_=cs, compare_op=ALU.is_ge, fill=0.0, base=0,
                            pattern=[[SL, SB], [1, SL]], channel_multiplier=-1)
            g.affine_select(out=k.inseq[:, :], in_=k.inseq[:, :], compare_op=ALU.is_ge, fill=0.0, base=0,
                            pattern=[[-SL, SB]], channel_multiplier=1)
            st(g.tensor_copy(k.pair[:, LEVELS, :], k.ident[:, :]))
            for l in range(LEVELS):
                s = 1 << l
                v = k.pair[:, l, :].rearrange("p (b h r) -> p b h r", h=2, r=s)[:, :, 1, :]
                g.affine_select(out=v, in_=v, compare_op=ALU.is_ge, fill=0.0, base=s - 1,
                                pattern=[[2 * s, C // (2 * s)], [0, s]], channel_multiplier=-1)
            g.affine_select(out=cs, in_=cs, compare_op=ALU.is_ge, fill=0.0, base=0,
                            pattern=[[-SL, SB], [0, SL]], channel_multiplier=1)
            g.affine_select(out=k.inseq[:, :], in_=k.inseq[:, :], compare_op=ALU.is_ge, fill=0.0, base=SL - 1,
                            pattern=[[SL, SB]], channel_multiplier=-1)
            for h in range(H):
                for n, r in enumerate((RG + h, RB + h, RE + h)):
                    g.tensor_copy(k.pick[:, 3 * h + n, :], bcast(k.ident[:, r:r + 1], P))
            for j in range(8):
                ins = g.tensor_copy(k.pick8[0:8, j, :], bcast(k.ident[0:8, j:j + 1], P))
            ins.then_inc(consts_done, 1)

        @block.scalar
        def _(act):
            act.wait_ge(c_loaded, 32)
            act.activation(csl[0:NSEQ, :], cin[0:NSEQ, :], ACT.Silu).then_inc(silu_done, 1)
            for t in range(9):
                n = P if t < 8 else NS
                act.wait_ge(x_turned, 2 * t + 2)
                act.activation(k.xT[:, 4:8, t * P:t * P + n], ps[:, 3, :].rearrange("p (k n) -> p k n", k=4)[:, :, 0:n],
                               ACT.Copy).then_inc(x_copied, 1)

        @block.tensor
        def _(pe):
            pe.wait_ge(consts_done, 1)
            pe.wait_ge(prm_loaded, 160)
            pe.transpose(ps[:, 0, 0:N_PRM], prm_in[0:N_PRM, :], k.ident[0:N_PRM, 0:N_PRM]).then_inc(p_turned, 1)
            pe.wait_ge(silu_done, 1)
            for j in range(KT):
                ins = pe.transpose(ps[:, 1, j * NSEQ:(j + 1) * NSEQ], csl[0:NSEQ, j * P:(j + 1) * P],
                                   k.ident[0:NSEQ, 0:NSEQ])
            ins.then_inc(p_turned, 1)
            pe.wait_ge(p_copied, 2)
            with pe.Fori(0, NB // NR) as i:
                for s in range(NR):
                    pe.wait_ge(ada_loaded[s], (i + 1) * 16)
                    for u in range(2):
                        for j in range(KT):
                            ins = pe.matmul(ps[:, 0, bass.ds(i * (2 * NR * NSEQ) + (2 * s + u) * NSEQ, NSEQ)],
                                            ring[:, s, j, u * P:(u + 1) * P], cT[:, j, :],
                                            start=(j == 0), stop=(j == KT - 1))
                    ins.then_inc(mod_done, 1)
            pe.wait_ge(x_loaded, 32)
            for t in range(9):
                n = P if t < 8 else NS
                for half in range(2):
                    if t:
                        pe.wait_ge(x_copied if half else x_copied_v, t)
                    for j in range(4):
                        ins = pe.transpose(ps[:, 2 + half, j * P:j * P + n],
                                           xin[0:n, t, (4 * half + j) * P:(4 * half + j + 1) * P],
                                           k.ident[0:n, 0:n])
                    ins.then_inc(x_turned, 1)

        @block.vector
        def _(v):
            st = Steps(v, dstep)
            v.wait_ge(p_turned, 1)
            v.tensor_copy(k.prm[:, 0:N_PRM], ps[:, 0, 0:N_PRM]).then_inc(p_copied, 1)
            v.wait_ge(p_turned, 2)
            v.tensor_copy(cT[:, :, :].rearrange("p a b -> p (a b)"), ps[:, 1, 0:KT * NSEQ]).then_inc(p_copied, 1)
            v.wait_ge(mod_done, NB)
            v.wait_ge(p_copied, 2)
            st(v.tensor_tensor(k.mod[:, :, :], ps[:, 0, 0:48 * NSEQ].rearrange("p (a b) -> p a b", b=NSEQ),
                               bcast(k.prm[:, 0:48].unsqueeze(2), 48, NSEQ), ALU.add))
            for slot, name in ((1, "norm_mix_w"), (4, "norm_ffn_w")):
                m = k.mod[:, slot * KT:(slot + 1) * KT, :]
                st.done(v.scalar_tensor_tensor(m, m, 1.0, bcast(k.prm[:, PRM[name]:PRM[name] + 8].unsqueeze(2), 8, NSEQ),
                                       ALU.add, ALU.mult))
            for t in range(9):
                n = P if t < 8 else NS
                v.wait_ge(x_turned, 2 * t + 1)
                v.tensor_copy(k.xT[:, 0:4, t * P:t * P + n], ps[:, 2, :].rearrange("p (k n) -> p k n", k=4)[:, :, 0:n])\
                 .then_inc(x_copied_v, 1)


def norm(k, tag, slot):
    nc, ps = k.nc, k.ps
    w = Area(k.work[:, :])
    sq = w.take(2, T)
    rstd = w.take(T)
    squared, summed, rooted = k.sem(tag + "_squared"), k.sem(tag + "_summed"), k.sem(tag + "_rooted")
    scaled, dstep = k.sem(tag + "_mean"), k.sem(tag + "_dve_step")

    with nc.Block() as block:
        @block.scalar
        def _(act):
            for j in range(KT):
                if j >= 2:
                    act.wait_ge(summed, j - 1)
                act.activation(sq[:, j % 2, :], k.xT[:, j, :], ACT.Square).then_inc(squared, 1)
            act.wait_ge(scaled, 1)
            act.activation(rstd[:, :], rstd[:, :], ACT.Sqrt).then_inc(rooted, 1)

        @block.tensor
        def _(pe):
            for j in range(KT):
                pe.wait_ge(squared, j + 1)
                for c in range(NCH):
                    ins = pe.matmul(ps[:, c, 0:CW], k.ones[:, :], sq[:, j % 2, c * CW:(c + 1) * CW],
                                    start=(j == 0), stop=(j == KT - 1))
                ins.then_inc(summed, 1)

        @block.vector
        def _(v):
            st = Steps(v, dstep)
            v.wait_ge(summed, KT)
            v.tensor_scalar(chunks(rstd), ps[:, 0:NCH, 0:CW], 1.0 / D, EPS, ALU.mult, ALU.add).then_inc(scaled, 1)
            v.wait_ge(rooted, 1)
            st(v.reciprocal(rstd[:, :], rstd[:, :]))
            for j in range(KT):
                if slot is None:
                    st.done(v.scalar_tensor_tensor(k.hT[:, j, :], k.xT[:, j, :], k.column("final_norm_w", j), rstd[:, :],
                                           ALU.mult, ALU.mult))
                    continue
                st.done(v.tensor_tensor(k.hT[:, j, :], k.xT[:, j, :], rstd[:, :], ALU.mult))
            if slot is not None:
                st.wait()
                shift = k.mod[:, slot * KT:(slot + 1) * KT, :]
                scale = k.mod[:, (slot + 1) * KT:(slot + 2) * KT, :]
                for j in range(KT):
                    v.tensor_scalar(k.hT[:, j, 0:SEQ], k.hT[:, j, 0:SEQ], scale[:, j, 0:1], shift[:, j, 0:1],
                                    ALU.mult, ALU.add)
                    s = samples(k.hT[:, j, :])
                    st.done(v.tensor_tensor(s, s, bcast(scale[:, j, 1:NSEQ].unsqueeze(2), SB, SL), ALU.mult))
                st.wait()
                for j in range(KT):
                    s = samples(k.hT[:, j, :])
                    st.done(v.tensor_tensor(s, s, bcast(shift[:, j, 1:NSEQ].unsqueeze(2), SB, SL), ALU.add))


def delta_project(k):
    nc, a, ps = k.nc, k.a, k.ps
    w = Area(k.work[:, :])
    k.qkv = w.take(DNC, T)
    k.work_after_qkv = w.at
    acc = w.take(2, T)
    tails = w.take(DNC, DNK * NSEQ)
    spare = Area(k.oT[:, 4:12, :].rearrange("p a b -> p (a b)"))
    ring = spare.take(2, KT, 256)
    cin = spare.take(2, DNK + T)
    cs = spare.take(2, SB, DNK + SL)
    sacc = spare.take(2, SB, SL)
    taps = spare.take((DNK + 1) * DNC)
    before = spare.take(DNC, SB, DNK)
    prev_in = w.take(D + 512)
    taps_in = prev_in[64:64 + 4 * DNC, 0:P]
    tails_rows = acc[:, :, :].rearrange("p a b -> p (a b)")[:, 0:DNC * P]
    win = a["w_in"][0].rearrange("(k p) n -> p k n", p=P)
    w_loaded = [k.sem(f"qkv_w_loaded{s}") for s in range(2)]
    filled = [k.sem(f"qkv_filled{u}") for u in range(2)]
    emptied = [k.sem(f"qkv_emptied{u}") for u in range(2)]
    conv_done = [k.sem(f"qkv_conv_done{u}") for u in range(2)]
    silu_done, dstep, astep = k.sem("qkv_silu_done"), k.sem("qkv_dve_step"), k.sem("qkv_act_step")
    st_loaded, st_turned, st_copied = k.sem("dn_state_loaded"), k.sem("dn_state_turned"), k.sem("dn_state_copied")
    tails_turned, tails_copied = k.sem("dn_tails_turned"), k.sem("dn_tails_copied")
    stored = k.sem("dn_conv_state_stored")
    act_passed = k.sem("qkv_act_passed")
    NBQ, NBZ = DNC // 2, 2

    with nc.Block() as block:
        @block.sync
        def _(sp):
            for s in range(2):
                sp.dma_start(ring[:, s], win[:, :, s * 256:(s + 1) * 256]).then_inc(w_loaded[s], 16)
            sp.dma_start(prev_in[0:SB * DNK, :], a["state_delta_conv"][0].rearrange("b r c -> (b r) c")).then_inc(st_loaded, 16)
            sp.dma_start(taps_in, a["dn_conv_w"][0].rearrange("w (t p) -> (w t) p", p=P)).then_inc(st_loaded, 16)
            with sp.Fori(0, (NBQ + NBZ) // 2 - 1) as i:
                for s in range(2):
                    sp.wait_ge(filled[1], i * 2 + (s + 1))
                    sp.dma_start(ring[:, s], win[:, :, bass.ds(i * 512 + (2 + s) * 256, 256)]).then_inc(w_loaded[s], 16)
            sp.wait_ge(tails_copied, 2)
            sp.dma_start(a["prompt_state_delta_conv"][0, 0], tails_rows[0:DNK, :]).then_inc(stored, 16)
            sp.dma_start(a["sample_state_delta_conv"][0].rearrange("b r c -> (b r) c"),
                         tails_rows[32:32 + SB * DNK, :]).then_inc(stored, 16)
            sp.wait_ge(stored, 32)

        @block.tensor
        def _(pe):
            pe.wait_ge(st_loaded, 32)
            for t in range(DNC):
                pe.transpose(ps[:, 6, t * SB * DNK:(t + 1) * SB * DNK], prev_in[0:SB * DNK, t * P:(t + 1) * P],
                             k.ident[0:SB * DNK, 0:SB * DNK])
            pe.transpose(ps[:, 7, 0:4 * DNC], taps_in, k.ident[64:64 + 4 * DNC, 64:64 + 4 * DNC]).then_inc(st_turned, 1)

            def block_of(i, s, b):
                pe.wait_ge(w_loaded[s], (i + 1) * 16)
                for u in range(2):
                    pe.wait_ge(emptied[u], b + 1)
                    for c in range(NCH):
                        for j in range(KT):
                            ins = pe.matmul(ps[:, 3 * u + c, 0:CW], ring[:, s, j, u * P:(u + 1) * P],
                                            k.hT[:, j, c * CW:(c + 1) * CW], start=(j == 0), stop=(j == KT - 1))
                    ins.then_inc(filled[u], 1)

            with pe.Fori(0, (NBQ + NBZ) // 2) as i:
                for s in range(2):
                    block_of(i, s, i * 2 + s)
            pe.wait_ge(conv_done[0], NBQ + 1)
            pe.wait_ge(conv_done[1], NBQ + 1)
            pe.wait_ge(emptied[0], NBQ + NBZ + 1)
            pe.wait_ge(emptied[1], NBQ + NBZ + 1)
            for t in range(DNC):
                pe.transpose(ps[0:DNK, t // 4, (t % 4) * P:(t % 4 + 1) * P], tails[:, t, 0:DNK], k.ident[:, :])
                ins = pe.transpose(ps[0:SB * DNK, 3 + t // 4, (t % 4) * P:(t % 4 + 1) * P], tails[:, t, DNK:DNK * NSEQ],
                                   k.ident[:, :])
            ins.then_inc(tails_turned, 1)

        @block.scalar
        def _(act):
            st = Steps(act, astep)
            act.sem_inc(silu_done, 2)
            for u in range(2):
                act.activation(cin[:, u, 0:DNK], k.ones[:, 0:DNK], ACT.Copy, scale=0.0).then_inc(emptied[u], 1)
            act.wait_ge(st_copied, 1)

            with act.Fori(0, NBQ) as i:
                for u in range(2):
                    act.wait_ge(filled[u], i + 1)
                    act.wait_ge(conv_done[u], i + 1)
                    act.activation(chunks(cin[:, u, DNK:DNK + T]), ps[:, 3 * u:3 * u + 3, 0:CW], ACT.Copy)
                    act.activation(cs[:, u, :, 0:DNK], before[:, bass.ds(i * 2 + u, 1), :, :].rearrange("p a s r -> p (a s) r"), ACT.Copy)
                    act.activation(cs[:, u, :, DNK:], ps[:, 3 * u + 2, CW - NS:CW].rearrange("p (s l) -> p s l", l=SL),
                                   ACT.Copy).then_inc(emptied[u], 1)
                for u in range(2):
                    wait_before_addressed(act, conv_done[u], i + 2, act_passed)
                    act.activation(k.qkv[:, bass.ds(i * 2 + u, 1), :].rearrange("p a t -> p (a t)"), acc[:, u, :], ACT.Silu)\
                       .then_inc(silu_done, 1)
            for b in range(NBZ):
                for u in range(2):
                    act.wait_ge(filled[u], NBQ + b + 1)
                    act.activation(chunks(k.oT[:, 2 * b + u, :]), ps[:, 3 * u:3 * u + 3, 0:CW], ACT.Silu)\
                       .then_inc(emptied[u], 1)
            act.wait_ge(tails_turned, 1)
            act.activation(tails_rows[0:DNK, :].rearrange("p (b n) -> p b n", n=512), ps[0:DNK, 0:3, :], ACT.Copy)\
               .then_inc(tails_copied, 1)

        @block.vector
        def _(v):
            st = Steps(v, dstep)
            v.wait_ge(st_turned, 1)
            v.tensor_copy(before[:, :, :, :].rearrange("p t s r -> p (t s r)"), ps[:, 6, 0:DNC * SB * DNK]).then_inc(st_copied, 1)
            st(v.tensor_copy(taps[:, :], ps[:, 7, 0:4 * DNC]))
            for u in range(2):
                v.sem_inc(conv_done[u], 1)
            with v.Fori(0, NBQ) as i:
                st.loop(i, 2 * DNK)
                for u in range(2):
                    v.wait_ge(emptied[u], i + 2)
                    v.wait_ge(silu_done, i * 2 + (u + 1))
                    for tap in range(DNK + 1):
                        f = taps[:, bass.ds(i * 2 + (tap * DNC + u), 1)]
                        x, y = cin[:, u, tap:tap + SEQ], acc[:, u, 0:SEQ]
                        xs, ys = cs[:, u, :, tap:tap + SL], samples(acc[:, u, :])
                        if tap == 0:
                            v.tensor_copy(tails[:, bass.ds(i * 2 + u, 1), 0:DNK].rearrange("p a r -> p (a r)"), cin[:, u, SEQ:SEQ + DNK])
                            v.tensor_copy(tails[:, bass.ds(i * 2 + u, 1), DNK:].rearrange("p a (s r) -> p (a s) r", r=DNK), cs[:, u, :, SL:])
                            v.tensor_scalar(y, x, f, None, ALU.mult)
                            st(v.tensor_scalar(ys, xs, f, None, ALU.mult))
                            continue
                        v.scalar_tensor_tensor(y, x, f, y, ALU.mult, ALU.add)
                        ins = v.scalar_tensor_tensor(ys, xs, f, ys, ALU.mult, ALU.add)
                        if tap < DNK:
                            st(ins)
                    ins.then_inc(conv_done[u], 1)
                st.end(NBQ)
            v.wait_ge(tails_turned, 1)
            v.wait_ge(silu_done, 2 * NBQ + 2)
            v.tensor_copy(tails_rows[32:32 + SB * DNK, :].rearrange("p (b n) -> p b n", n=512), ps[0:SB * DNK, 3:6, :])\
             .then_inc(tails_copied, 1)


OUTS = [("y_prompt", (1, SEQ, D)), ("y_sample", (SB, SL, D)),
        ("prompt_state_delta", (1, 1, H, P, P)), ("prompt_state_delta_conv", (1, 1, DNK, DNC * P)),
        ("prompt_state_gla", (1, 1, H, GDK, P)), ("prompt_state_conv", (1, 1, CFK, CFC * P)),
        ("sample_state_delta", (1, SB, H, P, P)), ("sample_state_delta_conv", (1, SB, DNK, DNC * P)),
        ("sample_state_gla", (1, SB, H, GDK, P)), ("sample_state_conv", (1, SB, CFK, CFC * P))]


def delta_rows(k):
    nc, a, ps = k.nc, k.a, k.ps
    w = Area(k.work[:, k.work_after_qkv:])
    k.rows, k.rows8 = w.take(T), w.take(T)
    k.delta_area = w
    t = Area(k.oT[:, 4:12, :].rearrange("p a b -> p (a b)"))
    sq = t.take(2, T)
    wsm = t.take(KT, 80)
    raw, x, e, g = t.take(T), t.take(T), t.take(T), t.take(T)
    head = t.take(4)
    G0, G1 = RG, RG + H
    w_loaded, zeroed = k.sem("rows_w_loaded"), k.sem("rows_zeroed")
    squared, summed, small = k.sem("qk_squared"), k.sem("qk_summed"), k.sem("rows_small_done")
    dve, act_done, dstep, astep = k.sem("rows_by_vector"), k.sem("rows_by_scalar"), k.sem("rows_dve_step"), k.sem("rows_act_step")
    win = a["w_in"][0].rearrange("(k p) n -> p k n", p=P)

    with nc.Block() as block:
        @block.gpsimd
        def _(gp):
            gp.memset(wsm[:, :, :], 0.0)
            gp.memset(k.rows[:, :], 0.0).then_inc(zeroed, 1)

        @block.sync
        def _(sp):
            sp.dma_start(head[G0:G1, 0:1], a["dn_dt_bias"].rearrange("a h -> h a")).then_inc(w_loaded, 16)
            sp.dma_start(head[G0:G1, 1:2], a["dn_A_log"].rearrange("a h -> h a")).then_inc(w_loaded, 16)
            sp.wait_ge(zeroed, 1)
            for at, c0, n in ((RB, COL["ba"], H), (RG, COL["ba"] + H, H), (RT, COL["glr"], 16)):
                sp.dma_start(wsm[:, :, at:at + n], win[:, :, c0:c0 + n]).then_inc(w_loaded, 16)

        @block.tensor
        def _(pe):
            for j in range(2 * H):
                pe.wait_ge(squared, j + 1)
                for c in range(NCH):
                    ins = pe.matmul(ps[0:8, 3 + c, 0:CW], k.unit8[:, j, :], sq[:, j % 2, c * CW:(c + 1) * CW],
                                    start=(j == 0), stop=(j == 2 * H - 1))
                ins.then_inc(summed, 1)
            pe.wait_ge(w_loaded, 80)
            for c in range(NCH):
                for j in range(KT):
                    ins = pe.matmul(ps[0:80, c, 0:CW], wsm[:, j, :], k.hT[:, j, c * CW:(c + 1) * CW],
                                    start=(j == 0), stop=(j == KT - 1))
            ins.then_inc(small, 1)

        @block.scalar
        def _(act):
            st = Steps(act, astep)
            for j in range(2 * H):
                if j >= 2:
                    act.wait_ge(summed, j - 1)
                act.activation(sq[:, j % 2, :], k.qkv[:, j, :], ACT.Square).then_inc(squared, 1)
            act.wait_ge(dve, 1)
            act.activation(k.rows8[0:8, :], k.rows8[0:8, :], ACT.Sqrt).then_inc(act_done, 1)
            act.wait_ge(small, 1)
            st(act.activation(chunks(raw[0:80, :]), ps[0:80, 0:3, 0:CW], ACT.Copy))
            act.wait_ge(zeroed, 1)
            act.activation(k.rows8[64:80, :], raw[64:80, :], ACT.Copy)
            act.activation(k.rows[RB:RB + H, :], raw[0:H, :], ACT.Sigmoid)
            act.activation(head[G0:G1, 2:3], head[G0:G1, 1:2], ACT.Exp).then_inc(act_done, 1)
            act.wait_ge(dve, 2)
            st(act.activation(e[G0:G1, :], e[G0:G1, :], ACT.Exp, scale=-1.0))
            act.activation(e[G0:G1, :], e[G0:G1, :], ACT.Ln, bias=1.0).then_inc(act_done, 1)
            act.wait_ge(dve, 3)
            act.activation(k.rows[RE:RE + H, :], k.rows[G0:G1, :], ACT.Exp).then_inc(act_done, 1)

        @block.vector
        def _(v):
            st = Steps(v, dstep)
            v.wait_ge(summed, 2 * H)
            v.tensor_scalar(chunks(k.rows8[0:8, :]), ps[0:8, 3:6, 0:CW], EPS, None, ALU.add).then_inc(dve, 1)
            v.wait_ge(act_done, 1)
            st(v.reciprocal(k.rows8[0:8, :], k.rows8[0:8, :]))
            v.tensor_scalar(k.rows8[0:H, :], k.rows8[0:H, :], float(P) ** -0.5, None, ALU.mult)
            v.wait_ge(act_done, 2)
            st(v.tensor_scalar(x[G0:G1, :], raw[G0:G1, :], head[G0:G1, 0:1], None, ALU.add))
            v.scalar_tensor_tensor(e[G0:G1, :], x[G0:G1, :], -1.0, x[G0:G1, :], ALU.mult, ALU.max).then_inc(dve, 1)
            v.wait_ge(act_done, 3)
            st(v.scalar_tensor_tensor(g[G0:G1, :], x[G0:G1, :], 0.0, e[G0:G1, :], ALU.max, ALU.add))
            st(v.tensor_scalar(g[G0:G1, :], g[G0:G1, :], head[G0:G1, 2:3], -1.0, ALU.mult, ALU.mult))
            v.tensor_tensor_scan(k.rows[G0:G1, :], k.carry[G0:G1, :], g[G0:G1, :], 0.0, ALU.mult, ALU.add).then_inc(dve, 1)
            v.wait_ge(dve, 3)
            G = k.rows[G0:G1, :]
            for src, dst, n, l in ((G[:, 0:SEQ], k.rows[RT:RT + H, 0:SEQ], NC, C), (G[:, SEQ:T], k.rows[RT:RT + H, SEQ:T], SB, SL)):
                src = src.rearrange("p (c l) -> p c l", l=l)
                dst = dst.rearrange("p (c l) -> p c l", l=l)
                v.tensor_tensor(dst, bcast(src[:, :, l - 1:l], n, l), src, ALU.subtract)


def delta_rule(k):
    nc, a, ps = k.nc, k.a, k.ps
    w = k.delta_area
    t = Area(k.oT[:, 4:12, :].rearrange("p a b -> p (a b)"))

    def take(*s):
        n = 1
        for x in s:
            n *= x
        return (t if t.at + n <= t.size else w).take(*s)

    stage = [take(3, C) for _ in range(H)]
    rb = [take(2, C) for _ in range(H)]
    XY = [take(2, C) for _ in range(H)]
    lv = [take(2, C) for _ in range(H)]
    dec, AT, MT, P1, vb, kbe, kd, nwT, vn, qe, S = ([take(C) for _ in range(H)] for _ in range(11))
    rst, tcol, ecol, bge = take(C), take(C), take(C), take(H)
    v_filled, v_drained, s_filled, s_drained = (k.sem("dr_" + x) for x in
                                                ("v_filled", "v_drained", "s_filled", "s_drained"))
    rows_staged, cols_exp, bge_ready = k.sem("dr_rows_staged"), k.sem("dr_cols_exp"), k.sem("dr_bge_ready")
    decay_ready, level_ready = k.sem("dr_decay_ready"), k.sem("dr_level_ready")
    vexp_ready, dstep, astep = k.sem("dr_vexp_ready"), k.sem("dr_dve_step"), k.sem("dr_act_step")
    s0_loaded = [k.sem(f"dr_s0_loaded{h}") for h in range(H)]
    q_free, s_stored, s_final = k.sem("dr_q_free"), k.sem("dr_state_stored"), k.sem("dr_state_final")
    act_passed, pe_passed = k.sem("dr_act_passed"), k.sem("dr_pe_passed")
    LS = 2
    VE, SE = H * (4 + LEVELS) + 1, H * (4 + LEVELS)

    class At:
        def __init__(self, i):
            self.i = i

        def v(self, e, h):
            return self.i * VE + (1 + H * e + h + 1 if e >= 0 else 1)

        def s(self, e, h):
            return self.i * SE + (H * e + h + 1)
    bankv = lambda h: ps[:, 2 * h, :]
    banks = lambda h: ps[:, 2 * h + 1, :]

    def columns(i):
        return bass.ds(i * C, C) if not isinstance(i, int) or i < NC else slice(SEQ, T)

    with nc.Block() as block:
        def pe_front(pe, i, n, levels):
            at = At(i)
            cols = columns(i)

            def v_free(e, h, wait=None):
                (wait or (lambda s, x: pe.wait_ge(s, x)))(v_drained, at.v(e - 1, h) + H if e > 0 or h == 0 and e == 0 else at.i * VE + (1 + h))

            def s_free(e, h):
                pe.wait_ge(s_drained, at.s(e - 1, h) + H if e > 0 else at.i * SE + (1 + h))

            pe.wait_ge(rows_staged, i + 1)
            pe.wait_ge(v_drained, at.i * VE + 1)
            pe.transpose(ps[0:n, 0, 0:P], rst[:, 0:n], k.ident[:, :]).then_inc(v_filled, 1)
            for h in range(H):
                v_free(0, h, lambda s, x: wait_before_addressed(pe, s, x, pe_passed))
                for m, x in enumerate((h, H + h)):
                    pe.matmul(bankv(h)[:, m * n:(m + 1) * n], k.pick8[0:8, x, :], k.rows8[0:8, cols], start=True, stop=True)
                pe.matmul(bankv(h)[:, 2 * n:3 * n], k.pick[:, 3 * h, :], k.rows[:, cols], start=True, stop=True)\
                  .then_inc(v_filled, 1)
                s_free(0, h)
                for m in range(2):
                    ins = pe.matmul(banks(h)[:, m * n:(m + 1) * n], k.pick[:, 3 * h + 1 + m, :], k.rows[:, cols],
                                    start=True, stop=True)
                ins.then_inc(s_filled, 1)
            for h in range(H):
                v_free(1, h)
                kT = stage[h][:, 1, 0:n]
                pe.matmul(bankv(h)[0:n, 0:n], kT, stage[h][:, 0, 0:n], start=True, stop=True)
                pe.matmul(bankv(h)[0:n, n:2 * n], kT, kT, start=True, stop=True).then_inc(v_filled, 1)
                s_free(1, h)
                pe.transpose(banks(h)[0:n, 0:P], kT, k.ident[:, :])
                pe.transpose(banks(h)[0:n, P:2 * P], stage[h][:, 2, 0:n], k.ident[:, :]).then_inc(s_filled, 1)
            for l in range(levels):
                for h in range(H):
                    pe.wait_ge(level_ready, at.i * (H * LEVELS) + (H * l + h + 1))
                    v_free(2 + l, h)
                    s_free(2 + l, h)
                    pe.matmul(banks(h)[0:n, 0:n], lv[h][0:n, l % 2, 0:n], XY[h][0:n, 0, 0:n], start=True, stop=True)\
                      .then_inc(s_filled, 1)
                for h in range(H):
                    pe.wait_ge(s_drained, at.s(2 + l, h) + H)
                    if l < levels - 1:
                        pe.matmul(bankv(h)[0:n, 0:n], XY[h][0:n, 1, 0:n], P1[h][0:n, 0:n], start=True, stop=True)
                    pe.matmul(bankv(h)[0:n, n:2 * n], P1[h][0:n, 0:n], XY[h][0:n, 1, 0:n], start=True, stop=True)\
                      .then_inc(v_filled, 1)
            e = 2 + levels
            for h in range(H):
                v_free(e, h)
                s_free(e, h)
                pe.matmul(banks(h)[:, 0:n], kbe[h][0:n, :], XY[h][0:n, 1, 0:n], start=True, stop=True).then_inc(s_filled, 1)
            return at, e

        @block.tensor
        def _(pe):
            with pe.Fori(0, NC) as i:
                at, e = pe_front(pe, i, C, LEVELS)
                for h in range(H):
                    pe.wait_ge(s_drained, at.s(e, h) + H)
                    pe.matmul(bankv(h)[:, 0:C], XY[h][:, 1, :], vb[h][:, :], start=True, stop=False)
                    pe.matmul(bankv(h)[:, 0:C], nwT[h][:, :], S[h][:, :], start=False, stop=True).then_inc(v_filled, 1)
                for h in range(H):
                    pe.wait_ge(v_drained, at.v(e, h) + H)
                    pe.matmul(banks(h)[:, 0:C], S[h][:, :], qe[h][:, :], start=True, stop=False)
                    pe.matmul(banks(h)[:, 0:C], vn[h][:, :], AT[h][:, :], start=False, stop=True).then_inc(s_filled, 1)
                    pe.matmul(bankv(h)[:, 0:C], kd[h][:, :], vn[h][:, :], start=True, stop=True).then_inc(v_filled, 1)
            at, e = pe_front(pe, NC, NS, LS)
            for h in range(H):
                pe.wait_ge(s_drained, at.s(e, h) + H)
                pe.wait_ge(s0_loaded[h], 16)
                S0 = k.qkv[:, h, 0:SEQ].rearrange("p (b e) -> p b e", b=SB)
                pe.matmul(bankv(h)[:, 0:NS], vb[h][0:NS, :], XY[h][0:NS, 1, 0:NS], start=True, stop=False)
                for b in range(SB):
                    ins = pe.matmul(bankv(h)[:, b * SL:(b + 1) * SL], S0[:, b, :], nwT[h][:, b * SL:(b + 1) * SL],
                                    start=False, stop=(b == SB - 1))
                ins.then_inc(v_filled, 1)
            for h in range(H):
                pe.wait_ge(v_drained, at.v(e, h) + H)
                pe.transpose(banks(h)[0:NS, 0:P], nwT[h][:, 0:NS], k.ident[:, :]).then_inc(s_filled, 1)
            for h in range(H):
                pe.wait_ge(s_drained, at.s(e + 1, h) + H)
                S0 = k.qkv[:, h, 0:SEQ].rearrange("p (b e) -> p b e", b=SB)
                pe.matmul(bankv(h)[:, 0:NS], vn[h][0:NS, :], AT[h][0:NS, 0:NS], start=True, stop=False)
                for b in range(SB):
                    ins = pe.matmul(bankv(h)[:, b * SL:(b + 1) * SL], S0[:, b, :], qe[h][:, b * SL:(b + 1) * SL],
                                    start=False, stop=(b == SB - 1))
                ins.then_inc(v_filled, 1)
            for half in range(2):
                for h in range(H):
                    pe.wait_ge(vexp_ready, h + 1)
                    pe.wait_ge(v_drained, at.v(e + 1 + half, h) + H)
                    pe.matmul(bankv(h)[:, :], kd[h][0:NS, :], k.qkv[0:NS, H + h, half * 512:(half + 1) * 512],
                              start=True, stop=True).then_inc(v_filled, 1)

        def act_front(act, i, n, levels):
            at = At(i)
            cols = columns(i)
            act.wait_ge(v_drained, at.v(-1, 0) + H)
            act.activation(ecol[0:n, RG:RT + H], tcol[0:n, RG:RT + H], ACT.Exp).then_inc(cols_exp, 1)
            for h in range(H):
                src = k.qkv[:, 2 * H + h, cols]
                act.activation(stage[h][:, 2, 0:n], src, ACT.Copy)
                act.wait_ge(s_filled, at.s(0, h))
                act.activation(rb[h][:, :, 0:n], banks(h)[:, 0:2 * n].rearrange("p (a b) -> p a b", a=2), ACT.Copy)\
                   .then_inc(s_drained, 1)
            for h in range(H):
                act.wait_ge(v_drained, at.v(0, h) + H)
                act.activation(dec[h][0:n, 0:n], dec[h][0:n, 0:n], ACT.Exp).then_inc(decay_ready, 1)
            act.wait_ge(bge_ready, i + 1)
            for h in range(H):
                act.wait_ge(s_filled, at.s(1, h))
                act.activation(vb[h][0:n, :], banks(h)[0:n, P:2 * P], ACT.Copy, scale=tcol[0:n, RB + h:RB + h + 1])
                act.activation(kbe[h][0:n, :], banks(h)[0:n, 0:P], ACT.Copy, scale=bge[0:n, h:h + 1])
                act.activation(kd[h][0:n, :], banks(h)[0:n, 0:P], ACT.Copy, scale=ecol[0:n, RT + h:RT + h + 1])\
                   .then_inc(s_drained, 1)
            for l in range(levels):
                for h in range(H):
                    act.wait_ge(s_filled, at.s(2 + l, h))
                    act.activation(P1[h][0:n, 0:n], banks(h)[0:n, 0:n], ACT.Copy).then_inc(s_drained, 1)
            e = 2 + levels
            for h in range(H):
                act.wait_ge(s_filled, at.s(e, h))
                act.activation(nwT[h][:, 0:n], banks(h)[:, 0:n], ACT.Copy, scale=-1.0).then_inc(s_drained, 1)
            return at, e

        @block.scalar
        def _(act):
            act.sem_inc(s_drained, H)
            with act.Fori(0, NC) as i:
                at, e = act_front(act, i, C, LEVELS)
                for h in range(H):
                    wait_before_addressed(act, s_filled, at.s(e + 1, h), act_passed)
                    act.activation(k.qkv[:, 2 * H + h, columns(i)], banks(h)[:, 0:C], ACT.Copy).then_inc(s_drained, 1)
            at, e = act_front(act, NC, NS, LS)
            for h in range(H):
                act.wait_ge(s_filled, at.s(e + 1, h))
                act.activation(vn[h][0:NS, :], banks(h)[0:NS, 0:P], ACT.Copy).then_inc(s_drained, 1)

        def dve_front(v, st, i, n, levels):
            at = At(i)
            cols = columns(i)
            v.tensor_copy(rst[:, 0:n], k.rows[:, cols]).then_inc(rows_staged, 1)
            v.wait_ge(v_filled, at.v(-1, 0))
            v.tensor_copy(tcol[0:n, :], ps[0:n, 0, 0:P]).then_inc(v_drained, 1)
            v.wait_ge(cols_exp, i + 1)
            v.wait_ge(v_drained, at.v(-1, 0) + H)
            v.tensor_tensor(bge[0:n, :], tcol[0:n, RB:RB + H], ecol[0:n, RG:RG + H], ALU.mult).then_inc(bge_ready, 1)
            for h in range(H):
                v.wait_ge(v_filled, at.v(0, h))
                v.tensor_tensor(stage[h][:, 0:2, 0:n], k.qkv[:, h:h + 5:4, cols],
                                bankv(h)[:, 0:2 * n].rearrange("p (a b) -> p a b", a=2), ALU.mult)
                v.tensor_scalar(dec[h][0:n, 0:n], bankv(h)[0:n, 2 * n:3 * n], tcol[0:n, RG + h:RG + h + 1], 0.0,
                                ALU.subtract, ALU.min).then_inc(v_drained, 1)
            mask = k.causal[:, :] if n == C else k.causal_s[0:n, :]
            for h in range(H):
                v.wait_ge(decay_ready, at.i * H + (h + 1))
                st.done(v.tensor_tensor(dec[h][0:n, 0:n], dec[h][0:n, 0:n], mask, ALU.mult))
            st.wait()
            for h in range(H):
                v.wait_ge(v_filled, at.v(1, h))
                v.tensor_tensor(AT[h][0:n, 0:n], bankv(h)[0:n, 0:n], dec[h][0:n, 0:n], ALU.mult)
                v.tensor_tensor(MT[h][0:n, 0:n], bankv(h)[0:n, n:2 * n], dec[h][0:n, 0:n], ALU.mult).then_inc(v_drained, 1)
            v.wait_ge(v_drained, at.v(1, H - 1) + H)
            v.wait_ge(s_drained, at.s(0, H - 1) + H)
            for h in range(H):
                v.tensor_tensor(qe[h][:, 0:n], stage[h][:, 0, 0:n], rb[h][:, 1, 0:n], ALU.mult)
                v.tensor_copy(XY[h][0:n, 0, 0:n], k.ident[0:n, 0:n])
                v.tensor_copy(XY[h][0:n, 1, 0:n], k.ident[0:n, 0:n])
                st.done(v.tensor_tensor(MT[h][0:n, 0:n], MT[h][0:n, 0:n], rb[h][0:n, 0, 0:n], ALU.mult))
            st.wait()
            for l in range(levels + 1):
                if l < levels:
                    for h in range(H):
                        v.tensor_tensor(lv[h][0:n, l % 2, 0:n], MT[h][0:n, 0:n], k.pair[0:n, l, 0:n], ALU.mult)\
                         .then_inc(level_ready, 1)
                if l:
                    for h in range(H):
                        v.wait_ge(v_filled, at.v(1 + l, h))
                        v.wait_ge(v_drained, at.v(l, h) + H)
                        lo = 0 if l < levels else 1
                        v.tensor_tensor(XY[h][0:n, lo:2, 0:n], XY[h][0:n, lo:2, 0:n],
                                        bankv(h)[0:n, lo * n:2 * n].rearrange("p (a b) -> p a b", b=n), ALU.subtract)\
                         .then_inc(v_drained, 1)
            return at, 2 + levels

        @block.vector
        def _(v):
            st = Steps(v, dstep)
            for h in range(H):
                v.memset(S[h][:, :], 0.0).then_inc(v_drained, 1)
            with v.Fori(0, NC) as i:
                st.loop(i, 2 * H)
                at, e = dve_front(v, st, i, C, LEVELS)
                st.end(NC)
                for h in range(H):
                    v.wait_ge(v_filled, at.v(e, h))
                    v.tensor_copy(vn[h][:, :], bankv(h)[:, 0:C]).then_inc(v_drained, 1)
                for h in range(H):
                    v.wait_ge(v_filled, at.v(e + 1, h))
                    v.scalar_tensor_tensor(S[h][:, :], S[h][:, :], rb[h][:, 1, C - 1:C], bankv(h)[:, 0:C],
                                           ALU.mult, ALU.add).then_inc(v_drained, 1)
            at, e = dve_front(v, st, NC, NS, LS)
            for h in range(H):
                v.wait_ge(v_filled, at.v(e, h))
                v.tensor_copy(nwT[h][:, 0:NS], bankv(h)[:, 0:NS]).then_inc(v_drained, 1)
            for h in range(H):
                v.wait_ge(s_drained, at.s(e + 1, h) + H)
                v.tensor_tensor(k.qkv[0:NS, H + h, 0:SEQ].rearrange("p (b e) -> p b e", b=SB),
                                bcast(vn[h][0:NS, :].unsqueeze(1), SB, P), bcast(k.inseq[0:NS, :].unsqueeze(2), SB, P),
                                ALU.mult).then_inc(vexp_ready, 1)
            for h in range(H):
                v.wait_ge(v_filled, at.v(e + 1, h))
                v.tensor_copy(k.qkv[:, 2 * H + h, SEQ:T], bankv(h)[:, 0:NS]).then_inc(v_drained, 1)
            for half in range(2):
                for h in range(H):
                    v.wait_ge(v_filled, at.v(e + 2 + half, h))
                    for b in range(4):
                        bb = 4 * half + b
                        S0 = k.qkv[:, h, bb * P:(bb + 1) * P]
                        ins = v.scalar_tensor_tensor(S0, S0, rb[h][:, 1, bb * SL + SL - 1:bb * SL + SL],
                                                     bankv(h)[:, b * P:(b + 1) * P], ALU.mult, ALU.add)
                    ins.then_inc(v_drained, 1)

        @block.sync
        def _(sp):
            for h in range(H):
                sp.wait_ge(v_drained, (NC - 1) * VE + (1 + H * 0 + h + 1) + H)
                sp.dma_start(k.qkv[:, h, 0:SEQ].rearrange("p (b e) -> p b e", b=SB),
                             a["state_delta"][0, :, h].rearrange("b d e -> d b e")).then_inc(s0_loaded[h], 16)
            for h in range(H):
                sp.wait_ge(v_drained, NC * VE + H)
                sp.dma_start(a["prompt_state_delta"][0, 0, h], S[h][:, :]).then_inc(s_stored, 16)
            for h in range(H):
                sp.wait_ge(v_drained, At(NC).v(7, h) + H)
                sp.dma_start(a["sample_state_delta"][0, :, h].rearrange("b d e -> d b e"),
                             k.qkv[:, h, 0:SEQ].rearrange("p (b e) -> p b e", b=SB)).then_inc(s_stored, 16)
            sp.wait_ge(s_stored, 16 * 2 * H)


def gated_norm(k, tag, src, dst, weight, area):
    nc, ps = k.nc, k.ps
    sq, fac = area.take(2, T), area.take(T)
    squared, summed, spread = k.sem(tag + "_squared"), k.sem(tag + "_summed"), k.sem(tag + "_spread")
    by_act, by_dve, dstep = k.sem(tag + "_by_act"), k.sem(tag + "_by_dve"), k.sem(tag + "_dve_step")
    drained = k.sem(tag + "_drained")

    with nc.Block() as block:
        @block.scalar
        def _(act):
            for h in range(H):
                if h >= 2:
                    act.wait_ge(summed, h - 1)
                act.activation(sq[:, h % 2, :], src[:, h, :], ACT.Square).then_inc(squared, 1)
            act.wait_ge(by_dve, 1)
            act.activation(fac[0:8, :], fac[0:8, :], ACT.Sqrt).then_inc(by_act, 1)

        @block.tensor
        def _(pe):
            for h in range(H):
                pe.wait_ge(squared, h + 1)
                for c in range(NCH):
                    ins = pe.matmul(ps[0:8, c, 0:CW], k.unit8[:, h, :], sq[:, h % 2, c * CW:(c + 1) * CW],
                                    start=(h == 0), stop=(h == H - 1))
                ins.then_inc(summed, 1)
            pe.wait_ge(by_dve, 2)
            for h in range(H):
                if h >= 2:
                    pe.wait_ge(drained, h - 1)
                for c in range(NCH):
                    ins = pe.matmul(ps[:, 3 * (h % 2) + c, 0:CW], k.pick8[0:8, h, :], fac[0:8, c * CW:(c + 1) * CW],
                                    start=True, stop=True)
                ins.then_inc(spread, 1)

        @block.vector
        def _(v):
            st = Steps(v, dstep)
            v.wait_ge(summed, H)
            v.tensor_scalar(chunks(fac[0:8, :]), ps[0:8, 0:3, 0:CW], 1.0 / P, EPS, ALU.mult, ALU.add).then_inc(by_dve, 1)
            v.wait_ge(by_act, 1)
            v.reciprocal(fac[0:8, :], fac[0:8, :]).then_inc(by_dve, 1)
            for h in range(H):
                v.wait_ge(spread, h + 1)
                v.scalar_tensor_tensor(chunks(src[:, h, :]), chunks(src[:, h, :]), weight,
                                       ps[:, 3 * (h % 2):3 * (h % 2) + 3, 0:CW], ALU.mult, ALU.mult).then_inc(drained, 1)
            v.wait_ge(drained, H)
            for h in range(H):
                v.tensor_tensor(dst[:, h, :], dst[:, h, :], src[:, h, :], ALU.mult)


def gla_project(k):
    nc, a, ps = k.nc, k.a, k.ps
    w = Area(k.work[:, :])
    low = k.rows8
    k.gla = w.take(8, T)
    w.take(k.work_after_qkv + 2 * T - w.at)
    k.bcum = k.oT[:, 8:10, :]
    lg, ab = w.take(T), w.take(T)
    ring = Area(k.work[:, 8 * T:k.work_after_qkv]).take(2, KT, 256)
    gw = w.take(256)
    win = a["w_in"][0].rearrange("(k p) n -> p k n", p=P)
    w_loaded = [k.sem(f"gla_w_loaded{s}") for s in range(2)]
    filled, drained = k.sem("gla_filled"), k.sem("gla_drained")
    gw_loaded, lg_done, by_dve, dstep, astep = (k.sem("gla_" + x) for x in ("gw_loaded", "lg_done", "by_dve", "dstep", "astep"))
    NB = 6

    with nc.Block() as block:
        @block.sync
        def _(sp):
            sp.dma_start(gw[64:80, :], a["gla_gate_w"][0]).then_inc(gw_loaded, 16)
            for b in range(NB):
                if b >= 2:
                    sp.wait_ge(filled, 2 * (b - 1))
                c0 = COL["gqk"] + b * 256
                sp.dma_start(ring[:, b % 2], win[:, :, c0:c0 + 256]).then_inc(w_loaded[b % 2], 16)

        @block.tensor
        def _(pe):
            for b in range(NB):
                pe.wait_ge(w_loaded[b % 2], 16 * (b // 2 + 1))
                for u in range(2):
                    f = 2 * b + u
                    if f >= 2:
                        pe.wait_ge(drained, f - 1)
                    for c in range(NCH):
                        for j in range(KT):
                            ins = pe.matmul(ps[:, 3 * u + c, 0:CW], ring[:, b % 2, j, u * P:(u + 1) * P],
                                            k.hT[:, j, c * CW:(c + 1) * CW], start=(j == 0), stop=(j == KT - 1))
                    ins.then_inc(filled, 1)
            pe.wait_ge(gw_loaded, 16)
            for u in range(2):
                f = 2 * NB + u
                pe.wait_ge(drained, f - 1)
                for c in range(NCH):
                    ins = pe.matmul(ps[:, 3 * u + c, 0:CW], gw[64:80, u * P:(u + 1) * P], low[64:80, c * CW:(c + 1) * CW],
                                    start=True, stop=True)
                ins.then_inc(filled, 1)

        @block.scalar
        def _(act):
            st = Steps(act, astep)
            for f in range(2 * NB):
                act.wait_ge(filled, f + 1)
                src = ps[:, 3 * (f % 2):3 * (f % 2) + 3, 0:CW]
                if f < 8:
                    act.activation(chunks(k.gla[:, f, :]), src, ACT.Copy, scale=GDK ** -0.5 if f < 2 else 1.0).then_inc(drained, 1)
                else:
                    act.activation(chunks(k.oT[:, f - 4, :]), src, ACT.Silu).then_inc(drained, 1)
            for u in range(2):
                act.wait_ge(filled, 2 * NB + u + 1)
                if u:
                    act.wait_ge(by_dve, 2)
                act.activation(chunks(lg), ps[:, 3 * u:3 * u + 3, 0:CW], ACT.Identity, bias=k.column("gla_gate_b", u))\
                   .then_inc(drained, 1)
                act.wait_ge(by_dve, 2 * u + 1)
                st(act.activation(ab[:, :], ab[:, :], ACT.Exp, scale=-1.0))
                act.activation(ab[:, :], ab[:, :], ACT.Ln, bias=1.0).then_inc(lg_done, 1)

        @block.vector
        def _(v):
            st = Steps(v, dstep)
            for u in range(2):
                v.wait_ge(drained, 2 * NB + u + 1)
                if u:
                    v.wait_ge(by_dve, 2)
                v.scalar_tensor_tensor(ab[:, :], lg[:, :], -1.0, lg[:, :], ALU.mult, ALU.max).then_inc(by_dve, 1)
                v.wait_ge(lg_done, u + 1)
                st(v.scalar_tensor_tensor(ab[:, :], lg[:, :], 0.0, ab[:, :], ALU.min, ALU.subtract))
                st(v.tensor_scalar(ab[:, :], ab[:, :], 1.0 / 16.0, None, ALU.mult))
                v.tensor_tensor_scan(k.bcum[:, u, :], k.carry[:, :], ab[:, :], 0.0, ALU.mult, ALU.add).then_inc(by_dve, 1)


def gla_rule(k):
    nc, a, ps = k.nc, k.a, k.ps
    w = Area(k.work[:, 8 * T:])
    t = Area(k.oT[:, 10:12, :].rearrange("p a b -> p (a b)"))
    E = [w.take(LEVELS + 2, C) for _ in range(2)]
    Kf = [w.take(LEVELS + 1, C) for _ in range(2)]
    Qf = [w.take(LEVELS + 1, C) for _ in range(2)]
    raw = [w.take(2, C) for _ in range(2)]
    vst = [w.take(2, C) for _ in range(2)]
    kdv = [w.take(3, P) for _ in range(2)]
    S = [w.take(2, P) for _ in range(2)]
    head_q, head_f = w.take(H, NS), w.take(H, NS)
    prod = [t.take(LEVELS + 1, C) for _ in range(2)]
    AT = [w.take(C) for _ in range(H)]
    L_filled, L_drained, T_filled, T_drained, O_filled, O_drained, S_filled, S_drained = (
        k.sem("gr_" + x) for x in ("levels_filled", "levels_drained", "turned_filled", "turned_drained",
                                   "out_filled", "out_drained", "state_filled", "state_drained"))
    diff_ready, exp_ready, kq_ready, staged, at_ready, vexp_ready = (
        k.sem("gr_" + x) for x in ("diff_ready", "exp_ready", "kq_ready", "staged", "at_ready", "vexp_ready"))
    dstep, astep, stored = k.sem("gr_dve_step"), k.sem("gr_act_step"), k.sem("gr_state_stored")
    s0_loaded = [k.sem(f"gr_s0_loaded{h}") for h in range(H)]
    shifted, act_passed = k.sem("gr_head_rows_shifted"), k.sem("gr_act_passed")
    S0 = [k.gla[0:GDK, h, 0:SEQ].rearrange("p (b e) -> p b e", b=SB) for h in range(H)]
    vexp = [x.rearrange("p a b -> p (a b)") for x in (Kf[0], Qf[0], Kf[1], Qf[1])]

    def columns(i):
        return bass.ds(i * C, C) if not isinstance(i, int) or i < NC else slice(SEQ, T)

    def level_bank(h, n):
        return ps[0:n, 2 * (h % 2):2 * (h % 2) + 2, :].rearrange("p a b -> p (a b)")

    with nc.Block() as block:
        def pe_front(pe, i, n, levels):
            for p in range(2):
                pe.wait_ge(kq_ready, 2 * i + p + 1)
                pe.wait_ge(staged, 2 * i + p + 1)
                for hh in range(2):
                    h, r = 2 * p + hh, slice(64 * hh, 64 * hh + 64)
                    pe.wait_ge(L_drained, 4 * i + h + 1)
                    out = level_bank(h, n)
                    for l in range(levels):
                        pe.matmul(out[:, l * n:(l + 1) * n], Kf[p][r, l, 0:n], Qf[p][r, l, 0:n], start=True, stop=True)
                    pe.matmul(out[:, levels * n:(levels + 1) * n], raw[p][r, 1, 0:n], raw[p][r, 0, 0:n],
                              start=True, stop=True).then_inc(L_filled, 1)
                pe.wait_ge(T_drained, 2 * i + p + 1)
                pe.transpose(ps[0:n, 4 + p, 0:P], Kf[p][:, LEVELS, 0:n], k.ident[:, :])
                for hh in range(2):
                    ins = pe.transpose(ps[0:n, 4 + p, (1 + hh) * P:(2 + hh) * P], vst[p][:, hh, 0:n], k.ident[:, :])
                ins.then_inc(T_filled, 1)
            pe.wait_ge(O_drained, i + 1)
            for p in range(2):
                pe.wait_ge(T_drained, 2 * i + p + 3)

        @block.tensor
        def _(pe):
            with pe.Fori(0, NC) as i:
                pe_front(pe, i, C, LEVELS)
                pe.wait_ge(S_drained, i + 1)
                for h in range(H):
                    p, hh = divmod(h, 2)
                    pe.wait_ge(at_ready, 4 * i + h + 1)
                    pe.matmul(ps[:, 7, h * C:(h + 1) * C], S[p][:, hh, :], Qf[p][:, LEVELS, :], start=True, stop=False)
                    ins = pe.matmul(ps[:, 7, h * C:(h + 1) * C], kdv[p][:, 1 + hh, :], AT[h][:, :], start=False, stop=True)
                ins.then_inc(O_filled, 1)
                for p in range(2):
                    ins = pe.matmul(ps[:, 6, p * 256:(p + 1) * 256], kdv[p][:, 0, :],
                                    kdv[p][:, 1:3, :].rearrange("p a b -> p (a b)"), start=True, stop=True)
                ins.then_inc(S_filled, 1)
            pe_front(pe, NC, NS, 2)
            pe.wait_ge(shifted, 1)
            for h in range(H):
                p, hh = divmod(h, 2)
                pe.wait_ge(s0_loaded[h], 16)
                pe.wait_ge(at_ready, 4 * NC + h + 1)
                out = ps[:, 7, h * NS:(h + 1) * NS]
                pe.matmul(out, kdv[p][0:NS, 1 + hh, :], AT[h][0:NS, 0:NS], start=True, stop=False)
                for b in range(SB):
                    ins = pe.matmul(out[:, b * SL:(b + 1) * SL], S0[h][:, b, :], head_q[0:GDK, h, b * SL:(b + 1) * SL],
                                    start=False, stop=(b == SB - 1))
            ins.then_inc(O_filled, 1)
            for n in range(2 * H):
                h, half = divmod(n, 2)
                p, hh = divmod(h, 2)
                pe.wait_ge(S_drained, NC + n + 1)
                pe.wait_ge(vexp_ready, h + 1)
                pe.matmul(ps[0:GDK, 6, :], kdv[p][0:NS, 0, GDK * hh:GDK * hh + GDK],
                          vexp[h][0:NS, half * 512:(half + 1) * 512], start=True, stop=True).then_inc(S_filled, 1)

        def act_front(act, i, n):
            for p in range(2):
                for m in range(2):
                    act.activation(raw[p][:, m, 0:n], k.gla[:, 2 * m + p, columns(i)], ACT.Copy)
                    ins = act.activation(vst[p][:, m, 0:n], k.gla[:, 4 + 2 * p + m, columns(i)], ACT.Copy)
                ins.then_inc(staged, 1)
            for p in range(2):
                act.wait_ge(diff_ready, 2 * i + p + 1)
                act.activation(E[p][:, :, 0:n], E[p][:, :, 0:n], ACT.Exp, scale=-1.0).then_inc(exp_ready, 1)
            for p in range(2):
                act.wait_ge(T_filled, 2 * i + p + 1)
                act.activation(kdv[p][0:n, :, :].rearrange("p a b -> p (a b)"), ps[0:n, 4 + p, 0:3 * P], ACT.Copy)\
                   .then_inc(T_drained, 1)

        @block.scalar
        def _(act):
            act.sem_inc(T_drained, 2)
            act.sem_inc(O_drained, 1)
            with act.Fori(0, NC) as i:
                act_front(act, i, C)
                wait_before_addressed(act, O_filled, i + 1, act_passed)
                act.activation(k.gla[:, 4:8, columns(i)], ps[:, 7, :].rearrange("p (h n) -> p h n", h=H), ACT.Copy)\
                   .then_inc(O_drained, 1)
            act_front(act, NC, NS)
            for p in range(2):
                act.wait_ge(kq_ready, 2 * NC + p + 1)
                for hh in range(2):
                    act.activation(head_q[0:GDK, 2 * p + hh, :], Qf[p][64 * hh:64 * hh + 64, LEVELS, 0:NS], ACT.Copy)
                    ins = act.activation(head_f[0:GDK, 2 * p + hh, :], E[p][64 * hh:64 * hh + 64, LEVELS + 1, 0:NS], ACT.Copy)
            ins.then_inc(shifted, 1)
            act.wait_ge(O_filled, NC + 1)
            act.activation(k.gla[:, 4:8, SEQ:T], ps[:, 7, 0:H * NS].rearrange("p (h n) -> p h n", h=H), ACT.Copy)\
               .then_inc(O_drained, 1)

        def dve_front(v, st, i, n, levels, length):
            for p in range(2):
                b = k.bcum[:, p, columns(i)]
                for l in range(levels):
                    s = 1 << l
                    bb = b.rearrange("p (m r) -> p m r", r=2 * s)
                    v.tensor_tensor(E[p][:, l, 0:n].rearrange("p (m r) -> p m r", r=2 * s), bb,
                                    bcast(bb[:, :, s - 1:s], n // (2 * s), 2 * s), ALU.subtract)
                for l in range(levels, LEVELS):
                    if n < C:
                        v.memset(E[p][:, l, 0:n], 0.0)
                bb = b.rearrange("p (m r) -> p m r", r=length)
                v.tensor_copy(E[p][:, LEVELS + 1, 0:n], b)
                st.done(v.tensor_tensor(E[p][:, LEVELS, 0:n].rearrange("p (m r) -> p m r", r=length),
                                        bcast(bb[:, :, length - 1:length], n // length, length), bb, ALU.subtract))
                st.wait()
                v.scalar_tensor_tensor(E[p][:, :, 0:n], E[p][:, :, 0:n], -1.0, E[p][:, :, 0:n], ALU.mult, ALU.max)\
                 .then_inc(diff_ready, 1)
            for p in range(2):
                v.wait_ge(exp_ready, 2 * i + p + 1)
                q, kk = k.gla[:, p, columns(i)], k.gla[:, 2 + p, columns(i)]
                v.tensor_tensor(Kf[p][:, :, 0:n], bcast(kk.unsqueeze(1), LEVELS + 1, n), E[p][:, 0:LEVELS + 1, 0:n], ALU.mult)
                v.tensor_tensor(Qf[p][:, LEVELS, 0:n], q, E[p][:, LEVELS + 1, 0:n], ALU.mult)
                v.tensor_tensor(Qf[p][:, 0:LEVELS, 0:n], bcast(q.unsqueeze(1), LEVELS, n), E[p][:, 0:LEVELS, 0:n], ALU.mult)\
                 .then_inc(kq_ready, 1)
            for h in range(H):
                v.wait_ge(L_filled, 4 * i + h + 1)
                out = level_bank(h, n)
                pr = prod[h % 2].rearrange("p a b -> p (a b)")[:, 0:(levels + 1) * n].rearrange("p (l n) -> p l n", n=n)
                o3 = out[:, 0:(levels + 1) * n].rearrange("p (l n) -> p l n", n=n)
                if levels == LEVELS:
                    v.tensor_tensor(pr[0:n], o3, k.pair[0:n, :, 0:n], ALU.mult).then_inc(L_drained, 1)
                else:
                    v.tensor_tensor(pr[0:n, 0:levels], o3[:, 0:levels], k.pair[0:n, 0:levels, 0:n], ALU.mult)
                    v.tensor_tensor(pr[0:n, levels], o3[:, levels], k.pair[0:n, LEVELS, 0:n], ALU.mult).then_inc(L_drained, 1)
                v.wait_ge(L_drained, 4 * i + h + 3)
                v.tensor_reduce(AT[h][0:n, 0:n], pr[0:n].rearrange("p l n -> p n l"), AX.X, ALU.add).then_inc(at_ready, 1)

        @block.vector
        def _(v):
            st = Steps(v, dstep)
            v.sem_inc(L_drained, 2)
            v.memset(S[0][:, :, :], 0.0)
            v.memset(S[1][:, :, :], 0.0).then_inc(S_drained, 1)
            with v.Fori(0, NC) as i:
                st.loop(i, 2)
                dve_front(v, st, i, C, LEVELS, C)
                st.end(NC)
                v.wait_ge(S_filled, i + 1)
                for p in range(2):
                    for hh in range(2):
                        r = slice(64 * hh, 64 * hh + 64)
                        ins = v.scalar_tensor_tensor(S[p][r, hh, :], S[p][r, hh, :], E[p][r, LEVELS + 1, C - 1:C],
                                                     ps[r, 6, p * 256 + hh * P:p * 256 + (hh + 1) * P], ALU.mult, ALU.add)
                ins.then_inc(S_drained, 1)
                v.wait_ge(S_drained, i + 2)
            dve_front(v, st, NC, NS, 2, SL)
            for h in range(H):
                p, hh = divmod(h, 2)
                if h == 0:
                    v.wait_ge(shifted, 1)
                v.wait_ge(T_drained, 2 * NC + p + 3)
                v.tensor_tensor(vexp[h][0:NS, :].rearrange("p (b e) -> p b e", b=SB),
                                bcast(kdv[p][0:NS, 1 + hh, :].unsqueeze(1), SB, P),
                                bcast(k.inseq[0:NS, :].unsqueeze(2), SB, P), ALU.mult).then_inc(vexp_ready, 1)
            for n in range(2 * H):
                h, half = divmod(n, 2)
                v.wait_ge(S_filled, NC + n + 1)
                for b in range(4):
                    bb = 4 * half + b
                    ins = v.scalar_tensor_tensor(S0[h][:, bb, :], S0[h][:, bb, :],
                                                 head_f[0:GDK, h, bb * SL + SL - 1:bb * SL + SL],
                                                 ps[0:GDK, 6, b * P:(b + 1) * P], ALU.mult, ALU.add)
                ins.then_inc(S_drained, 1)

        @block.sync
        def _(sp):
            sp.wait_ge(L_filled, 4 * NC)
            for h in range(H):
                sp.dma_start(S0[h], a["state_gla"][0, :, h].rearrange("b d e -> d b e")).then_inc(s0_loaded[h], 16)
            sp.wait_ge(S_drained, NC + 1)
            for h in range(H):
                r = slice(64 * (h % 2), 64 * (h % 2) + 64)
                sp.dma_start(a["prompt_state_gla"][0, 0, h], S[h // 2][r, h % 2, :]).then_inc(stored, 16)
            sp.wait_ge(S_drained, NC + 1 + 2 * H)
            for h in range(H):
                sp.dma_start(a["sample_state_gla"][0, :, h].rearrange("b d e -> d b e"), S0[h]).then_inc(stored, 16)
            sp.wait_ge(stored, 16 * 2 * H)


def conformer(k):
    nc, a, ps = k.nc, k.a, k.ps
    w = Area(k.work[:, :])
    ring = w.take(2, KT, 2, P)
    sg, cin, cs = w.take(T), w.take(2, CFK + T), w.take(2, SB, CFK + SL)
    before, taps = w.take(CFC, SB * CFK), w.take(CFK + 1, CFC)
    prev_in, taps_in = w.take(2, CFC * P), w.take(P)
    last = w.take(2, CFC * P)
    tails = w.take(CFC, CFK + NS)
    sq, mean, rstd = w.take(2, T), w.take(T), w.take(T)
    HR = SB // 2 * CFK
    y = k.oT[:, 8:12, :]
    win = a["w_in"][0].rearrange("(k p) n -> p k n", p=P)
    w_loaded = [k.sem(f"cf_w_loaded{s}") for s in range(2)]
    st_loaded, st_turned, st_copied = k.sem("cf_state_loaded"), k.sem("cf_state_turned"), k.sem("cf_state_copied")
    a_filled, g_filled, glu_done, sig_done, conv_done = (k.sem("cf_" + x) for x in
                                                         ("a_filled", "g_filled", "glu_done", "sig_done", "conv_done"))
    tails_turned, tails_copied, summed, squared = (k.sem("cf_" + x) for x in ("tails_turned", "tails_copied", "summed", "squared"))
    by_dve, by_act, dstep, stored = (k.sem("cf_" + x) for x in ("by_dve", "by_act", "dve_step", "stored"))

    with nc.Block() as block:
        @block.sync
        def _(sp):
            def load(j):
                for m in range(2):
                    c0 = COL["conf"] + m * CFC * P + j * P
                    sp.dma_start(ring[:, j % 2, :, m, :], win[:, :, c0:c0 + P]).then_inc(w_loaded[j % 2], 16)
            load(0)
            load(1)
            rows = a["state_conv"][0].rearrange("b r c -> (b r) c")
            for m in range(2):
                sp.dma_start(prev_in[0:HR, m, :], rows[m * HR:(m + 1) * HR]).then_inc(st_loaded, 16)
            sp.dma_start(taps_in[0:(CFK + 1) * CFC, :], a["conf_dw_w"][0].rearrange("w (t p) -> (w t) p", p=P)).then_inc(st_loaded, 16)
            for j in range(2, CFC):
                sp.wait_ge(g_filled, j - 1)
                load(j)
            sp.dma_start(a["sample_state_conv"][0, :, 0:CFK - SL, :], a["state_conv"][0, :, SL:CFK, :]).then_inc(stored, 16)
            sp.wait_ge(tails_copied, 2)
            sp.dma_start(a["prompt_state_conv"][0, 0], last[0:CFK, 0, :]).then_inc(stored, 16)
            for b in range(SB):
                sp.dma_start(a["sample_state_conv"][0, b, CFK - SL:CFK, :], last[b * SL:(b + 1) * SL, 1, :]).then_inc(stored, 16)
            sp.wait_ge(stored, 16 * (2 + SB))

        @block.tensor
        def _(pe):
            pe.wait_ge(st_loaded, 48)
            for m in range(2):
                for t in range(CFC):
                    pe.transpose(ps[:, 6 + m, t * HR:(t + 1) * HR], prev_in[0:HR, m, t * P:(t + 1) * P], k.ident[0:HR, 0:HR])
            n = (CFK + 1) * CFC
            pe.transpose(ps[:, 0, 0:n], taps_in[0:n, :], k.ident[0:n, 0:n]).then_inc(st_turned, 1)
            pe.wait_ge(st_copied, 1)
            for j in range(CFC):
                pe.wait_ge(w_loaded[j % 2], 32 * (j // 2 + 1))
                for m, (filled, free) in enumerate(((a_filled, glu_done), (g_filled, sig_done))):
                    if j:
                        pe.wait_ge(free, j)
                    for c in range(NCH):
                        for q in range(KT):
                            ins = pe.matmul(ps[:, 3 * m + c, 0:CW], ring[:, j % 2, q, m, :], k.hT[:, q, c * CW:(c + 1) * CW],
                                            start=(q == 0), stop=(q == KT - 1))
                    ins.then_inc(filled, 1)
            pe.wait_ge(glu_done, CFC)
            pe.wait_ge(sig_done, CFC)
            for t in range(CFC):
                pe.wait_ge(conv_done, t + 1)
                for c in range(NCH):
                    ins = pe.matmul(ps[:, c, 0:CW], k.ones[:, :], y[:, t, c * CW:(c + 1) * CW], start=(t == 0), stop=(t == CFC - 1))
            ins.then_inc(summed, 1)
            for t in range(CFC):
                pe.transpose(ps[0:CFK, 6, t * P:(t + 1) * P], tails[:, t, 0:CFK], k.ident[:, :])
                ins = pe.transpose(ps[0:NS, 7, t * P:(t + 1) * P], tails[:, t, CFK:], k.ident[:, :])
            ins.then_inc(tails_turned, 1)
            for t in range(CFC):
                pe.wait_ge(squared, t + 1)
                for c in range(NCH):
                    ins = pe.matmul(ps[:, 3 + c, 0:CW], k.ones[:, :], sq[:, t % 2, c * CW:(c + 1) * CW], start=(t == 0), stop=(t == CFC - 1))
                ins.then_inc(summed, 1)

        @block.scalar
        def _(act):
            for j in range(CFC):
                act.wait_ge(g_filled, j + 1)
                if j:
                    act.wait_ge(glu_done, j)
                act.activation(chunks(sg), ps[:, 3:6, 0:CW], ACT.Sigmoid).then_inc(sig_done, 1)
            act.wait_ge(tails_turned, 1)
            act.activation(last[0:CFK, 0, :], ps[0:CFK, 6, :], ACT.Copy).then_inc(tails_copied, 1)
            act.activation(last[0:NS, 1, :], ps[0:NS, 7, :], ACT.Copy).then_inc(tails_copied, 1)
            for t in range(CFC):
                act.wait_ge(by_dve, 1 + t + 1)
                if t >= 2:
                    act.wait_ge(summed, 1 + t - 1)
                act.activation(sq[:, t % 2, :], y[:, t, :], ACT.Square).then_inc(squared, 1)
            act.wait_ge(by_dve, 2 + CFC)
            act.activation(rstd[:, :], rstd[:, :], ACT.Sqrt).then_inc(by_act, 1)
            for t in range(CFC):
                act.wait_ge(by_dve, 3 + CFC + t)
                act.activation(y[:, t, :], y[:, t, :], ACT.Silu, bias=k.column("conf_ln_b", t), scale=k.column("conf_ln_w", t))

        @block.vector
        def _(v):
            st = Steps(v, dstep)
            v.wait_ge(st_turned, 1)
            for m in range(2):
                v.tensor_copy(before[:, :, m * HR:(m + 1) * HR], ps[:, 6 + m, 0:CFC * HR].rearrange("p (t r) -> p t r", t=CFC))
            v.tensor_copy(taps[:, :, :].rearrange("p a b -> p (a b)"), ps[:, 0, 0:(CFK + 1) * CFC]).then_inc(st_copied, 1)
            st(v.memset(cin[:, :, 0:CFK], 0.0))
            v.wait_ge(st_copied, 1)
            for j in range(CFC):
                u = j % 2
                v.wait_ge(a_filled, j + 1)
                v.wait_ge(sig_done, j + 1)
                v.tensor_tensor(chunks(cin[:, u, CFK:]), ps[:, 0:3, 0:CW], chunks(sg), ALU.mult).then_inc(glu_done, 1)
                v.wait_ge(glu_done, j + 1)
                v.tensor_copy(cs[:, u, :, 0:CFK], before[:, j, :].rearrange("p (b r) -> p b r", b=SB))
                v.tensor_copy(tails[:, j, 0:CFK], cin[:, u, SEQ:SEQ + CFK])
                v.tensor_copy(tails[:, j, CFK:], cin[:, u, CFK + SEQ:CFK + T])
                st(v.tensor_copy(cs[:, u, :, CFK:], cin[:, u, CFK + SEQ:CFK + T].rearrange("p (b r) -> p b r", b=SB)))
                for tap in range(CFK + 1):
                    f = taps[:, tap, j:j + 1]
                    x, o = cin[:, u, tap:tap + SEQ], y[:, j, 0:SEQ]
                    xs, os = cs[:, u, :, tap:tap + SL], samples(y[:, j, :])
                    if tap == 0:
                        v.tensor_scalar(o, x, f, k.column("conf_dw_b", j), ALU.mult, ALU.add)
                        ins = v.tensor_scalar(os, xs, f, k.column("conf_dw_b", j), ALU.mult, ALU.add)
                    else:
                        v.scalar_tensor_tensor(o, x, f, o, ALU.mult, ALU.add)
                        ins = v.scalar_tensor_tensor(os, xs, f, os, ALU.mult, ALU.add)
                    if tap < CFK:
                        st(ins)
                ins.then_inc(conv_done, 1)
            v.wait_ge(conv_done, CFC)
            v.wait_ge(summed, 1)
            v.tensor_scalar(chunks(mean), ps[:, 0:3, 0:CW], 1.0 / (CFC * P), None, ALU.mult).then_inc(by_dve, 1)
            v.wait_ge(by_dve, 1)
            for t in range(CFC):
                v.tensor_tensor(y[:, t, :], y[:, t, :], mean[:, :], ALU.subtract).then_inc(by_dve, 1)
            v.wait_ge(summed, 1 + CFC)
            v.tensor_scalar(chunks(rstd), ps[:, 3:6, 0:CW], 1.0 / (CFC * P), EPS, ALU.mult, ALU.add).then_inc(by_dve, 1)
            v.wait_ge(by_act, 1)
            st(v.reciprocal(rstd[:, :], rstd[:, :]))
            v.wait_ge(by_dve, 2 + CFC)
            for t in range(CFC):
                v.tensor_tensor(y[:, t, :], y[:, t, :], rstd[:, :], ALU.mult).then_inc(by_dve, 1)


def merge(k):
    nc, a, ps = k.nc, k.a, k.ps
    w = Area(k.work[:, :])
    k.merged = w.take(KT, T)
    ring_g, ring_b, sig = w.take(3, KT, P), w.take(3, 4, P), w.take(3, T)
    win = a["w_in"][0].rearrange("(k p) n -> p k n", p=P)
    wb = a["w_branch"][0].rearrange("n (k p) c -> n p k c", p=P)
    w_loaded = [k.sem(f"mg_w_loaded{n}") for n in range(3)]
    g_filled, y_filled, sig_done, y_drained, step_merged = (
        k.sem("mg_" + x) for x in ("g_filled", "y_filled", "sig_done", "y_drained", "step_merged"))

    with nc.Block() as block:
        @block.sync
        def _(sp):
            def load(m, n):
                sp.dma_start(ring_g[:, n], win[:, :, bass.ds(m * P + (COL["br"] + n * D), P)]).then_inc(w_loaded[n], 16)
                sp.dma_start(ring_b[:, n], wb[n][:, :, bass.ds(m * P, P)]).then_inc(w_loaded[n], 16)
            for n in range(3):
                load(0, n)
            with sp.Fori(0, KT - 1) as m:
                for n in range(3):
                    sp.wait_ge(y_filled, m * 3 + (n + 1))
                    load(m + 1, n)

        @block.tensor
        def _(pe):
            with pe.Fori(0, KT) as m:
                for n in range(3):
                    pe.wait_ge(w_loaded[n], (m + 1) * 32)
                    pe.wait_ge(sig_done, m * 3 + (n + 1))
                    for c in range(NCH):
                        for j in range(KT):
                            ins = pe.matmul(ps[:, c, 0:CW], ring_g[:, n, j, :], k.hT[:, j, c * CW:(c + 1) * CW],
                                            start=(j == 0), stop=(j == KT - 1))
                    ins.then_inc(g_filled, 1)
                    pe.wait_ge(y_drained, m * 3 + (n + 1))
                    for c in range(NCH):
                        for j in range(4):
                            ins = pe.matmul(ps[:, 3 + c, 0:CW], ring_b[:, n, j, :], k.oT[:, 4 * n + j, c * CW:(c + 1) * CW],
                                            start=(j == 0), stop=(j == 3))
                    ins.then_inc(y_filled, 1)

        @block.scalar
        def _(act):
            act.sem_inc(sig_done, 1)
            with act.Fori(0, KT) as m:
                for n in range(3):
                    act.wait_ge(g_filled, m * 3 + (n + 1))
                    act.wait_ge(step_merged, m * 3 + (n + 1))
                    act.activation(chunks(sig[:, n, :]), ps[:, 0:3, 0:CW], ACT.Sigmoid).then_inc(sig_done, 1)

        @block.vector
        def _(v):
            v.sem_inc(y_drained, 1)
            v.sem_inc(step_merged, 3)
            with v.Fori(0, KT) as m:
                out = k.merged[:, bass.ds(m, 1), :].rearrange("p a t -> p (a t)")
                for n in range(3):
                    v.wait_ge(y_filled, m * 3 + (n + 1))
                    v.wait_ge(sig_done, m * 3 + (n + 2))
                    v.tensor_tensor(chunks(sig[:, n, :]), ps[:, 3:6, 0:CW], chunks(sig[:, n, :]), ALU.mult).then_inc(y_drained, 1)
                    v.wait_ge(y_drained, m * 3 + (n + 2))
                    if n == 0:
                        v.tensor_copy(out, sig[:, n, :]).then_inc(step_merged, 1)
                        continue
                    v.wait_ge(step_merged, m * 3 + (n + 3))
                    v.tensor_tensor(out, out, sig[:, n, :], ALU.add).then_inc(step_merged, 1)


def add_gated(v, k, st, m, slot, src):
    gate = k.mod[:, slot * KT + m, :]
    x = k.xT[:, m, :]
    tmp = k.gate_tmp
    n = SEQ - 2 * CW
    v.scalar_tensor_tensor(x[:, 0:2 * CW].rearrange("p (c w) -> p c w", c=2), src[:, 0:2, 0:CW], gate[:, 0:1],
                           x[:, 0:2 * CW].rearrange("p (c w) -> p c w", c=2), ALU.mult, ALU.add)
    v.scalar_tensor_tensor(x[:, 2 * CW:SEQ], src[:, 2, 0:n], gate[:, 0:1], x[:, 2 * CW:SEQ], ALU.mult, ALU.add)
    return v.tensor_tensor(tmp[:, m, :, :], src[:, 2, n:CW].rearrange("p (s l) -> p s l", l=SL),
                           bcast(gate[:, 1:NSEQ].unsqueeze(2), SB, SL), ALU.mult)


def project_out(k):
    nc, a, ps = k.nc, k.a, k.ps
    w = Area(k.work[:, KT * T:])
    ring = w.take(2, KT, 256)
    k.gate_tmp = w.take(KT, SB, SL)
    wo = a["w_out"][0].rearrange("(k p) n -> p k n", p=P)
    w_loaded = [k.sem(f"po_w_loaded{s}") for s in range(2)]
    filled, drained, dstep = k.sem("po_filled"), k.sem("po_drained"), k.sem("po_dve_step")
    with nc.Block() as block:
        @block.sync
        def _(sp):
            for b in range(4):
                if b >= 2:
                    sp.wait_ge(filled, 2 * (b - 1))
                sp.dma_start(ring[:, b % 2], wo[:, :, b * 256:(b + 1) * 256]).then_inc(w_loaded[b % 2], 16)

        @block.tensor
        def _(pe):
            for m in range(KT):
                b, u = divmod(m, 2)
                pe.wait_ge(w_loaded[b % 2], 16 * (b // 2 + 1))
                if m >= 2:
                    pe.wait_ge(drained, m - 1)
                for c in range(NCH):
                    for j in range(KT):
                        ins = pe.matmul(ps[:, 3 * u + c, 0:CW], ring[:, b % 2, j, u * P:(u + 1) * P],
                                        k.merged[:, j, c * CW:(c + 1) * CW], start=(j == 0), stop=(j == KT - 1))
                ins.then_inc(filled, 1)

        @block.vector
        def _(v):
            for m in range(KT):
                v.wait_ge(filled, m + 1)
                add_gated(v, k, None, m, 2, ps[:, 3 * (m % 2):3 * (m % 2) + 3, :]).then_inc(drained, 1)
            v.wait_ge(drained, KT)
            for m in range(KT):
                s = samples(k.xT[:, m, :])
                v.tensor_tensor(s, s, k.gate_tmp[:, m], ALU.add)


NT = 9
NG, TOPG, EG, TOPK = 8, 4, 8, 8
NBLK = (E_N + (T * TOPK) // P + 1) // 2 * 2
assert NBLK * P >= T * TOPK and NBLK >= E_N + (T * TOPK - 1) // P
SLOT = 3 * KT * FF
NW = 3
RANGES = ((0, 3 * E_N // 2), (3 * E_N // 2, 7 * E_N // 4), (7 * E_N // 4, NBLK))
ROWS = T + P


def tokens_of(t):
    return P if t < 8 else NS


def plan_moe(k):
    k.ring = k.big[:, 0:NW * SLOT]
    w = Area(k.big[:, NW * SLOT:])
    k.token_idx = w.take(NBLK).bitcast(mybir.dt.int32)
    k.token_gate = w.take(NBLK)
    k.expert_tab = w.take(NBLK).bitcast(mybir.dt.int32)
    k.offset_tab = w.take(NBLK).bitcast(mybir.dt.int32)
    k.end_tab = w.take(E_N).bitcast(mybir.dt.int32)
    k.moe_rest = w.at
    k.u_rows = k.nc.dram_tensor("u_rows", (ROWS, D), F32, kind="Internal").ap()
    k.y_rows = k.nc.dram_tensor("y_rows", (ROWS, D), F32, kind="Internal").ap()


def route(k):
    nc, a, ps = k.nc, k.a, k.ps
    w = Area(k.ring[:, 0:2 * SLOT])
    gates = w.take(NT, E_N)
    rw, bias, brow = w.take(KT, E_N), w.take(E_N), w.take(E_N)
    s, sb, msk, sel = w.take(NT, E_N), w.take(NT, E_N), w.take(NT, E_N), w.take(NT, E_N)
    top2, grp = w.take(NT * NG, 8), w.take(NT, NG)
    gt, eq, before = w.take(NT, NG, NG), w.take(NT, NG, NG), w.take(NG, NG)
    rank, pen, top8, total = w.take(NT, NG), w.take(NT, NG), w.take(NT, 8), w.take(NT)
    prefix, cnt = w.take(NT + 1, E_N), w.take(E_N)
    nblk, bend, steps_row = w.take(E_N), w.take(E_N), w.take(E_N)
    place, slots, slot_gate = w.take(NT, E_N), w.take(NT, TOPK), w.take(NT, TOPK)
    slot_i, blk_i, lane_i = (w.take(NT, TOPK).bitcast(mybir.dt.int32) for _ in range(3))
    blk, lane = w.take(NT, TOPK), w.take(NT, TOPK)
    iota_i, iota_f = w.take(NBLK).bitcast(mybir.dt.int32), w.take(NBLK)
    tok_i, tok, empty = w.take(NT + 1).bitcast(mybir.dt.int32), w.take(NT + 1), w.take(NBLK)
    column, passed_end = w.take(2), w.take(NBLK)
    big = w.take(TOPK * (P + 2 * NBLK))
    match = big[:, 0:NT // 3 * TOPK * E_N].rearrange("p (t s e) -> p t s e", t=NT // 3, s=TOPK)
    place_w = Area(big)
    at_lane, at_blk = place_w.take(TOPK, P), place_w.take(TOPK, 2, NBLK)
    sw = Area(k.ring[:, 2 * SLOT:3 * SLOT])
    wg, wu, wd = sw.take(KT, FF), sw.take(KT, FF), sw.take(2, D)
    tw = Area(k.big[:, NW * SLOT + k.moe_rest:])
    sg, su, hid = tw.take(T), tw.take(T), tw.take(2, T)
    rows = tw.take(2, D)
    zero = tw.take(D)

    names = ("router_loaded", "shared_loaded", "logits", "scored", "bias_ready", "zeroed", "zeros_stored",
             "u_turned", "u_drained", "u_stored0", "u_stored1", "sh_filled", "sh_drained", "sh_hid_ready", "sel_ready", "counted",
             "column_ready", "column_turned", "steps_ready", "stepped", "lanes_ready", "placed", "route_step",
             "route_pool_step", "iota_ready", "columns_copied")
    q = {n: k.sem("rt_" + n) for n in names}
    SH = [(n, f) for f in range(2) for n in "gu"] + [("d", m) for m in range(KT)]

    with nc.Block() as block:
        @block.sync
        def _(sp):
            sp.dma_start(rw[:, :, :], a["router_w"][0].rearrange("(k p) e -> p k e", p=P)).then_inc(q["router_loaded"], 16)
            sp.dma_start(brow[0:1, :], a["router_bias"]).then_inc(q["router_loaded"], 16)
            sp.dma_start(wg[:, :, :], a["sh_w_gate"][0].rearrange("(k p) f -> p k f", p=P)).then_inc(q["shared_loaded"], 16)
            sp.dma_start(wu[:, :, :], a["sh_w_up"][0].rearrange("(k p) f -> p k f", p=P)).then_inc(q["shared_loaded"], 16)
            sp.dma_start(wd[:, :, :], a["sh_w_down"][0].rearrange("(k p) d -> p k d", p=P)).then_inc(q["shared_loaded"], 16)
            sp.wait_ge(q["zeroed"], 1)
            for t in range(8):
                sp.dma_start(k.y_rows[t * P:(t + 1) * P, :], zero[:, :]).then_inc(q["zeros_stored"], 16)
            sp.dma_start(k.y_rows[SEQ:T, :], zero[0:NS, :]).then_inc(q["zeros_stored"], 16)
            for rows_of in (k.y_rows, k.u_rows):
                sp.dma_start(rows_of[T:ROWS, :], zero[:, :]).then_inc(q["zeros_stored"], 16)
            for t in range(NT):
                n = tokens_of(t)
                sp.wait_ge(q["u_drained"], 2 * t + 2)
                sp.dma_start(k.u_rows[t * P:t * P + n, :], rows[0:n, t % 2, :]).then_inc(q[f"u_stored{t % 2}"], 16)
            sp.wait_ge(q["zeros_stored"], 16 * 11)
            sp.wait_ge(q["u_stored0"], 80)
            sp.wait_ge(q["u_stored1"], 64)

        @block.gpsimd
        def _(g):
            st = Steps(g, q["route_pool_step"])
            g.memset(zero[:, :], 0.0).then_inc(q["zeroed"], 1)
            g.iota(iota_i[:, :], pattern=[[1, NBLK]], base=0, channel_multiplier=0)
            g.iota(tok_i[:, 0:NT], pattern=[[P, NT]], base=1, channel_multiplier=1)
            g.iota(tok_i[:, NT:NT + 1], pattern=[[0, 1]], base=T + 1, channel_multiplier=1)
            st(g.memset(steps_row[0:1, :], float(SLOT)))
            g.tensor_copy(iota_f[:, :], iota_i[:, :])
            g.tensor_copy(tok[:, :], tok_i[:, :])
            g.memset(steps_row[0:1, NW - 1:E_N:NW], float(-(NW - 1) * SLOT)).then_inc(q["iota_ready"], 1)
            for f in range(2):
                g.wait_ge(q["sh_drained"], 2 * f + 2)
                g.tensor_tensor(hid[:, f, :], sg[:, :], su[:, :], ALU.mult).then_inc(q["sh_hid_ready"], 1)

        @block.tensor
        def _(pe):
            pe.wait_ge(q["router_loaded"], 32)
            for t in range(NT):
                n = tokens_of(t)
                out = ps[0:n, 6, t * E_N:(t + 1) * E_N] if t < 8 else ps[0:n, 7, 0:E_N]
                for j in range(KT):
                    pe.matmul(out, k.hT[:, j, t * P:t * P + n], rw[:, j, :], start=(j == 0), stop=(j == KT - 1))
            pe.matmul(ps[:, 7, E_N:2 * E_N], k.ones[0:1, :], brow[0:1, :], start=True, stop=True).then_inc(q["logits"], 1)
            for t in range(NT):
                n = tokens_of(t)
                for half in range(2):
                    if t >= 2:
                        pe.wait_ge(q["u_drained"], 2 * (t - 2) + half + 1)
                    for j in range(4):
                        ins = pe.transpose(ps[0:n, 2 * (t % 2) + half, j * P:(j + 1) * P],
                                           k.hT[:, 4 * half + j, t * P:t * P + n], k.ident[:, :])
                    ins.then_inc(q["u_turned"], 1)
            pe.wait_ge(q["shared_loaded"], 48)
            for i, (kind, x) in enumerate(SH):
                out = ps[:, 3 * (i % 2):3 * (i % 2) + 3, 0:CW]
                if i >= 2:
                    pe.wait_ge(q["sh_drained"], i - 1)
                else:
                    pe.wait_ge(q["u_drained"], 2 * NT)
                if kind == "d" and x == 0:
                    pe.wait_ge(q["sh_hid_ready"], 2)
                for c in range(NCH):
                    cc = slice(c * CW, (c + 1) * CW)
                    if kind in "gu":
                        ww = wg if kind == "g" else wu
                        for j in range(KT):
                            ins = pe.matmul(out[:, c, :], ww[:, j, x * P:(x + 1) * P], k.hT[:, j, cc],
                                            start=(j == 0), stop=(j == KT - 1))
                    else:
                        for j in range(2):
                            ins = pe.matmul(out[:, c, :], wd[:, j, x * P:(x + 1) * P], hid[:, j, cc],
                                            start=(j == 0), stop=(j == 1))
                ins.then_inc(q["sh_filled"], 1)
                if i == 3:
                    pe.wait_ge(q["sel_ready"], 1)
                    flat = lambda x: x.rearrange("p t e -> p (t e)")
                    pe.matmul(ps[:, 6, :], k.causal[:, :], flat(sel[:, 0:8, :]), start=True, stop=False)
                    pe.matmul(ps[:, 6, :], k.ones[:, :], flat(prefix[:, 0:8, :]), start=False, stop=True)
                    pe.matmul(ps[:, 7, 0:E_N], k.causal[:, :], sel[:, 8, :], start=True, stop=False)
                    pe.matmul(ps[:, 7, 0:E_N], k.ones[:, :], prefix[:, 8, :], start=False, stop=True)
                    pe.matmul(ps[:, 7, E_N:2 * E_N], k.ones[:, :], prefix[:, NT, :], start=True, stop=True).then_inc(q["counted"], 1)
                if i == 4:
                    pe.wait_ge(q["column_ready"], 1)
                    pe.wait_ge(q["iota_ready"], 1)
                    pe.matmul(ps[0:E_N, 7, 0:1], bend[0:1, :], k.ones[0:1, 0:1], start=True, stop=True)
                    pe.matmul(ps[0:E_N, 7, 1:2], steps_row[0:1, :], k.ones[0:1, 0:1], start=True, stop=True)\
                      .then_inc(q["column_turned"], 1)
                if i == 5:
                    pe.wait_ge(q["steps_ready"], 1)
                    pe.matmul(ps[0:1, 7, 0:NBLK], k.ones[0:E_N - 1, 0:1], passed_end[0:E_N - 1, :], start=True, stop=True)
                    pe.matmul(ps[0:1, 7, NBLK:2 * NBLK], column[0:E_N - 1, 1:2], passed_end[0:E_N - 1, :],
                              start=True, stop=True).then_inc(q["stepped"], 1)
            for t in range(NT):
                pe.wait_ge(q["lanes_ready"], t + 1)
                for n in range(TOPK):
                    ins = pe.matmul(ps[:, 6, 0:2 * NBLK], at_lane[:, n, :], at_blk[:, n, :, :].rearrange("p a b -> p (a b)"),
                                    start=(t == 0 and n == 0), stop=(t == NT - 1 and n == TOPK - 1))
                ins.then_inc(q["placed"], 1)

        @block.scalar
        def _(act):
            act.wait_ge(q["bias_ready"], 1)
            act.wait_ge(q["logits"], 1)
            act.activation(bias[:, :], ps[:, 7, E_N:2 * E_N], ACT.Copy)
            act.activation(s[:, 0:8, :].rearrange("p t e -> p (t e)"), ps[:, 6, :], ACT.Sigmoid)
            act.activation(s[0:NS, 8, :], ps[0:NS, 7, 0:E_N], ACT.Sigmoid).then_inc(q["scored"], 1)
            for t in range(NT):
                n = tokens_of(t)
                for half in range(2):
                    act.wait_ge(q["u_turned"], 2 * t + half + 1)
                    if t >= 2:
                        act.wait_ge(q[f"u_stored{t % 2}"], 16 * (t // 2))
                    act.activation(rows[0:n, t % 2, half * 512:(half + 1) * 512], ps[0:n, 2 * (t % 2) + half, :],
                                   ACT.Copy).then_inc(q["u_drained"], 1)
            for i, (kind, x) in enumerate(SH):
                act.wait_ge(q["sh_filled"], i + 1)
                if kind in "gu" and x == 1:
                    act.wait_ge(q["sh_hid_ready"], 1)
                dst = {"g": sg, "u": su}[kind] if kind in "gu" else k.hT[:, x, :]
                act.activation(chunks(dst), ps[:, 3 * (i % 2):3 * (i % 2) + 3, 0:CW], ACT.Silu if kind == "g" else ACT.Copy)\
                   .then_inc(q["sh_drained"], 1)

        @block.vector
        def _(v):
            st = Steps(v, q["route_step"])
            v.memset(s[:, 8, :], 0.5).then_inc(q["bias_ready"], 1)
            st(v.memset(before[:, :, :], 0.0))
            for i in range(1, NG):
                v.memset(before[:, i, 0:i], 1.0)
            v.wait_ge(q["scored"], 1)
            st(v.tensor_tensor(sb[:, :, :], s[:, :, :], bcast(bias.unsqueeze(1), NT, E_N), ALU.add))
            for t in range(NT):
                for g in range(NG):
                    ins = v.max(top2[:, t * NG + g, :], sb[:, t, g * EG:(g + 1) * EG])
            st(ins)
            pair = top2.rearrange("p (t g) e -> p t g e", g=NG)
            st(v.tensor_tensor(grp[:, :, :], pair[:, :, :, 0], pair[:, :, :, 1], ALU.add))
            mine, other = bcast(grp.unsqueeze(3), NT, NG, NG), bcast(grp.unsqueeze(2), NT, NG, NG)
            v.tensor_tensor(gt[:, :, :, :], other, mine, ALU.is_gt)
            st(v.tensor_tensor(eq[:, :, :, :], other, mine, ALU.is_equal))
            st(v.tensor_tensor(eq[:, :, :, :], eq[:, :, :, :], bcast(before.unsqueeze(1), NT, NG, NG), ALU.mult))
            st(v.tensor_tensor(gt[:, :, :, :], gt[:, :, :, :], eq[:, :, :, :], ALU.add))
            st(v.tensor_reduce(rank[:, :, :], gt[:, :, :, :], AX.X, ALU.add))
            st(v.tensor_scalar(pen[:, :, :], rank[:, :, :], float(TOPG) - 0.5, -1e30, ALU.is_gt, ALU.mult))
            st(v.tensor_tensor(msk.rearrange("p t (g e) -> p t g e", g=NG), sb.rearrange("p t (g e) -> p t g e", g=NG),
                               bcast(pen.unsqueeze(3), NT, NG, EG), ALU.add))
            for t in range(NT):
                ins = v.max(top8[:, t, :], msk[:, t, :])
            st(ins)
            for t in range(NT):
                ins = v.match_replace(out=sel[:, t, :], in_to_replace=top8[:, t, :], in_values=msk[:, t, :], imm_value=-3e38)
            st(ins)
            st(v.tensor_tensor(sel[:, :, :], sel[:, :, :], msk[:, :, :], ALU.not_equal))
            v.memset(sel[NS:2 * NS, 8, :], 0.0)
            st(v.memset(sel[2 * NS:P, 8, :], 0.0))
            st(v.memset(prefix[:, 0, :], 0.0))
            for t in range(NT):
                st(v.tensor_tensor(prefix[:, t + 1, :], prefix[:, t, :], sel[:, t, :], ALU.add))
            v.sem_inc(q["sel_ready"], 1)
            st(v.tensor_tensor(gates[:, :, :], s[:, :, :], sel[:, :, :], ALU.mult))
            st(v.tensor_reduce(total[:, 0:8], gates[:, 0:8, :], AX.X, ALU.add))
            st(v.memset(total[:, 8:9], 1.0))
            st(v.tensor_reduce(total[0:NS, 8:9], gates[0:NS, 8:9, :], AX.X, ALU.add))
            st(v.reciprocal(total[:, :], total[:, :]))
            st(v.tensor_scalar(total[:, :], total[:, :], 2.5, None, ALU.mult))
            st(v.tensor_tensor(gates[:, :, :], gates[:, :, :], bcast(total.unsqueeze(2), NT, E_N), ALU.mult))

            v.wait_ge(q["counted"], 1)
            st(v.tensor_copy(cnt[:, :], ps[:, 7, E_N:2 * E_N]))
            st(v.tensor_scalar(nblk[:, :], cnt[:, :], float(P), 1.0, ALU.is_gt, ALU.add))
            for n in range(2, -(-T // P)):
                st(v.scalar_tensor_tensor(nblk[:, :], cnt[:, :], float(n * P), nblk[:, :], ALU.is_gt, ALU.add))
            st(v.tensor_tensor_scan(bend[:, :], k.ones[:, 0:E_N], nblk[:, :], 0.0, ALU.mult, ALU.add))
            st(v.tensor_tensor(nblk[:, :], bend[:, :], nblk[:, :], ALU.subtract))
            st(v.tensor_scalar(nblk[:, :], nblk[:, :], float(P), None, ALU.mult))
            v.tensor_tensor(place[:, 0:8, :], ps[:, 6, :].rearrange("p (t e) -> p t e", e=E_N), bcast(nblk.unsqueeze(1), 8, E_N), ALU.add)
            st(v.tensor_tensor(place[:, 8, :], ps[:, 7, 0:E_N], nblk[:, :], ALU.add))
            st(v.tensor_tensor(place[:, :, :], place[:, :, :], sel[:, :, :], ALU.mult))
            v.sem_inc(q["column_ready"], 1)
            for t in range(NT):
                ins = v.max(slots[:, t, :], place[:, t, :])
            st(ins)
            st(v.tensor_scalar(slot_i[:, :, :], slots[:, :, :], -1.0, None, ALU.add))
            v.tensor_scalar(blk_i[:, :, :], slot_i[:, :, :], 7, None, ALU.arith_shift_right)
            st(v.tensor_scalar(lane_i[:, :, :], slot_i[:, :, :], P - 1, None, ALU.bitwise_and))
            v.tensor_copy(blk[:, :, :], blk_i[:, :, :])
            st(v.tensor_copy(lane[:, :, :], lane_i[:, :, :]))
            for t in range(0, NT, 3):
                st(v.tensor_tensor(match[:, :, :, :], bcast(slots[:, t:t + 3, :].unsqueeze(3), 3, TOPK, E_N),
                                   bcast(place[:, t:t + 3, :].unsqueeze(2), 3, TOPK, E_N), ALU.is_equal))
                st(v.tensor_tensor(match[:, :, :, :], match[:, :, :, :], bcast(gates[:, t:t + 3, :].unsqueeze(2), 3, TOPK, E_N), ALU.mult))
                st(v.tensor_reduce(slot_gate[:, t:t + 3, :], match[:, :, :, :], AX.X, ALU.add))

            v.wait_ge(q["column_turned"], 1)
            st(v.tensor_copy(column[0:E_N, :], ps[0:E_N, 7, 0:2]))
            st(v.tensor_copy(k.end_tab[0:1, :], bend[0:1, :]))
            v.tensor_scalar(passed_end[0:E_N, :], iota_f[0:E_N, :], column[0:E_N, 0:1], None, ALU.is_ge).then_inc(q["steps_ready"], 1)
            for t in range(NT):
                if t:
                    v.wait_ge(q["placed"], t)
                v.tensor_tensor(at_lane[:, :, :], bcast(lane[:, t, :].unsqueeze(2), TOPK, P), bcast(iota_f[:, 0:P].unsqueeze(1), TOPK, P), ALU.is_equal)
                st(v.tensor_tensor(at_blk[:, :, 0, :], bcast(blk[:, t, :].unsqueeze(2), TOPK, NBLK), bcast(iota_f.unsqueeze(1), TOPK, NBLK), ALU.is_equal))
                v.tensor_tensor(at_blk[:, :, 1, :], at_blk[:, :, 0, :], bcast(slot_gate[:, t, :].unsqueeze(2), TOPK, NBLK), ALU.mult)
                st(v.tensor_scalar(at_blk[:, :, 0, :], at_blk[:, :, 0, :], tok[:, t:t + 1], None, ALU.mult))
                v.sem_inc(q["lanes_ready"], 1)
            v.wait_ge(q["stepped"], 1)
            v.tensor_copy(k.expert_tab[0:1, :], ps[0:1, 7, 0:NBLK])
            v.tensor_copy(k.offset_tab[0:1, :], ps[0:1, 7, NBLK:2 * NBLK])
            v.wait_ge(q["placed"], NT)
            st(v.tensor_scalar(empty[:, :], ps[:, 6, 0:NBLK], 0.0, tok[:, NT:NT + 1], ALU.is_equal, ALU.mult))
            v.scalar_tensor_tensor(k.token_idx[:, :], ps[:, 6, 0:NBLK], -1.0, empty[:, :], ALU.add, ALU.add)
            v.tensor_copy(k.token_gate[:, :], ps[:, 6, NBLK:2 * NBLK])


def experts(k):
    nc, a, ps = k.nc, k.a, k.ps
    w = Area(k.big[:, NW * SLOT + k.moe_rest:])
    x_rows, xT = w.take(2, D), w.take(2, KT, P)
    sg, hid, hidT = w.take(2, FF), w.take(2, FF), w.take(2, 2, P)
    y_out = w.take(2, D)
    idx_in, idx_out = w.take(2).bitcast(mybir.dt.int32), w.take(2).bitcast(mybir.dt.int32)
    DOWN = 2 * KT * FF
    weights_loaded = [k.sem(f"ex_weights_loaded{s}") for s in range(NW)]
    weights_ready = k.sem("ex_weights_ready")
    gathered = [k.sem(f"ex_gathered{u}") for u in range(2)]
    added = k.sem("ex_added")
    x_turned, x_by_act, x_by_dve, up_done, silu_done, hid_done, hid_turned, hid_copied, down_done, y_by_act, y_by_dve = (
        k.sem("ex_" + x) for x in ("x_turned", "x_by_act", "x_by_dve", "up_done", "silu_done", "hid_done", "hid_turned",
                                   "hid_copied", "down_done", "y_by_act", "y_by_dve"))
    idx_in_ready, idx_out_ready, passed, sp_passed = (k.sem("ex_" + x) for x in ("idx_in_ready", "idx_out_ready", "passed", "sp_passed"))

    def over_ranges(eng, run):
        total = eng.value_load(k.end_tab[0:1, E_N - 1:E_N], min_val=1, max_val=NBLK)
        run(*RANGES[0])
        for first, last in RANGES[1:]:
            with eng.If(total > first):
                run(first, last)

    with nc.Block() as block:
        @block.sync
        def _(sp):
            def load(e, s):
                w_s = k.ring[:, s * SLOT:(s + 1) * SLOT]
                up = w_s[:, 0:DOWN].rearrange("p (k g f) -> p k g f", g=2, f=FF)
                for g, name in enumerate(("exp_w_gate", "exp_w_up")):
                    sp.dma_start(up[:, :, g, :], a[name][0, bass.ds(e, 1)].rearrange("e (k p) f -> p (e k) f", p=P))\
                      .then_inc(weights_loaded[s], 16)
                sp.dma_start(w_s[:, DOWN:SLOT].rearrange("p (k d) -> p k d", d=D),
                             a["exp_w_down"][0, bass.ds(e, 1)].rearrange("e (k p) d -> p (e k) d", p=P))\
                  .then_inc(weights_loaded[s], 16)

            for e in range(NW):
                load(e, e)
            for e in range(NW - 1):
                sp.wait_ge(weights_loaded[e], 48)
                sp.sem_inc(weights_ready, 1)
            with sp.Fori(0, (E_N - NW) // NW) as i:
                for s in range(NW):
                    before = sp.value_load(k.end_tab[0:1, bass.ds(i * NW + s, 1)], min_val=1, max_val=NBLK)
                    wait_before_addressed(sp, down_done, before, sp_passed)
                    load(i * NW + (NW + s), s)
                    sp.wait_ge(weights_loaded[(s - 1) % NW], (i + (1 if s == 0 else 2)) * 48)
                    sp.sem_inc(weights_ready, 1)
            for e in range(NW + (E_N - NW) // NW * NW, E_N):
                before = sp.value_load(k.end_tab[0:1, e - NW:e - NW + 1], min_val=1, max_val=NBLK)
                wait_before_addressed(sp, down_done, before, sp_passed)
                load(e, e % NW)
                sp.wait_ge(weights_loaded[(e - 1) % NW], ((e - 1) // NW + 1) * 48)
                sp.sem_inc(weights_ready, 1)
            sp.wait_ge(weights_loaded[(E_N - 1) % NW], ((E_N - 1) // NW + 1) * 48)
            sp.sem_inc(weights_ready, 1)

        @block.gpsimd
        def _(g):
            def gather(n, u):
                if not (isinstance(n, int) and n < 2):
                    g.wait_ge(x_turned, n - 1)
                    g.sem_inc(passed, 1)
                g.tensor_copy(idx_in[:, u:u + 1], k.token_idx[:, bass.ds(n, 1)]).then_inc(idx_in_ready, 1)
                g.wait_ge(idx_in_ready, n + 1)
                g.sem_inc(passed, 1)
                g.indirect_dma_start(out=x_rows[:, u, :], out_offset=None, in_=k.u_rows,
                                     in_offset=bass.IndirectOffsetOnAxis(idx_in[:, u:u + 1], 0)).then_inc(gathered[u], 16)

            def add(n, u):
                if not (isinstance(n, int) and n == 0):
                    g.wait_ge(added, n * 16)
                    g.sem_inc(passed, 1)
                g.tensor_copy(idx_out[:, u:u + 1], k.token_idx[:, bass.ds(n, 1)]).then_inc(idx_out_ready, 1)
                g.wait_ge(idx_out_ready, n + 1)
                g.sem_inc(passed, 1)
                g.wait_ge(y_by_act, n + 2)
                g.sem_inc(passed, 1)
                g.wait_ge(y_by_dve, n + 2)
                g.sem_inc(passed, 1)
                g.indirect_dma_start(out=k.y_rows, out_offset=bass.IndirectOffsetOnAxis(idx_out[:, u:u + 1], 0),
                                     in_=y_out[:, u, :], in_offset=None, compute_op=ALU.add).then_inc(added, 16)

            def run(first, last):
                for n in range(3):
                    gather(first + n, n % 2)
                for n in range(2):
                    gather(first + n + 3, (n + 1) % 2)
                    add(first + n, n)
                with g.Fori(1, (last - first) // 2 - 2) as j:
                    for r in range(2):
                        gather(j * 2 + (first + 3 + r), (1 + r) % 2)
                        add(j * 2 + (first + r), r)
                gather(last - 1, 1)
                for n in range(last - 4, last):
                    add(n, n % 2)
                g.wait_ge(added, 16 * last)
            over_ranges(g, run)

        def offset_of(pe, n):
            return pe.value_load(k.offset_tab[0:1, bass.ds(n, 1)], min_val=0, max_val=(NW - 1) * SLOT)

        @block.tensor
        def _(pe):
            def turn_x(n, u, half):
                pe.wait_ge(gathered[u], (half + 1) * 16)
                if not (isinstance(n, int) and n == 0):
                    pe.wait_ge(x_by_act, n)
                    pe.wait_ge(x_by_dve, n)
                for j in range(KT):
                    ins = pe.transpose(ps[:, j // 4, (j % 4) * P:(j % 4 + 1) * P], x_rows[:, u, j * P:(j + 1) * P], k.ident[:, :])
                ins.then_inc(x_turned, 1)

            def up(n, u):
                e = pe.value_load(k.expert_tab[0:1, bass.ds(n, 1)], min_val=0, max_val=E_N - 1)
                off = offset_of(pe, n)
                pe.wait_ge(x_by_act, n + 1)
                pe.wait_ge(x_by_dve, n + 1)
                pe.wait_ge(weights_ready, e + 1)
                for j in range(KT):
                    ins = pe.matmul(ps[:, 2 + u, :], xT[:, u, j, :], k.big[:, bass.ds(off + j * (2 * FF), 2 * FF)],
                                    start=(j == 0), stop=(j == KT - 1))
                ins.then_inc(up_done, 1)

            def down(n, u):
                off = offset_of(pe, n)
                pe.wait_ge(hid_copied, n + 1)
                pe.wait_ge(y_by_act, n + 1)
                pe.wait_ge(y_by_dve, n + 1)
                for half in range(2):
                    for j in range(2):
                        ins = pe.matmul(ps[:, 5 + half, :], hidT[:, u, j, :], k.big[:, bass.ds(off + (DOWN + j * D + half * 512), 512)],
                                        start=(j == 0), stop=(j == 1))
                ins.then_inc(down_done, 1)

            def turn_hid(n, u):
                pe.wait_ge(hid_done, n + 1)
                if not (isinstance(n, int) and n == 0):
                    pe.wait_ge(hid_copied, n)
                for j in range(2):
                    ins = pe.transpose(ps[:, 4, j * P:(j + 1) * P], hid[:, u, j * P:(j + 1) * P], k.ident[:, :])
                ins.then_inc(hid_turned, 1)

            def run(first, last):
                turn_x(first, 0, first // 2)
                up(first, 0)
                turn_x(first + 1, 1, first // 2)
                turn_hid(first, 0)
                with pe.Fori(0, (last - first) // 2 - 1) as j:
                    for r in range(2):
                        n, u = j * 2 + (first + 1 + r), (1 + r) % 2
                        up(n, u)
                        turn_x(j * 2 + (first + 2 + r), 1 - u, j + (first // 2 + 1))
                        down(j * 2 + (first + r), 1 - u)
                        turn_hid(n, u)
                up(last - 1, 1)
                down(last - 2, 0)
                turn_hid(last - 1, 1)
                down(last - 1, 1)
            over_ranges(pe, run)

        @block.scalar
        def _(act):
            def copy_x(n, u):
                act.wait_ge(x_turned, n + 1)
                act.activation(xT[:, u, 0:4, :].rearrange("p a b -> p (a b)"), ps[:, 0, :], ACT.Copy).then_inc(x_by_act, 1)

            def silu(n, u):
                act.wait_ge(up_done, n + 1)
                act.activation(sg[:, u, :], ps[:, 2 + u, 0:FF], ACT.Silu).then_inc(silu_done, 1)

            def copy_y(n, u):
                act.wait_ge(down_done, n + 1)
                if not (isinstance(n, int) and n < 2):
                    act.wait_ge(added, (n - 1) * 16)
                act.activation(y_out[:, u, 0:512], ps[:, 5, :], ACT.Copy).then_inc(y_by_act, 1)

            def copy_hid(n, u):
                act.wait_ge(hid_turned, n + 1)
                act.activation(hidT[:, u, :, :].rearrange("p a b -> p (a b)"), ps[:, 4, 0:FF], ACT.Copy).then_inc(hid_copied, 1)

            act.sem_inc(y_by_act, 1)

            def run(first, last):
                copy_x(first, 0)
                silu(first, 0)
                copy_x(first + 1, 1)
                copy_hid(first, 0)

                def step(n, u):
                    silu(n, u)
                    copy_x(n + 1, 1 - u)
                    copy_y(n - 1, 1 - u)
                    copy_hid(n, u)
                step(first + 1, 1)
                step(first + 2, 0)
                with act.Fori(1, (last - first) // 2 - 1) as j:
                    for r in range(2):
                        step(j * 2 + (first + 1 + r), (1 + r) % 2)
                silu(last - 1, 1)
                copy_y(last - 2, 0)
                copy_hid(last - 1, 1)
                copy_y(last - 1, 1)
            over_ranges(act, run)

        @block.vector
        def _(v):
            def copy_x(n, u):
                v.wait_ge(x_turned, n + 1)
                v.tensor_copy(xT[:, u, 4:8, :].rearrange("p a b -> p (a b)"), ps[:, 1, :]).then_inc(x_by_dve, 1)

            def hidden(n, u):
                v.wait_ge(silu_done, n + 1)
                v.scalar_tensor_tensor(hid[:, u, :], sg[:, u, :], k.token_gate[:, bass.ds(n, 1)], ps[:, 2 + u, FF:2 * FF],
                                       ALU.mult, ALU.mult).then_inc(hid_done, 1)

            def copy_y(n, u):
                v.wait_ge(down_done, n + 1)
                if not (isinstance(n, int) and n < 2):
                    v.wait_ge(added, (n - 1) * 16)
                v.tensor_copy(y_out[:, u, 512:D], ps[:, 6, :]).then_inc(y_by_dve, 1)

            v.sem_inc(y_by_dve, 1)

            def run(first, last):
                copy_x(first, 0)
                hidden(first, 0)
                copy_x(first + 1, 1)

                def step(n, u):
                    hidden(n, u)
                    copy_x(n + 1, 1 - u)
                    copy_y(n - 1, 1 - u)
                step(first + 1, 1)
                step(first + 2, 0)
                with v.Fori(1, (last - first) // 2 - 1) as j:
                    for r in range(2):
                        step(j * 2 + (first + 1 + r), (1 + r) % 2)
                hidden(last - 1, 1)
                copy_y(last - 2, 0)
                copy_y(last - 1, 1)
            over_ranges(v, run)


def add_experts(k):
    nc, ps = k.nc, k.ps
    rows = Area(k.ring).take(NT, D)
    k.y = k.hT
    loaded = [k.sem(f"ae_loaded{t}") for t in range(NT)]
    turned, taken = k.sem("ae_turned"), k.sem("ae_added")
    with nc.Block() as block:
        @block.sync
        def _(sp):
            for t in range(NT):
                n = tokens_of(t)
                sp.dma_start(rows[0:n, t, :], k.y_rows[t * P:t * P + n, :]).then_inc(loaded[t], 16)

        @block.tensor
        def _(pe):
            for t in range(NT):
                n = tokens_of(t)
                pe.wait_ge(loaded[t], 16)
                for half in range(2):
                    b = 2 * t + half
                    if b >= 4:
                        pe.wait_ge(taken, b - 3)
                    for j in range(4):
                        ins = pe.transpose(ps[:, b % 4, j * P:j * P + n], rows[0:n, t, (4 * half + j) * P:(4 * half + j + 1) * P],
                                           k.ident[0:n, 0:n])
                    ins.then_inc(turned, 1)

        @block.vector
        def _(v):
            for t in range(NT):
                n = tokens_of(t)
                for half in range(2):
                    b = 2 * t + half
                    v.wait_ge(turned, b + 1)
                    y = k.y[:, 4 * half:4 * half + 4, t * P:t * P + n]
                    v.tensor_tensor(y, y, ps[:, b % 4, :].rearrange("p (a b) -> p a b", a=4)[:, :, 0:n], ALU.add).then_inc(taken, 1)


def add_moe(k):
    nc = k.nc
    dstep = k.sem("am_step")
    with nc.Block() as block:
        @block.vector
        def _(v):
            st = Steps(v, dstep)
            for m in range(KT):
                gate = k.mod[:, 5 * KT + m, :]
                x = k.xT[:, m, :]
                v.scalar_tensor_tensor(x[:, 0:SEQ], k.y[:, m, 0:SEQ], gate[:, 0:1], x[:, 0:SEQ], ALU.mult, ALU.add)
                ys = samples(k.y[:, m, :])
                st.done(v.tensor_tensor(ys, ys, bcast(gate[:, 1:NSEQ].unsqueeze(2), SB, SL), ALU.mult))
            st.wait()
            for m in range(KT):
                s = samples(k.xT[:, m, :])
                v.tensor_tensor(s, s, samples(k.y[:, m, :]), ALU.add)


def store_y(k):
    nc, a, ps = k.nc, k.a, k.ps
    rows = Area(k.oT[:, :, :].rearrange("p a b -> p (a b)")).take(9, D)
    filled, drained_a, drained_v, stored = k.sem("sy_filled"), k.sem("sy_by_act"), k.sem("sy_by_dve"), k.sem("sy_stored")
    with nc.Block() as block:
        @block.tensor
        def _(pe):
            for t in range(NT):
                n = P if t < 8 else NS
                for half in range(2):
                    if t >= 2:
                        pe.wait_ge(drained_v if half else drained_a, t - 1)
                    for j in range(4):
                        ins = pe.transpose(ps[0:n, 2 * (t % 2) + half, j * P:(j + 1) * P], k.hT[:, 4 * half + j, t * P:t * P + n], k.ident[:, :])
                    ins.then_inc(filled, 1)

        @block.scalar
        def _(act):
            for t in range(NT):
                n = P if t < 8 else NS
                act.wait_ge(filled, 2 * t + 1)
                act.activation(rows[0:n, t, 0:512], ps[0:n, 2 * (t % 2), :], ACT.Copy).then_inc(drained_a, 1)

        @block.vector
        def _(v):
            for t in range(NT):
                n = P if t < 8 else NS
                v.wait_ge(filled, 2 * t + 2)
                v.tensor_copy(rows[0:n, t, 512:D], ps[0:n, 2 * (t % 2) + 1, :]).then_inc(drained_v, 1)

        @block.sync
        def _(sp):
            for t in range(NT):
                sp.wait_ge(drained_a, t + 1)
                sp.wait_ge(drained_v, t + 1)
                if t < 8:
                    sp.dma_start(a["y_prompt"][0, t * P:(t + 1) * P, :], rows[:, t, :]).then_inc(stored, 16)
                else:
                    sp.dma_start(a["y_sample"].rearrange("s l d -> (s l) d"), rows[0:NS, t, :]).then_inc(stored, 16)
            sp.wait_ge(stored, 16 * NT)


def step_program(nc, a):
    with ExitStack() as ctx:
        k = Core(nc, ctx, a)
        setup(k)
        norm(k, "mix", 0)
        delta_project(k)
        delta_rows(k)
        delta_rule(k)
        gated_norm(k, "dn", k.qkv[:, 2 * H:3 * H, :], k.oT[:, 0:H, :], k.column("dn_norm_w"), Area(k.work[:, 0:2 * H * T]))
        gla_project(k)
        gla_rule(k)
        gated_norm(k, "gn", k.gla[:, 4:8, :], k.oT[:, 4:8, :], k.column("gla_norm_w"), Area(k.work[:, 0:4 * T]))
        k.fresh_semaphores()
        conformer(k)
        merge(k)
        project_out(k)
        norm(k, "ffn", 3)
        k.fresh_semaphores()
        plan_moe(k)
        route(k)
        experts(k)
        add_experts(k)
        add_moe(k)
        norm(k, "final", None)
        store_y(k)
        k.fresh_semaphores()


INS = ["x_prompt", "x_sample", "state_delta", "state_delta_conv", "state_gla", "state_conv", "c_prompt", "c_sample",
       "ada_w", "ada_b", "norm_mix_w", "w_in", "dn_conv_w", "dn_A_log", "dn_dt_bias", "dn_norm_w", "gla_gate_w",
       "gla_gate_b", "gla_norm_w", "conf_dw_w", "conf_dw_b", "conf_ln_w", "conf_ln_b", "w_branch", "w_out",
       "norm_ffn_w", "router_w", "router_bias", "exp_w_gate", "exp_w_up", "exp_w_down", "sh_w_gate", "sh_w_up",
       "sh_w_down", "final_norm_w"]


def kernel(**inputs):
    import numpy as np
    import concourse.bacc as bacc
    from concourse.bass_utils import run_bass_kernel_spmd

    nc = bacc.Bacc("TRN2", target_bir_lowering=False, num_devices=1)
    arrays, a = {}, {}
    for name in INS:
        x = np.ascontiguousarray(inputs[name])
        arrays[f"in_{name}"] = x
        a[name] = nc.dram_tensor(f"in_{name}", x.shape, mybir.dt.from_np(x.dtype), kind="ExternalInput").ap()
    for name, shape in OUTS:
        a[name] = nc.dram_tensor(f"out_{name}", shape, F32, kind="ExternalOutput").ap()
    step_program(nc, a)
    r = run_bass_kernel_spmd(nc, [arrays], core_ids=[0])
    return tuple(r.results[0][f"out_{name}"] for name, _ in OUTS)
```

```python
from contextlib import ExitStack

import concourse.bass as bass
from concourse import mybir

F32 = mybir.dt.float32
ACT = mybir.ActivationFunctionType
ALU = mybir.AluOpType
AX = mybir.AxisListType

P = 128
D = 1024
KT = D // P
SEQ = 1024
SB, SL = 8, 4
NS = SB * SL
T = SEQ + NS
NCH = 3
CW = T // NCH
C = 128
NC = SEQ // C
H = 4
LEVELS = 7
DNK, DNC = 3, 12
GDK = 64
CFK, CFC = 30, 4
NSEQ = 1 + SB
E_N, FF = 64, 256
EPS = 1e-6
COL = dict(qkv=0, z=1536, ba=2048, gqk=2056, gv=2568, gr=3080, glr=3592, conf=3608, br=4632)
RB, RG, RT, RE = 0, 32, 64, 96

PRM = {}
_at = 0
for _name, _n in (("ada_b", 48), ("norm_mix_w", 8), ("norm_ffn_w", 8), ("final_norm_w", 8), ("conf_dw_b", 4),
                  ("conf_ln_w", 4), ("conf_ln_b", 4), ("dn_norm_w", 1), ("gla_norm_w", 1), ("gla_gate_b", 2)):
    PRM[_name] = _at
    _at += _n
N_PRM = _at
WORK = 17920


class Area:

    def __init__(self, ap):
        self.ap, self.at, self.size = ap, 0, ap.shape[1]

    def take(self, *shape):
        n = 1
        for s in shape:
            n *= s
        piece = self.ap[:, self.at:self.at + n]
        self.at += n
        assert self.at <= self.size, (self.at, self.size)
        if len(shape) == 1:
            return piece
        names = "abcd"[:len(shape)]
        return piece.rearrange(f"p ({' '.join(names)}) -> p {' '.join(names)}", **dict(zip(names, shape)))


class Steps:

    def __init__(self, eng, sem):
        self.eng, self.sem, self.n, self.base = eng, sem, 0, 0

    def loop(self, i, per):
        self.base, self.first, self.per = self.n + i * per, self.n, per
        self.n = 0

    def end(self, count):
        assert self.n == self.per, (self.n, self.per)
        self.n, self.base = self.first + self.per * count, 0

    def done(self, ins):
        ins.then_inc(self.sem, 1)
        self.n += 1

    def wait(self):
        self.eng.wait_ge(self.sem, self.base + self.n)

    def __call__(self, ins):
        self.done(ins)
        self.wait()


def chunks(ap):
    return ap.rearrange("p (c w) -> p c w", c=NCH)


def wait_before_addressed(eng, sem, value, passed):
    eng.wait_ge(sem, value)
    eng.sem_inc(passed, 1)


def bcast(ap, *shape):
    return ap.to_broadcast([ap.shape[0], *shape])


def samples(ap):
    return ap[:, SEQ:T].rearrange("p (s l) -> p s l", l=SL)


class Core:
    def __init__(self, nc, ctx, a):
        self.nc, self.ctx, self.a = nc, ctx, a
        self.sems = []
        sb = lambda name, *shape: ctx.enter_context(nc.sbuf_tensor(name, [P, *shape], F32))
        self.xT = sb("xT", KT, T)
        self.hT = sb("hT", KT, T)
        self.big = sb("big", 12 * T + WORK)
        self.oT = self.big[:, 0:12 * T].rearrange("p (a b) -> p a b", b=T)
        self.work = self.big[:, 12 * T:]
        self.ident = sb("ident", P)
        self.ones = sb("ones", P)
        self.pair = sb("pair", LEVELS + 1, C)
        self.causal = sb("causal", C)
        self.causal_s = sb("causal_s", NS)
        self.inseq = sb("inseq", SB)
        self.carry = sb("carry", T)
        self.pick = sb("pick", 3 * H, P)
        self.pick8 = sb("pick8", 8, P)
        self.unit8 = sb("unit8", 8, 8)
        self.prm = sb("prm", P)
        self.mod = sb("mod", 6 * KT, NSEQ)
        self.ps = ctx.enter_context(nc.psum_tensor("ps", [P, 8, 512], F32))

    def sem(self, name):
        self.sems.append(self.nc.alloc_semaphore(name))
        return self.sems[-1]

    def fresh_semaphores(self):
        self.nc.all_engine_barrier()
        self.nc.clear_and_free_semaphores(self.sems)
        self.nc.all_engine_barrier()
        self.sems = []

    def column(self, name, n=0):
        return self.prm[:, PRM[name] + n:PRM[name] + n + 1]


def setup(k):
    nc, a, ps = k.nc, k.a, k.ps
    w = Area(k.work[:, :])
    xin = w.take(9, D)
    prm_in = w.take(P)
    cin = w.take(D)
    csl = w.take(D)
    cT = w.take(KT, NSEQ)
    AW = 512
    NR = 3
    NB = 6 * D // AW
    ring = k.oT[:, :, :].rearrange("p a b -> p (a b)")[:, 0:NR * KT * AW].rearrange("p (s k n) -> p s k n", s=NR, k=KT)
    mod_rows = w.take(6 * D)
    x_loaded, prm_loaded, c_loaded = k.sem("x_loaded"), k.sem("prm_loaded"), k.sem("c_loaded")
    ada_loaded = [k.sem(f"ada_loaded{s}") for s in range(NR)]
    consts_done, pool_step = k.sem("consts_done"), k.sem("setup_pool_step")
    ones_done, silu_done = k.sem("ones_done"), k.sem("silu_c_done")
    x_turned, x_copied = k.sem("x_turned"), k.sem("x_copied")
    p_turned, p_copied = k.sem("p_turned"), k.sem("p_copied")
    x_copied_v = k.sem("x_copied_by_vector")
    mod_done, mod_copied, mod_turned = k.sem("mod_done"), k.sem("mod_copied"), k.sem("mod_turned")
    ident_done, dstep = k.sem("ident_done"), k.sem("setup_dve_step")
    ada = a["ada_w"][0].rearrange("(k p) n -> p k n", p=P)

    with nc.Block() as block:
        @block.sync
        def _(sp):
            for name, n in (("ada_b", 48), ("norm_mix_w", 8), ("norm_ffn_w", 8), ("conf_dw_b", 4), ("conf_ln_w", 4),
                            ("conf_ln_b", 4), ("dn_norm_w", 1), ("gla_norm_w", 1), ("gla_gate_b", 2)):
                src = a[name][0].rearrange("(n p) -> n p", p=P)
                sp.dma_start(prm_in[PRM[name]:PRM[name] + n, :], src).then_inc(prm_loaded, 16)
            r = PRM["final_norm_w"]
            sp.dma_start(prm_in[r:r + 8, :], a["final_norm_w"].rearrange("(n p) -> n p", p=P)).then_inc(prm_loaded, 16)
            sp.dma_start(cin[0:1, :], a["c_prompt"]).then_inc(c_loaded, 16)
            sp.dma_start(cin[1:NSEQ, :], a["c_sample"]).then_inc(c_loaded, 16)
            for s in range(NR):
                sp.dma_start(ring[:, s], ada[:, :, s * AW:(s + 1) * AW]).then_inc(ada_loaded[s], 16)
            sp.dma_start(xin[:, 0:8, :], a["x_prompt"][0].rearrange("(t p) d -> p t d", p=P)).then_inc(x_loaded, 16)
            sp.dma_start(xin[0:NS, 8, :], a["x_sample"].rearrange("s l d -> (s l) d")).then_inc(x_loaded, 16)
            with sp.Fori(0, NB // NR - 1) as i:
                for s in range(NR):
                    sp.wait_ge(mod_done, i * NR + (s + 1))
                    sp.dma_start(ring[:, s], ada[:, :, bass.ds((i + 1) * (NR * AW) + s * AW, AW)])\
                      .then_inc(ada_loaded[s], 16)

        @block.gpsimd
        def _(g):
            st = Steps(g, pool_step)
            st(g.memset(k.ident[:, :], 0.0))
            g.affine_select(out=k.ident[:, :], in_=k.ident[:, :], compare_op=ALU.not_equal, fill=1.0,
                            base=0, pattern=[[-1, P]], channel_multiplier=1).then_inc(ident_done, 1)
            g.memset(k.pair[:, :, :], 0.0)
            g.memset(k.causal[:, :], 1.0)
            g.memset(k.causal_s[:, :], 1.0)
            g.memset(k.inseq[:, :], 1.0)
            g.memset(k.unit8[:, :, :], 0.0)
            g.memset(k.carry[:, :], 1.0)
            st(g.memset(k.ones[:, :], 1.0))
            g.wait_ge(ident_done, 1)
            g.affine_select(out=k.causal[:, :], in_=k.causal[:, :], compare_op=ALU.is_ge, fill=0.0,
                            base=0, pattern=[[1, C]], channel_multiplier=-1)
            for l in range(LEVELS):
                s = 1 << l
                v = k.pair[:, l, :].rearrange("p (b h r) -> p b h r", h=2, r=s)
                g.memset(v[:, :, 1, :], 1.0)
            g.memset(k.unit8[:, :, :].rearrange("p a b -> p (a b)")[:, 0:64:9], 1.0)
            st(g.memset(k.carry[:, 0:SEQ:C], 0.0))
            g.memset(k.carry[:, SEQ:T:SL], 0.0)
            for l in range(LEVELS):
                s = 1 << l
                v = k.pair[:, l, :].rearrange("p (b h r) -> p b h r", h=2, r=s)[:, :, 1, :]
                g.affine_select(out=v, in_=v, compare_op=ALU.is_ge, fill=0.0, base=0,
                                pattern=[[-2 * s, C // (2 * s)], [0, s]], channel_multiplier=1)
            cs = k.causal_s[:, :].rearrange("p (b r) -> p b r", r=SL)
            g.affine_select(out=cs, in_=cs, compare_op=ALU.is_ge, fill=0.0, base=0,
                            pattern=[[SL, SB], [1, SL]], channel_multiplier=-1)
            g.affine_select(out=k.inseq[:, :], in_=k.inseq[:, :], compare_op=ALU.is_ge, fill=0.0, base=0,
                            pattern=[[-SL, SB]], channel_multiplier=1)
            st(g.tensor_copy(k.pair[:, LEVELS, :], k.ident[:, :]))
            for l in range(LEVELS):
                s = 1 << l
                v = k.pair[:, l, :].rearrange("p (b h r) -> p b h r", h=2, r=s)[:, :, 1, :]
                g.affine_select(out=v, in_=v, compare_op=ALU.is_ge, fill=0.0, base=s - 1,
                                pattern=[[2 * s, C // (2 * s)], [0, s]], channel_multiplier=-1)
            g.affine_select(out=cs, in_=cs, compare_op=ALU.is_ge, fill=0.0, base=0,
                            pattern=[[-SL, SB], [0, SL]], channel_multiplier=1)
            g.affine_select(out=k.inseq[:, :], in_=k.inseq[:, :], compare_op=ALU.is_ge, fill=0.0, base=SL - 1,
                            pattern=[[SL, SB]], channel_multiplier=-1)
            for h in range(H):
                for n, r in enumerate((RG + h, RB + h, RE + h)):
                    g.tensor_copy(k.pick[:, 3 * h + n, :], bcast(k.ident[:, r:r + 1], P))
            for j in range(8):
                ins = g.tensor_copy(k.pick8[0:8, j, :], bcast(k.ident[0:8, j:j + 1], P))
            ins.then_inc(consts_done, 1)

        @block.scalar
        def _(act):
            act.wait_ge(c_loaded, 32)
            act.activation(csl[0:NSEQ, :], cin[0:NSEQ, :], ACT.Silu).then_inc(silu_done, 1)
            for b in range(NB):
                act.wait_ge(mod_done, b + 1)
                act.activation(mod_rows[0:NSEQ, b * AW:(b + 1) * AW], ps[0:NSEQ, 4 + b % 2, :], ACT.Copy).then_inc(mod_copied, 1)
            for t in range(9):
                n = P if t < 8 else NS
                act.wait_ge(x_turned, 2 * t + 2)
                act.activation(k.xT[:, 4:8, t * P:t * P + n], ps[:, 3, :].rearrange("p (k n) -> p k n", k=4)[:, :, 0:n],
                               ACT.Copy).then_inc(x_copied, 1)

        @block.tensor
        def _(pe):
            pe.wait_ge(ident_done, 1)
            pe.wait_ge(prm_loaded, 160)
            pe.transpose(ps[:, 0, 0:N_PRM], prm_in[0:N_PRM, :], k.ident[0:N_PRM, 0:N_PRM]).then_inc(p_turned, 1)
            pe.wait_ge(silu_done, 1)
            for j in range(KT):
                ins = pe.transpose(ps[:, 1, j * NSEQ:(j + 1) * NSEQ], csl[0:NSEQ, j * P:(j + 1) * P],
                                   k.ident[0:NSEQ, 0:NSEQ])
            ins.then_inc(p_turned, 1)
            pe.wait_ge(p_copied, 2)
            def mod_block(b, slot, times):
                pe.wait_ge(ada_loaded[slot], times * 16)
                if not (isinstance(b, int) and b < 2):
                    pe.wait_ge(mod_copied, b - 1)
                for j in range(KT):
                    ins = pe.matmul(ps[0:NSEQ, 4 + b % 2, :], cT[:, j, :], ring[:, slot, j, :], start=(j == 0), stop=(j == KT - 1))
                ins.then_inc(mod_done, 1)

            def turn_mod(b):
                pe.wait_ge(mod_copied, b + 1)
                for u in range(AW // P):
                    n = b * (AW // P) + u
                    ins = pe.transpose(ps[:, 0, n * NSEQ:(n + 1) * NSEQ], mod_rows[0:NSEQ, n * P:(n + 1) * P],
                                       k.ident[0:NSEQ, 0:NSEQ])
                return ins
            for b in range(NB):
                mod_block(b, b % NR, b // NR + 1)
                if b:
                    turn_mod(b - 1)
            turn_mod(NB - 1).then_inc(mod_turned, 1)
            pe.wait_ge(x_loaded, 32)
            for t in range(9):
                n = P if t < 8 else NS
                for half in range(2):
                    if t:
                        pe.wait_ge(x_copied if half else x_copied_v, t)
                    for j in range(4):
                        ins = pe.transpose(ps[:, 2 + half, j * P:j * P + n],
                                           xin[0:n, t, (4 * half + j) * P:(4 * half + j + 1) * P],
                                           k.ident[0:n, 0:n])
                    ins.then_inc(x_turned, 1)

        @block.vector
        def _(v):
            st = Steps(v, dstep)
            v.wait_ge(p_turned, 1)
            v.tensor_copy(k.prm[:, 0:N_PRM], ps[:, 0, 0:N_PRM]).then_inc(p_copied, 1)
            v.wait_ge(p_turned, 2)
            v.tensor_copy(cT[:, :, :].rearrange("p a b -> p (a b)"), ps[:, 1, 0:KT * NSEQ]).then_inc(p_copied, 1)
            v.wait_ge(mod_turned, 1)
            v.wait_ge(p_copied, 2)
            st(v.tensor_tensor(k.mod[:, :, :], ps[:, 0, 0:48 * NSEQ].rearrange("p (a b) -> p a b", b=NSEQ),
                               bcast(k.prm[:, 0:48].unsqueeze(2), 48, NSEQ), ALU.add))
            for slot, name in ((1, "norm_mix_w"), (4, "norm_ffn_w")):
                m = k.mod[:, slot * KT:(slot + 1) * KT, :]
                st.done(v.scalar_tensor_tensor(m, m, 1.0, bcast(k.prm[:, PRM[name]:PRM[name] + 8].unsqueeze(2), 8, NSEQ),
                                       ALU.add, ALU.mult))
            for t in range(9):
                n = P if t < 8 else NS
                v.wait_ge(x_turned, 2 * t + 1)
                v.tensor_copy(k.xT[:, 0:4, t * P:t * P + n], ps[:, 2, :].rearrange("p (k n) -> p k n", k=4)[:, :, 0:n])\
                 .then_inc(x_copied_v, 1)


def norm(k, tag, slot, first_loads):
    nc, ps = k.nc, k.ps
    w = Area(k.work[:, :])
    sq = w.take(2, T)
    rstd = w.take(T)
    squared, summed, rooted = k.sem(tag + "_squared"), k.sem(tag + "_summed"), k.sem(tag + "_rooted")
    scaled, normed, dstep = k.sem(tag + "_mean"), k.sem(tag + "_normed"), k.sem(tag + "_dve_step")

    with nc.Block() as block:
        @block.sync
        def _(sp):
            first_loads(sp)

        @block.scalar
        def _(act):
            for j in range(KT):
                if j >= 2:
                    act.wait_ge(summed, j - 1)
                act.activation(sq[:, j % 2, :], k.xT[:, j, :], ACT.Square).then_inc(squared, 1)
            act.wait_ge(scaled, 1)
            act.activation(rstd[:, :], rstd[:, :], ACT.Sqrt).then_inc(rooted, 1)
            for j in range(KT):
                act.wait_ge(normed, j + 1)
                act.activation(k.hT[:, j, 0:SEQ], k.hT[:, j, 0:SEQ], ACT.Identity, scale=k.mod[:, (slot + 1) * KT + j, 0:1],
                               bias=k.mod[:, slot * KT + j, 0:1])

        @block.tensor
        def _(pe):
            for j in range(KT):
                pe.wait_ge(squared, j + 1)
                for c in range(NCH):
                    ins = pe.matmul(ps[:, c, 0:CW], k.ones[:, :], sq[:, j % 2, c * CW:(c + 1) * CW],
                                    start=(j == 0), stop=(j == KT - 1))
                ins.then_inc(summed, 1)

        @block.vector
        def _(v):
            st = Steps(v, dstep)
            v.wait_ge(summed, KT)
            v.tensor_scalar(chunks(rstd), ps[:, 0:NCH, 0:CW], 1.0 / D, EPS, ALU.mult, ALU.add).then_inc(scaled, 1)
            v.wait_ge(rooted, 1)
            st(v.reciprocal(rstd[:, :], rstd[:, :]))
            for j in range(KT):
                v.tensor_tensor(k.hT[:, j, :], k.xT[:, j, :], rstd[:, :], ALU.mult).then_inc(normed, 1)
            v.wait_ge(normed, KT)
            scale = k.mod[:, (slot + 1) * KT:(slot + 2) * KT, 1:NSEQ]
            s = k.hT[:, :, SEQ:T].rearrange("p k (s l) -> p k s l", l=SL)
            st(v.tensor_tensor(s, s, bcast(scale.unsqueeze(3), KT, SB, SL), ALU.mult))
            v.tensor_tensor(s, s, bcast(k.mod[:, slot * KT:(slot + 1) * KT, 1:NSEQ].unsqueeze(3), KT, SB, SL), ALU.add)


def delta_project(k):
    nc, a, ps = k.nc, k.a, k.ps
    w = Area(k.work[:, :])
    k.qkv = w.take(DNC, T)
    k.work_after_qkv = w.at
    acc = w.take(2, T)
    tails = w.take(DNC, DNK * NSEQ)
    spare = Area(k.oT[:, 4:12, :].rearrange("p a b -> p (a b)"))
    ring = spare.take(2, KT, 256)
    cin = spare.take(2, DNK + T)
    cs = spare.take(2, SB, DNK + SL)
    sacc = spare.take(2, SB, SL)
    taps = spare.take((DNK + 1) * DNC)
    before = spare.take(DNC, SB, DNK)
    prev_in = w.take(D + 512)
    taps_in = prev_in[64:64 + 4 * DNC, 0:P]
    tails_rows = acc[:, :, :].rearrange("p a b -> p (a b)")[:, 0:DNC * P]
    win = a["w_in"][0].rearrange("(k p) n -> p k n", p=P)
    w_loaded = [k.sem(f"qkv_w_loaded{s}") for s in range(2)]
    filled = [k.sem(f"qkv_filled{u}") for u in range(2)]
    emptied = [k.sem(f"qkv_emptied{u}") for u in range(2)]
    conv_done = [k.sem(f"qkv_conv_done{u}") for u in range(2)]
    silu_done, dstep, astep = k.sem("qkv_silu_done"), k.sem("qkv_dve_step"), k.sem("qkv_act_step")
    st_loaded, st_turned, st_copied = k.sem("dn_state_loaded"), k.sem("dn_state_turned"), k.sem("dn_state_copied")
    tails_turned, tails_copied = k.sem("dn_tails_turned"), k.sem("dn_tails_copied")
    stored = k.sem("dn_conv_state_stored")
    act_passed = k.sem("qkv_act_passed")
    NBQ, NBZ = DNC // 2, 2

    def first_loads(sp):
        for s in range(2):
            sp.dma_start(ring[:, s], win[:, :, s * 256:(s + 1) * 256]).then_inc(w_loaded[s], 16)
        sp.dma_start(prev_in[0:SB * DNK, :], a["state_delta_conv"][0].rearrange("b r c -> (b r) c")).then_inc(st_loaded, 16)
        sp.dma_start(taps_in, a["dn_conv_w"][0].rearrange("w (t p) -> (w t) p", p=P)).then_inc(st_loaded, 16)

    norm(k, "mix", 0, first_loads)
    with nc.Block() as block:
        @block.sync
        def _(sp):
            with sp.Fori(0, (NBQ + NBZ) // 2 - 1) as i:
                for s in range(2):
                    sp.wait_ge(filled[1], i * 2 + (s + 1))
                    sp.dma_start(ring[:, s], win[:, :, bass.ds(i * 512 + (2 + s) * 256, 256)]).then_inc(w_loaded[s], 16)
            sp.wait_ge(tails_copied, 2)
            sp.dma_start(a["prompt_state_delta_conv"][0, 0], tails_rows[0:DNK, :]).then_inc(stored, 16)
            sp.dma_start(a["sample_state_delta_conv"][0].rearrange("b r c -> (b r) c"),
                         tails_rows[32:32 + SB * DNK, :]).then_inc(stored, 16)
            sp.wait_ge(stored, 32)

        @block.tensor
        def _(pe):
            pe.wait_ge(st_loaded, 32)
            for t in range(DNC):
                pe.transpose(ps[:, 6, t * SB * DNK:(t + 1) * SB * DNK], prev_in[0:SB * DNK, t * P:(t + 1) * P],
                             k.ident[0:SB * DNK, 0:SB * DNK])
            pe.transpose(ps[:, 7, 0:4 * DNC], taps_in, k.ident[64:64 + 4 * DNC, 64:64 + 4 * DNC]).then_inc(st_turned, 1)

            def block_of(i, s, b):
                pe.wait_ge(w_loaded[s], (i + 1) * 16)
                for u in range(2):
                    pe.wait_ge(emptied[u], b + 1)
                    for c in range(NCH):
                        for j in range(KT):
                            ins = pe.matmul(ps[:, 3 * u + c, 0:CW], ring[:, s, j, u * P:(u + 1) * P],
                                            k.hT[:, j, c * CW:(c + 1) * CW], start=(j == 0), stop=(j == KT - 1))
                    ins.then_inc(filled[u], 1)

            with pe.Fori(0, (NBQ + NBZ) // 2) as i:
                for s in range(2):
                    block_of(i, s, i * 2 + s)
            pe.wait_ge(conv_done[0], NBQ + 1)
            pe.wait_ge(conv_done[1], NBQ + 1)
            pe.wait_ge(emptied[0], NBQ + NBZ + 1)
            pe.wait_ge(emptied[1], NBQ + NBZ + 1)
            for t in range(DNC):
                pe.transpose(ps[0:DNK, t // 4, (t % 4) * P:(t % 4 + 1) * P], tails[:, t, 0:DNK], k.ident[:, :])
                ins = pe.transpose(ps[0:SB * DNK, 3 + t // 4, (t % 4) * P:(t % 4 + 1) * P], tails[:, t, DNK:DNK * NSEQ],
                                   k.ident[:, :])
            ins.then_inc(tails_turned, 1)

        @block.scalar
        def _(act):
            st = Steps(act, astep)
            act.sem_inc(silu_done, 2)
            for u in range(2):
                act.activation(cin[:, u, 0:DNK], k.ones[:, 0:DNK], ACT.Copy, scale=0.0).then_inc(emptied[u], 1)
            act.wait_ge(st_copied, 1)

            with act.Fori(0, NBQ) as i:
                for u in range(2):
                    act.wait_ge(filled[u], i + 1)
                    act.wait_ge(conv_done[u], i + 1)
                    act.activation(chunks(cin[:, u, DNK:DNK + T]), ps[:, 3 * u:3 * u + 3, 0:CW], ACT.Copy)
                    act.activation(cs[:, u, :, 0:DNK], before[:, bass.ds(i * 2 + u, 1), :, :].rearrange("p a s r -> p (a s) r"), ACT.Copy)
                    act.activation(cs[:, u, :, DNK:], ps[:, 3 * u + 2, CW - NS:CW].rearrange("p (s l) -> p s l", l=SL),
                                   ACT.Copy).then_inc(emptied[u], 1)
                for u in range(2):
                    wait_before_addressed(act, conv_done[u], i + 2, act_passed)
                    act.activation(k.qkv[:, bass.ds(i * 2 + u, 1), :].rearrange("p a t -> p (a t)"), acc[:, u, :], ACT.Silu)\
                       .then_inc(silu_done, 1)
            for b in range(NBZ):
                for u in range(2):
                    act.wait_ge(filled[u], NBQ + b + 1)
                    act.activation(chunks(k.oT[:, 2 * b + u, :]), ps[:, 3 * u:3 * u + 3, 0:CW], ACT.Silu)\
                       .then_inc(emptied[u], 1)
            act.wait_ge(tails_turned, 1)
            act.activation(tails_rows[0:DNK, :].rearrange("p (b n) -> p b n", n=512), ps[0:DNK, 0:3, :], ACT.Copy)\
               .then_inc(tails_copied, 1)

        @block.vector
        def _(v):
            st = Steps(v, dstep)
            v.wait_ge(st_turned, 1)
            v.tensor_copy(before[:, :, :, :].rearrange("p t s r -> p (t s r)"), ps[:, 6, 0:DNC * SB * DNK]).then_inc(st_copied, 1)
            st(v.tensor_copy(taps[:, :], ps[:, 7, 0:4 * DNC]))
            for u in range(2):
                v.sem_inc(conv_done[u], 1)
            with v.Fori(0, NBQ) as i:
                st.loop(i, 2 * DNK)
                for u in range(2):
                    v.wait_ge(emptied[u], i + 2)
                    v.wait_ge(silu_done, i * 2 + (u + 1))
                    for tap in range(DNK + 1):
                        f = taps[:, bass.ds(i * 2 + (tap * DNC + u), 1)]
                        x, y = cin[:, u, tap:tap + SEQ], acc[:, u, 0:SEQ]
                        xs, ys = cs[:, u, :, tap:tap + SL], samples(acc[:, u, :])
                        if tap == 0:
                            v.tensor_copy(tails[:, bass.ds(i * 2 + u, 1), 0:DNK].rearrange("p a r -> p (a r)"), cin[:, u, SEQ:SEQ + DNK])
                            v.tensor_copy(tails[:, bass.ds(i * 2 + u, 1), DNK:].rearrange("p a (s r) -> p (a s) r", r=DNK), cs[:, u, :, SL:])
                            v.tensor_scalar(y, x, f, None, ALU.mult)
                            st(v.tensor_scalar(ys, xs, f, None, ALU.mult))
                            continue
                        v.scalar_tensor_tensor(y, x, f, y, ALU.mult, ALU.add)
                        ins = v.scalar_tensor_tensor(ys, xs, f, ys, ALU.mult, ALU.add)
                        if tap < DNK:
                            st(ins)
                    ins.then_inc(conv_done[u], 1)
                st.end(NBQ)
            v.wait_ge(tails_turned, 1)
            v.wait_ge(silu_done, 2 * NBQ + 2)
            v.tensor_copy(tails_rows[32:32 + SB * DNK, :].rearrange("p (b n) -> p b n", n=512), ps[0:SB * DNK, 3:6, :])\
             .then_inc(tails_copied, 1)


OUTS = [("y_prompt", (1, SEQ, D)), ("y_sample", (SB, SL, D)),
        ("prompt_state_delta", (1, 1, H, P, P)), ("prompt_state_delta_conv", (1, 1, DNK, DNC * P)),
        ("prompt_state_gla", (1, 1, H, GDK, P)), ("prompt_state_conv", (1, 1, CFK, CFC * P)),
        ("sample_state_delta", (1, SB, H, P, P)), ("sample_state_delta_conv", (1, SB, DNK, DNC * P)),
        ("sample_state_gla", (1, SB, H, GDK, P)), ("sample_state_conv", (1, SB, CFK, CFC * P))]


def delta_rows(k):
    nc, a, ps = k.nc, k.a, k.ps
    w = Area(k.work[:, k.work_after_qkv:])
    k.rows, k.rows8 = w.take(T), w.take(T)
    k.delta_area = w
    t = Area(k.oT[:, 4:12, :].rearrange("p a b -> p (a b)"))
    sq = t.take(2, T)
    wsm = t.take(KT, 80)
    raw, x, e, g = t.take(T), t.take(T), t.take(T), t.take(T)
    head = t.take(4)
    G0, G1 = RG, RG + H
    w_loaded, zeroed = k.sem("rows_w_loaded"), k.sem("rows_zeroed")
    squared, summed, small = k.sem("qk_squared"), k.sem("qk_summed"), k.sem("rows_small_done")
    dve, act_done, dstep, astep = k.sem("rows_by_vector"), k.sem("rows_by_scalar"), k.sem("rows_dve_step"), k.sem("rows_act_step")
    win = a["w_in"][0].rearrange("(k p) n -> p k n", p=P)

    with nc.Block() as block:
        @block.gpsimd
        def _(gp):
            gp.memset(wsm[:, :, :], 0.0)
            gp.memset(k.rows[:, :], 0.0).then_inc(zeroed, 1)

        @block.sync
        def _(sp):
            sp.dma_start(head[G0:G1, 0:1], a["dn_dt_bias"].rearrange("a h -> h a")).then_inc(w_loaded, 16)
            sp.dma_start(head[G0:G1, 1:2], a["dn_A_log"].rearrange("a h -> h a")).then_inc(w_loaded, 16)
            sp.wait_ge(zeroed, 1)
            for at, c0, n in ((RB, COL["ba"], H), (RG, COL["ba"] + H, H), (RT, COL["glr"], 16)):
                sp.dma_start(wsm[:, :, at:at + n], win[:, :, c0:c0 + n]).then_inc(w_loaded, 16)

        @block.tensor
        def _(pe):
            for j in range(2 * H):
                pe.wait_ge(squared, j + 1)
                for c in range(NCH):
                    ins = pe.matmul(ps[0:8, 3 + c, 0:CW], k.unit8[:, j, :], sq[:, j % 2, c * CW:(c + 1) * CW],
                                    start=(j == 0), stop=(j == 2 * H - 1))
                ins.then_inc(summed, 1)
            pe.wait_ge(w_loaded, 80)
            for c in range(NCH):
                for j in range(KT):
                    ins = pe.matmul(ps[0:80, c, 0:CW], wsm[:, j, :], k.hT[:, j, c * CW:(c + 1) * CW],
                                    start=(j == 0), stop=(j == KT - 1))
            ins.then_inc(small, 1)

        @block.scalar
        def _(act):
            st = Steps(act, astep)
            for j in range(2 * H):
                if j >= 2:
                    act.wait_ge(summed, j - 1)
                act.activation(sq[:, j % 2, :], k.qkv[:, j, :], ACT.Square).then_inc(squared, 1)
            act.wait_ge(dve, 1)
            act.activation(k.rows8[0:8, :], k.rows8[0:8, :], ACT.Sqrt).then_inc(act_done, 1)
            act.wait_ge(small, 1)
            st(act.activation(chunks(raw[0:80, :]), ps[0:80, 0:3, 0:CW], ACT.Copy))
            act.wait_ge(zeroed, 1)
            act.activation(k.rows8[64:80, :], raw[64:80, :], ACT.Copy)
            act.activation(k.rows[RB:RB + H, :], raw[0:H, :], ACT.Sigmoid)
            act.activation(head[G0:G1, 2:3], head[G0:G1, 1:2], ACT.Exp).then_inc(act_done, 1)
            act.wait_ge(dve, 2)
            st(act.activation(e[G0:G1, :], e[G0:G1, :], ACT.Exp, scale=-1.0))
            act.activation(e[G0:G1, :], e[G0:G1, :], ACT.Ln, bias=1.0).then_inc(act_done, 1)
            act.wait_ge(dve, 3)
            act.activation(k.rows[RE:RE + H, :], k.rows[G0:G1, :], ACT.Exp).then_inc(act_done, 1)

        @block.vector
        def _(v):
            st = Steps(v, dstep)
            v.wait_ge(summed, 2 * H)
            v.tensor_scalar(chunks(k.rows8[0:8, :]), ps[0:8, 3:6, 0:CW], EPS, None, ALU.add).then_inc(dve, 1)
            v.wait_ge(act_done, 1)
            st(v.reciprocal(k.rows8[0:8, :], k.rows8[0:8, :]))
            v.tensor_scalar(k.rows8[0:H, :], k.rows8[0:H, :], float(P) ** -0.5, None, ALU.mult)
            v.wait_ge(act_done, 2)
            st(v.tensor_scalar(x[G0:G1, :], raw[G0:G1, :], head[G0:G1, 0:1], None, ALU.add))
            v.scalar_tensor_tensor(e[G0:G1, :], x[G0:G1, :], -1.0, x[G0:G1, :], ALU.mult, ALU.max).then_inc(dve, 1)
            v.wait_ge(act_done, 3)
            st(v.scalar_tensor_tensor(g[G0:G1, :], x[G0:G1, :], 0.0, e[G0:G1, :], ALU.max, ALU.add))
            st(v.tensor_scalar(g[G0:G1, :], g[G0:G1, :], head[G0:G1, 2:3], -1.0, ALU.mult, ALU.mult))
            v.tensor_tensor_scan(k.rows[G0:G1, :], k.carry[G0:G1, :], g[G0:G1, :], 0.0, ALU.mult, ALU.add).then_inc(dve, 1)
            v.wait_ge(dve, 3)
            G = k.rows[G0:G1, :]
            for src, dst, n, l in ((G[:, 0:SEQ], k.rows[RT:RT + H, 0:SEQ], NC, C), (G[:, SEQ:T], k.rows[RT:RT + H, SEQ:T], SB, SL)):
                src = src.rearrange("p (c l) -> p c l", l=l)
                dst = dst.rearrange("p (c l) -> p c l", l=l)
                v.tensor_tensor(dst, bcast(src[:, :, l - 1:l], n, l), src, ALU.subtract)


def delta_rule(k):
    nc, a, ps = k.nc, k.a, k.ps
    w = k.delta_area
    t = Area(k.oT[:, 4:12, :].rearrange("p a b -> p (a b)"))

    def take(*s):
        n = 1
        for x in s:
            n *= x
        return (t if t.at + n <= t.size else w).take(*s)

    stage = [take(3, C) for _ in range(H)]
    rb = [take(2, C) for _ in range(H)]
    XY = [take(2, C) for _ in range(H)]
    lv = [take(2, C) for _ in range(H)]
    dec, AT, MT, P1, vb, kbe, kd, nwT, vn, qe, S = ([take(C) for _ in range(H)] for _ in range(11))
    rst, tcol, ecol, bge = take(C), take(C), take(C), take(H)
    v_filled, v_drained, s_filled, s_drained = (k.sem("dr_" + x) for x in
                                                ("v_filled", "v_drained", "s_filled", "s_drained"))
    rows_staged, cols_exp, bge_ready = k.sem("dr_rows_staged"), k.sem("dr_cols_exp"), k.sem("dr_bge_ready")
    decay_ready, level_ready = k.sem("dr_decay_ready"), k.sem("dr_level_ready")
    vexp_ready, dstep, astep = k.sem("dr_vexp_ready"), k.sem("dr_dve_step"), k.sem("dr_act_step")
    s0_loaded = [k.sem(f"dr_s0_loaded{h}") for h in range(H)]
    s_stored = k.sem("dr_state_stored")
    act_passed, pe_passed = k.sem("dr_act_passed"), k.sem("dr_pe_passed")
    LS = 2
    VE, SE = H * (4 + LEVELS) + 1, H * (3 + LEVELS)

    class At:
        def __init__(self, i):
            self.i = i

        def v(self, e, h):
            return self.i * VE + (1 + H * e + h + 1 if e >= 0 else 1)

        def s(self, e, h):
            return self.i * SE + (H * (e - (e >= 2)) + h + 1)
    bankv = lambda h: ps[:, 2 * h, :]
    banks = lambda h: ps[:, 2 * h + 1, :]

    def columns(i):
        return bass.ds(i * C, C) if not isinstance(i, int) or i < NC else slice(SEQ, T)

    with nc.Block() as block:
        def pe_front(pe, i, n, levels):
            at = At(i)
            cols = columns(i)

            def v_free(e, h, wait=None):
                (wait or (lambda s, x: pe.wait_ge(s, x)))(v_drained, at.v(e - 1, h) + H if e > 0 or h == 0 and e == 0 else at.i * VE + (1 + h))

            def s_free(e, h):
                pe.wait_ge(s_drained, at.s(e - 1, h) + H if e > 0 else at.i * SE + (1 + h))

            pe.wait_ge(rows_staged, i + 1)
            pe.wait_ge(v_drained, at.i * VE + 1)
            pe.transpose(ps[0:n, 0, 0:P], rst[:, 0:n], k.ident[:, :]).then_inc(v_filled, 1)
            for h in range(H):
                v_free(0, h, lambda s, x: wait_before_addressed(pe, s, x, pe_passed))
                for m, x in enumerate((h, H + h)):
                    pe.matmul(bankv(h)[:, m * n:(m + 1) * n], k.pick8[0:8, x, :], k.rows8[0:8, cols], start=True, stop=True)
                pe.matmul(bankv(h)[:, 2 * n:3 * n], k.pick[:, 3 * h, :], k.rows[:, cols], start=True, stop=True)\
                  .then_inc(v_filled, 1)
                s_free(0, h)
                for m in range(2):
                    ins = pe.matmul(banks(h)[:, m * n:(m + 1) * n], k.pick[:, 3 * h + 1 + m, :], k.rows[:, cols],
                                    start=True, stop=True)
                ins.then_inc(s_filled, 1)
            for h in range(H):
                v_free(1, h)
                kT = stage[h][:, 1, 0:n]
                pe.matmul(bankv(h)[0:n, 0:n], kT, stage[h][:, 0, 0:n], start=True, stop=True)
                pe.matmul(bankv(h)[0:n, n:2 * n], kT, kT, start=True, stop=True).then_inc(v_filled, 1)
                s_free(1, h)
                pe.transpose(banks(h)[0:n, 0:P], kT, k.ident[:, :])
                pe.transpose(banks(h)[0:n, P:2 * P], stage[h][:, 2, 0:n], k.ident[:, :]).then_inc(s_filled, 1)
            for h in range(H):
                pe.wait_ge(level_ready, at.i * (H * LEVELS) + (h + 1))
                v_free(2, h)
                pe.transpose(bankv(h)[0:n, 0:n], lv[h][0:n, 0, 0:n], k.ident[0:n, 0:n]).then_inc(v_filled, 1)
            for l in range(1, levels):
                for h in range(H):
                    pe.wait_ge(level_ready, at.i * (H * LEVELS) + (H * l + h + 1))
                    v_free(2 + l, h)
                    s_free(2 + l, h)
                    pe.matmul(banks(h)[0:n, 0:n], lv[h][0:n, l % 2, 0:n], XY[h][0:n, 0, 0:n], start=True, stop=True)\
                      .then_inc(s_filled, 1)
                for h in range(H):
                    pe.wait_ge(s_drained, at.s(2 + l, h) + H)
                    if l < levels - 1:
                        pe.matmul(bankv(h)[0:n, 0:n], XY[h][0:n, 1, 0:n], P1[h][0:n, 0:n], start=True, stop=True)
                    pe.matmul(bankv(h)[0:n, n:2 * n], P1[h][0:n, 0:n], XY[h][0:n, 1, 0:n], start=True, stop=True)\
                      .then_inc(v_filled, 1)
            e = 2 + levels
            for h in range(H):
                v_free(e, h)
                s_free(e, h)
                pe.matmul(banks(h)[:, 0:n], kbe[h][0:n, :], XY[h][0:n, 1, 0:n], start=True, stop=True).then_inc(s_filled, 1)
            return at, e

        @block.tensor
        def _(pe):
            with pe.Fori(0, NC) as i:
                at, e = pe_front(pe, i, C, LEVELS)
                for h in range(H):
                    pe.wait_ge(s_drained, at.s(e, h) + H)
                    pe.matmul(bankv(h)[:, 0:C], XY[h][:, 1, :], vb[h][:, :], start=True, stop=False)
                    pe.matmul(bankv(h)[:, 0:C], nwT[h][:, :], S[h][:, :], start=False, stop=True).then_inc(v_filled, 1)
                for h in range(H):
                    pe.wait_ge(v_drained, at.v(e, h) + H)
                    pe.matmul(banks(h)[:, 0:C], S[h][:, :], qe[h][:, :], start=True, stop=False)
                    pe.matmul(banks(h)[:, 0:C], vn[h][:, :], AT[h][:, :], start=False, stop=True).then_inc(s_filled, 1)
                    pe.matmul(bankv(h)[:, 0:C], kd[h][:, :], vn[h][:, :], start=True, stop=True).then_inc(v_filled, 1)
            at, e = pe_front(pe, NC, NS, LS)
            for h in range(H):
                pe.wait_ge(s_drained, at.s(e, h) + H)
                pe.wait_ge(s0_loaded[h], 16)
                S0 = k.qkv[:, h, 0:SEQ].rearrange("p (b e) -> p b e", b=SB)
                pe.matmul(bankv(h)[:, 0:NS], vb[h][0:NS, :], XY[h][0:NS, 1, 0:NS], start=True, stop=False)
                for b in range(SB):
                    ins = pe.matmul(bankv(h)[:, b * SL:(b + 1) * SL], S0[:, b, :], nwT[h][:, b * SL:(b + 1) * SL],
                                    start=False, stop=(b == SB - 1))
                ins.then_inc(v_filled, 1)
            for h in range(H):
                pe.wait_ge(v_drained, at.v(e, h) + H)
                pe.transpose(banks(h)[0:NS, 0:P], nwT[h][:, 0:NS], k.ident[:, :]).then_inc(s_filled, 1)
            for h in range(H):
                pe.wait_ge(s_drained, at.s(e + 1, h) + H)
                S0 = k.qkv[:, h, 0:SEQ].rearrange("p (b e) -> p b e", b=SB)
                pe.matmul(bankv(h)[:, 0:NS], vn[h][0:NS, :], AT[h][0:NS, 0:NS], start=True, stop=False)
                for b in range(SB):
                    ins = pe.matmul(bankv(h)[:, b * SL:(b + 1) * SL], S0[:, b, :], qe[h][:, b * SL:(b + 1) * SL],
                                    start=False, stop=(b == SB - 1))
                ins.then_inc(v_filled, 1)
            for half in range(2):
                for h in range(H):
                    pe.wait_ge(vexp_ready, h + 1)
                    pe.wait_ge(v_drained, at.v(e + 1 + half, h) + H)
                    pe.matmul(bankv(h)[:, :], kd[h][0:NS, :], k.qkv[0:NS, H + h, half * 512:(half + 1) * 512],
                              start=True, stop=True).then_inc(v_filled, 1)

        def act_front(act, i, n, levels):
            at = At(i)
            cols = columns(i)
            act.wait_ge(v_drained, at.v(-1, 0) + H)
            act.activation(ecol[0:n, RG:RT + H], tcol[0:n, RG:RT + H], ACT.Exp).then_inc(cols_exp, 1)
            for h in range(H):
                src = k.qkv[:, 2 * H + h, cols]
                act.activation(stage[h][:, 2, 0:n], src, ACT.Copy)
                act.wait_ge(s_filled, at.s(0, h))
                act.activation(rb[h][:, :, 0:n], banks(h)[:, 0:2 * n].rearrange("p (a b) -> p a b", a=2), ACT.Copy)\
                   .then_inc(s_drained, 1)
            for h in range(H):
                act.wait_ge(v_drained, at.v(0, h) + H)
                act.activation(dec[h][0:n, 0:n], dec[h][0:n, 0:n], ACT.Exp).then_inc(decay_ready, 1)
            act.wait_ge(bge_ready, i + 1)
            for h in range(H):
                act.wait_ge(s_filled, at.s(1, h))
                act.activation(vb[h][0:n, :], banks(h)[0:n, P:2 * P], ACT.Copy, scale=tcol[0:n, RB + h:RB + h + 1])
                act.activation(kbe[h][0:n, :], banks(h)[0:n, 0:P], ACT.Copy, scale=bge[0:n, h:h + 1])
                act.activation(kd[h][0:n, :], banks(h)[0:n, 0:P], ACT.Copy, scale=ecol[0:n, RT + h:RT + h + 1])\
                   .then_inc(s_drained, 1)
            for l in range(1, levels):
                for h in range(H):
                    act.wait_ge(s_filled, at.s(2 + l, h))
                    act.activation(P1[h][0:n, 0:n], banks(h)[0:n, 0:n], ACT.Copy).then_inc(s_drained, 1)
            e = 2 + levels
            for h in range(H):
                act.wait_ge(s_filled, at.s(e, h))
                act.activation(nwT[h][:, 0:n], banks(h)[:, 0:n], ACT.Copy, scale=-1.0).then_inc(s_drained, 1)
            return at, e

        @block.scalar
        def _(act):
            act.sem_inc(s_drained, H)
            with act.Fori(0, NC) as i:
                at, e = act_front(act, i, C, LEVELS)
                for h in range(H):
                    wait_before_addressed(act, s_filled, at.s(e + 1, h), act_passed)
                    act.activation(k.qkv[:, 2 * H + h, columns(i)], banks(h)[:, 0:C], ACT.Copy).then_inc(s_drained, 1)
            at, e = act_front(act, NC, NS, LS)
            for h in range(H):
                act.wait_ge(s_filled, at.s(e + 1, h))
                act.activation(vn[h][0:NS, :], banks(h)[0:NS, 0:P], ACT.Copy).then_inc(s_drained, 1)

        def dve_front(v, st, i, n, levels):
            at = At(i)
            cols = columns(i)
            v.tensor_copy(rst[:, 0:n], k.rows[:, cols]).then_inc(rows_staged, 1)
            v.wait_ge(v_filled, at.v(-1, 0))
            v.tensor_copy(tcol[0:n, :], ps[0:n, 0, 0:P]).then_inc(v_drained, 1)
            v.wait_ge(cols_exp, i + 1)
            v.wait_ge(v_drained, at.v(-1, 0) + H)
            v.tensor_tensor(bge[0:n, :], tcol[0:n, RB:RB + H], ecol[0:n, RG:RG + H], ALU.mult).then_inc(bge_ready, 1)
            for h in range(H):
                v.wait_ge(v_filled, at.v(0, h))
                v.tensor_tensor(stage[h][:, 0:2, 0:n], k.qkv[:, h:h + 5:4, cols],
                                bankv(h)[:, 0:2 * n].rearrange("p (a b) -> p a b", a=2), ALU.mult)
                v.tensor_scalar(dec[h][0:n, 0:n], bankv(h)[0:n, 2 * n:3 * n], tcol[0:n, RG + h:RG + h + 1], 0.0,
                                ALU.subtract, ALU.min).then_inc(v_drained, 1)
            mask = k.causal[:, :] if n == C else k.causal_s[0:n, :]
            for h in range(H):
                v.wait_ge(decay_ready, at.i * H + (h + 1))
                st.done(v.tensor_tensor(dec[h][0:n, 0:n], dec[h][0:n, 0:n], mask, ALU.mult))
            st.wait()
            for h in range(H):
                v.wait_ge(v_filled, at.v(1, h))
                v.tensor_tensor(AT[h][0:n, 0:n], bankv(h)[0:n, 0:n], dec[h][0:n, 0:n], ALU.mult)
                v.tensor_tensor(MT[h][0:n, 0:n], bankv(h)[0:n, n:2 * n], dec[h][0:n, 0:n], ALU.mult).then_inc(v_drained, 1)
            v.wait_ge(v_drained, at.v(1, H - 1) + H)
            v.wait_ge(s_drained, at.s(0, H - 1) + H)
            for h in range(H):
                v.tensor_tensor(qe[h][:, 0:n], stage[h][:, 0, 0:n], rb[h][:, 1, 0:n], ALU.mult)
                st.done(v.tensor_tensor(MT[h][0:n, 0:n], MT[h][0:n, 0:n], rb[h][0:n, 0, 0:n], ALU.mult))
            st.wait()
            for l in range(levels + 1):
                if l < levels:
                    for h in range(H):
                        v.tensor_tensor(lv[h][0:n, l % 2, 0:n], MT[h][0:n, 0:n], k.pair[0:n, l, 0:n], ALU.mult)\
                         .then_inc(level_ready, 1)
                if l == 0:
                    for h in range(H):
                        v.wait_ge(level_ready, at.i * (H * LEVELS) + (h + 1))
                        st.done(v.tensor_tensor(XY[h][0:n, 1, 0:n], k.ident[0:n, 0:n], lv[h][0:n, 0, 0:n], ALU.subtract))
                elif l == 1:
                    st.wait()
                    for h in range(H):
                        v.wait_ge(v_filled, at.v(2, h))
                        v.tensor_tensor(XY[h][0:n, 0, 0:n], k.ident[0:n, 0:n], bankv(h)[0:n, 0:n], ALU.subtract)\
                         .then_inc(v_drained, 1)
                else:
                    for h in range(H):
                        v.wait_ge(v_filled, at.v(1 + l, h))
                        v.wait_ge(v_drained, at.v(l, h) + H)
                        lo = 0 if l < levels else 1
                        v.tensor_tensor(XY[h][0:n, lo:2, 0:n], XY[h][0:n, lo:2, 0:n],
                                        bankv(h)[0:n, lo * n:2 * n].rearrange("p (a b) -> p a b", b=n), ALU.subtract)\
                         .then_inc(v_drained, 1)
            return at, 2 + levels

        @block.vector
        def _(v):
            st = Steps(v, dstep)
            for h in range(H):
                v.memset(S[h][:, :], 0.0).then_inc(v_drained, 1)
            with v.Fori(0, NC) as i:
                st.loop(i, 3 * H)
                at, e = dve_front(v, st, i, C, LEVELS)
                st.end(NC)
                for h in range(H):
                    v.wait_ge(v_filled, at.v(e, h))
                    v.tensor_copy(vn[h][:, :], bankv(h)[:, 0:C]).then_inc(v_drained, 1)
                for h in range(H):
                    v.wait_ge(v_filled, at.v(e + 1, h))
                    v.scalar_tensor_tensor(S[h][:, :], S[h][:, :], rb[h][:, 1, C - 1:C], bankv(h)[:, 0:C],
                                           ALU.mult, ALU.add).then_inc(v_drained, 1)
            at, e = dve_front(v, st, NC, NS, LS)
            for h in range(H):
                v.wait_ge(v_filled, at.v(e, h))
                v.tensor_copy(nwT[h][:, 0:NS], bankv(h)[:, 0:NS]).then_inc(v_drained, 1)
            for h in range(H):
                v.wait_ge(s_drained, at.s(e + 1, h) + H)
                v.tensor_tensor(k.qkv[0:NS, H + h, 0:SEQ].rearrange("p (b e) -> p b e", b=SB),
                                bcast(vn[h][0:NS, :].unsqueeze(1), SB, P), bcast(k.inseq[0:NS, :].unsqueeze(2), SB, P),
                                ALU.mult).then_inc(vexp_ready, 1)
            for h in range(H):
                v.wait_ge(v_filled, at.v(e + 1, h))
                v.tensor_copy(k.qkv[:, 2 * H + h, SEQ:T], bankv(h)[:, 0:NS]).then_inc(v_drained, 1)
            for half in range(2):
                for h in range(H):
                    v.wait_ge(v_filled, at.v(e + 2 + half, h))
                    for b in range(4):
                        bb = 4 * half + b
                        S0 = k.qkv[:, h, bb * P:(bb + 1) * P]
                        ins = v.scalar_tensor_tensor(S0, S0, rb[h][:, 1, bb * SL + SL - 1:bb * SL + SL],
                                                     bankv(h)[:, b * P:(b + 1) * P], ALU.mult, ALU.add)
                    ins.then_inc(v_drained, 1)

        @block.sync
        def _(sp):
            for h in range(H):
                sp.wait_ge(v_drained, (NC - 1) * VE + (1 + H * 0 + h + 1) + H)
                sp.dma_start(k.qkv[:, h, 0:SEQ].rearrange("p (b e) -> p b e", b=SB),
                             a["state_delta"][0, :, h].rearrange("b d e -> d b e")).then_inc(s0_loaded[h], 16)
            for h in range(H):
                sp.wait_ge(v_drained, NC * VE + H)
                sp.dma_start(a["prompt_state_delta"][0, 0, h], S[h][:, :]).then_inc(s_stored, 16)
            for h in range(H):
                sp.wait_ge(v_drained, At(NC).v(7, h) + H)
                sp.dma_start(a["sample_state_delta"][0, :, h].rearrange("b d e -> d b e"),
                             k.qkv[:, h, 0:SEQ].rearrange("p (b e) -> p b e", b=SB)).then_inc(s_stored, 16)
            sp.wait_ge(s_stored, 16 * 2 * H)


def gated_norm(k, tag, src, dst, weight, area, first_loads=None):
    nc, ps = k.nc, k.ps
    sq, fac = area.take(2, T), area.take(T)
    squared, summed, spread = k.sem(tag + "_squared"), k.sem(tag + "_summed"), k.sem(tag + "_spread")
    by_act, by_dve, dstep = k.sem(tag + "_by_act"), k.sem(tag + "_by_dve"), k.sem(tag + "_dve_step")
    drained = k.sem(tag + "_drained")

    with nc.Block() as block:
        if first_loads:
            @block.sync
            def _(sp):
                first_loads(sp)

        @block.scalar
        def _(act):
            for h in range(H):
                if h >= 2:
                    act.wait_ge(summed, h - 1)
                act.activation(sq[:, h % 2, :], src[:, h, :], ACT.Square).then_inc(squared, 1)
            act.wait_ge(by_dve, 1)
            act.activation(fac[0:8, :], fac[0:8, :], ACT.Sqrt).then_inc(by_act, 1)

        @block.tensor
        def _(pe):
            for h in range(H):
                pe.wait_ge(squared, h + 1)
                for c in range(NCH):
                    ins = pe.matmul(ps[0:8, c, 0:CW], k.unit8[:, h, :], sq[:, h % 2, c * CW:(c + 1) * CW],
                                    start=(h == 0), stop=(h == H - 1))
                ins.then_inc(summed, 1)
            pe.wait_ge(by_dve, 2)
            for h in range(H):
                if h >= 2:
                    pe.wait_ge(drained, h - 1)
                for c in range(NCH):
                    ins = pe.matmul(ps[:, 3 * (h % 2) + c, 0:CW], k.pick8[0:8, h, :], fac[0:8, c * CW:(c + 1) * CW],
                                    start=True, stop=True)
                ins.then_inc(spread, 1)

        @block.vector
        def _(v):
            st = Steps(v, dstep)
            v.wait_ge(summed, H)
            v.tensor_scalar(chunks(fac[0:8, :]), ps[0:8, 0:3, 0:CW], 1.0 / P, EPS, ALU.mult, ALU.add).then_inc(by_dve, 1)
            v.wait_ge(by_act, 1)
            v.reciprocal(fac[0:8, :], fac[0:8, :]).then_inc(by_dve, 1)
            for h in range(H):
                v.wait_ge(spread, h + 1)
                v.scalar_tensor_tensor(chunks(src[:, h, :]), chunks(src[:, h, :]), weight,
                                       ps[:, 3 * (h % 2):3 * (h % 2) + 3, 0:CW], ALU.mult, ALU.mult).then_inc(drained, 1)
            v.wait_ge(drained, H)
            for h in range(H):
                v.tensor_tensor(dst[:, h, :], dst[:, h, :], src[:, h, :], ALU.mult)


def gla_project(k):
    nc, a, ps = k.nc, k.a, k.ps
    w = Area(k.work[:, :])
    low = k.rows8
    k.gla = w.take(8, T)
    w.take(k.work_after_qkv + 2 * T - w.at)
    k.bcum = k.oT[:, 8:10, :]
    lg, ab = w.take(T), w.take(T)
    ring = Area(k.work[:, 8 * T:k.work_after_qkv]).take(2, KT, 256)
    gw = w.take(256)
    win = a["w_in"][0].rearrange("(k p) n -> p k n", p=P)
    w_loaded = [k.sem(f"gla_w_loaded{s}") for s in range(2)]
    filled, drained = k.sem("gla_filled"), k.sem("gla_drained")
    gw_loaded, lg_done, by_dve, dstep, astep = (k.sem("gla_" + x) for x in ("gw_loaded", "lg_done", "by_dve", "dstep", "astep"))
    NB = 6

    with nc.Block() as block:
        @block.sync
        def _(sp):
            sp.dma_start(gw[64:80, :], a["gla_gate_w"][0]).then_inc(gw_loaded, 16)
            for b in range(NB):
                if b >= 2:
                    sp.wait_ge(filled, 2 * (b - 1))
                c0 = COL["gqk"] + b * 256
                sp.dma_start(ring[:, b % 2], win[:, :, c0:c0 + 256]).then_inc(w_loaded[b % 2], 16)

        @block.tensor
        def _(pe):
            for b in range(NB):
                pe.wait_ge(w_loaded[b % 2], 16 * (b // 2 + 1))
                for u in range(2):
                    f = 2 * b + u
                    if f >= 2:
                        pe.wait_ge(drained, f - 1)
                    for c in range(NCH):
                        for j in range(KT):
                            ins = pe.matmul(ps[:, 3 * u + c, 0:CW], ring[:, b % 2, j, u * P:(u + 1) * P],
                                            k.hT[:, j, c * CW:(c + 1) * CW], start=(j == 0), stop=(j == KT - 1))
                    ins.then_inc(filled, 1)
            pe.wait_ge(gw_loaded, 16)
            for u in range(2):
                f = 2 * NB + u
                pe.wait_ge(drained, f - 1)
                for c in range(NCH):
                    ins = pe.matmul(ps[:, 3 * u + c, 0:CW], gw[64:80, u * P:(u + 1) * P], low[64:80, c * CW:(c + 1) * CW],
                                    start=True, stop=True)
                ins.then_inc(filled, 1)

        @block.scalar
        def _(act):
            st = Steps(act, astep)
            for f in range(2 * NB):
                act.wait_ge(filled, f + 1)
                src = ps[:, 3 * (f % 2):3 * (f % 2) + 3, 0:CW]
                if f < 8:
                    act.activation(chunks(k.gla[:, f, :]), src, ACT.Copy, scale=GDK ** -0.5 if f < 2 else 1.0).then_inc(drained, 1)
                else:
                    act.activation(chunks(k.oT[:, f - 4, :]), src, ACT.Silu).then_inc(drained, 1)
            for u in range(2):
                act.wait_ge(filled, 2 * NB + u + 1)
                if u:
                    act.wait_ge(by_dve, 2)
                act.activation(chunks(lg), ps[:, 3 * u:3 * u + 3, 0:CW], ACT.Identity, bias=k.column("gla_gate_b", u))\
                   .then_inc(drained, 1)
                act.wait_ge(by_dve, 2 * u + 1)
                st(act.activation(ab[:, :], ab[:, :], ACT.Exp, scale=-1.0))
                act.activation(ab[:, :], ab[:, :], ACT.Ln, bias=1.0).then_inc(lg_done, 1)

        @block.vector
        def _(v):
            st = Steps(v, dstep)
            for u in range(2):
                v.wait_ge(drained, 2 * NB + u + 1)
                if u:
                    v.wait_ge(by_dve, 2)
                v.scalar_tensor_tensor(ab[:, :], lg[:, :], -1.0, lg[:, :], ALU.mult, ALU.max).then_inc(by_dve, 1)
                v.wait_ge(lg_done, u + 1)
                st(v.scalar_tensor_tensor(ab[:, :], lg[:, :], 0.0, ab[:, :], ALU.min, ALU.subtract))
                st(v.tensor_scalar(ab[:, :], ab[:, :], 1.0 / 16.0, None, ALU.mult))
                v.tensor_tensor_scan(k.bcum[:, u, :], k.carry[:, :], ab[:, :], 0.0, ALU.mult, ALU.add).then_inc(by_dve, 1)


def gla_rule(k):
    nc, a, ps = k.nc, k.a, k.ps
    w = Area(k.work[:, 8 * T:])
    t = Area(k.oT[:, 10:12, :].rearrange("p a b -> p (a b)"))
    pick_w, carry_w = Area(k.pick[:, :, :].rearrange("p a b -> p (a b)")), Area(k.carry[:, :])
    E = [[w.take(LEVELS + 2, C) for _ in range(2)], [w.take(LEVELS + 2, C), pick_w.take(LEVELS + 2, C)]]
    Kf = [w.take(LEVELS + 1, C) for _ in range(2)]
    Qf = [w.take(LEVELS + 1, C) for _ in range(2)]
    Qs = [[x[:, LEVELS, :] for x in Qf], [carry_w.take(C) for _ in range(2)]]
    raw = [w.take(2, C) for _ in range(2)]
    vst = [w.take(2, C) for _ in range(2)]
    kdv = [(w, pick_w)[p].take(3, P) for p in range(2)]
    S = [carry_w.take(2, P) for _ in range(2)]
    head_q, head_f = carry_w.take(H, NS), carry_w.take(H, NS)
    prod = [t.take(LEVELS + 1, C) for _ in range(2)]
    AT = [w.take(C) for _ in range(H)]
    L_filled, L_drained, T_filled, T_drained, O_filled, O_drained, S_filled, S_drained = (
        k.sem("gr_" + x) for x in ("levels_filled", "levels_drained", "turned_filled", "turned_drained",
                                   "out_filled", "out_drained", "state_filled", "state_drained"))
    diff_ready, exp_ready, kq_ready, staged, at_ready, vexp_ready = (
        k.sem("gr_" + x) for x in ("diff_ready", "exp_ready", "kq_ready", "staged", "at_ready", "vexp_ready"))
    astep, stored = k.sem("gr_act_step"), k.sem("gr_state_stored")
    s0_loaded = [k.sem(f"gr_s0_loaded{h}") for h in range(H)]
    shifted, act_passed = k.sem("gr_head_rows_shifted"), k.sem("gr_act_passed")
    S0 = [k.gla[0:GDK, h, 0:SEQ].rearrange("p (b e) -> p b e", b=SB) for h in range(H)]
    vexp = [x.rearrange("p a b -> p (a b)") for x in (Kf[0], Qf[0], Kf[1], Qf[1])]

    def columns(i):
        return bass.ds(i * C, C) if not isinstance(i, int) or i < NC else slice(SEQ, T)

    def level_bank(h, n):
        return ps[0:n, 2 * (h % 2):2 * (h % 2) + 2, :].rearrange("p a b -> p (a b)")

    with nc.Block() as block:
        def pe_front(pe, i, n, levels):
            for p in range(2):
                pe.wait_ge(kq_ready, 2 * i + p + 1)
                pe.wait_ge(staged, 2 * i + p + 1)
                for hh in range(2):
                    h, r = 2 * p + hh, slice(64 * hh, 64 * hh + 64)
                    pe.wait_ge(L_drained, 4 * i + h + 1)
                    out = level_bank(h, n)
                    for l in range(levels):
                        pe.matmul(out[:, l * n:(l + 1) * n], Kf[p][r, l, 0:n], Qf[p][r, l, 0:n], start=True, stop=True)
                    pe.matmul(out[:, levels * n:(levels + 1) * n], raw[p][r, 1, 0:n], raw[p][r, 0, 0:n],
                              start=True, stop=True).then_inc(L_filled, 1)
                pe.wait_ge(T_drained, 2 * i + p + 1)
                pe.transpose(ps[0:n, 4 + p, 0:P], Kf[p][:, LEVELS, 0:n], k.ident[:, :])
                for hh in range(2):
                    ins = pe.transpose(ps[0:n, 4 + p, (1 + hh) * P:(2 + hh) * P], vst[p][:, hh, 0:n], k.ident[:, :])
                ins.then_inc(T_filled, 1)
            pe.wait_ge(O_drained, i + 1)
            for p in range(2):
                pe.wait_ge(T_drained, 2 * i + p + 3)

        @block.tensor
        def _(pe):
            def chunk(i, u):
                pe_front(pe, i, C, LEVELS)
                pe.wait_ge(S_drained, i + 1)
                for h in range(H):
                    p, hh = divmod(h, 2)
                    pe.wait_ge(at_ready, 4 * i + h + 1)
                    pe.matmul(ps[:, 7, h * C:(h + 1) * C], S[p][:, hh, :], Qs[u][p], start=True, stop=False)
                    ins = pe.matmul(ps[:, 7, h * C:(h + 1) * C], kdv[p][:, 1 + hh, :], AT[h][:, :], start=False, stop=True)
                ins.then_inc(O_filled, 1)
                for p in range(2):
                    ins = pe.matmul(ps[:, 6, p * 256:(p + 1) * 256], kdv[p][:, 0, :],
                                    kdv[p][:, 1:3, :].rearrange("p a b -> p (a b)"), start=True, stop=True)
                ins.then_inc(S_filled, 1)
            with pe.Fori(0, NC // 2) as g:
                for u in range(2):
                    chunk(g * 2 + u, u)
            pe_front(pe, NC, NS, 2)
            pe.wait_ge(shifted, 1)
            for h in range(H):
                p, hh = divmod(h, 2)
                pe.wait_ge(s0_loaded[h], 16)
                pe.wait_ge(at_ready, 4 * NC + h + 1)
                out = ps[:, 7, h * NS:(h + 1) * NS]
                pe.matmul(out, kdv[p][0:NS, 1 + hh, :], AT[h][0:NS, 0:NS], start=True, stop=False)
                for b in range(SB):
                    ins = pe.matmul(out[:, b * SL:(b + 1) * SL], S0[h][:, b, :], head_q[0:GDK, h, b * SL:(b + 1) * SL],
                                    start=False, stop=(b == SB - 1))
            ins.then_inc(O_filled, 1)
            for n in range(2 * H):
                h, half = divmod(n, 2)
                p, hh = divmod(h, 2)
                pe.wait_ge(S_drained, NC + n + 1)
                pe.wait_ge(vexp_ready, h + 1)
                pe.matmul(ps[0:GDK, 6, :], kdv[p][0:NS, 0, GDK * hh:GDK * hh + GDK],
                          vexp[h][0:NS, half * 512:(half + 1) * 512], start=True, stop=True).then_inc(S_filled, 1)

        def act_stage(act, i, n, p):
            for m in range(2):
                act.activation(raw[p][:, m, 0:n], k.gla[:, 2 * m + p, columns(i)], ACT.Copy)
                ins = act.activation(vst[p][:, m, 0:n], k.gla[:, 4 + 2 * p + m, columns(i)], ACT.Copy)
            ins.then_inc(staged, 1)

        def act_exp(act, i, n, p, u):
            act.wait_ge(diff_ready, 2 * i + p + 1)
            act.activation(E[u][p][:, :, 0:n], E[u][p][:, :, 0:n], ACT.Abs).then_inc(astep, 1)
            act.wait_ge(astep, 2 * i + p + 1)
            act.activation(E[u][p][:, :, 0:n], E[u][p][:, :, 0:n], ACT.Exp, scale=-1.0).then_inc(exp_ready, 1)

        def act_turned(act, i, n, p):
            act.wait_ge(T_filled, 2 * i + p + 1)
            act.activation(kdv[p][0:n, :, :].rearrange("p a b -> p (a b)"), ps[0:n, 4 + p, 0:3 * P], ACT.Copy)\
               .then_inc(T_drained, 1)

        @block.scalar
        def _(act):
            act.sem_inc(T_drained, 2)
            act.sem_inc(O_drained, 1)
            for p in range(2):
                act_stage(act, 0, C, p)
                act_exp(act, 0, C, p, 0)

            def chunk(i, u, more):
                for p in range(2):
                    if more:
                        act_exp(act, i + 1, C, p, 1 - u)
                    act_turned(act, i, C, p)
                    if more:
                        act_stage(act, i + 1, C, p)
                wait_before_addressed(act, O_filled, i + 1, act_passed)
                act.activation(k.gla[:, 4:8, columns(i)], ps[:, 7, :].rearrange("p (h n) -> p h n", h=H), ACT.Copy)\
                   .then_inc(O_drained, 1)
            with act.Fori(0, NC // 2 - 1) as g:
                for u in range(2):
                    chunk(g * 2 + u, u, True)
            chunk(NC - 2, 0, True)
            chunk(NC - 1, 1, False)
            for p in range(2):
                act_stage(act, NC, NS, p)
            for p in range(2):
                act_exp(act, NC, NS, p, 0)
            for p in range(2):
                act_turned(act, NC, NS, p)
            for p in range(2):
                act.wait_ge(kq_ready, 2 * NC + p + 1)
                for hh in range(2):
                    act.activation(head_q[0:GDK, 2 * p + hh, :], Qf[p][64 * hh:64 * hh + 64, LEVELS, 0:NS], ACT.Copy)
                    ins = act.activation(head_f[0:GDK, 2 * p + hh, :], E[0][p][64 * hh:64 * hh + 64, LEVELS + 1, 0:NS], ACT.Copy)
            ins.then_inc(shifted, 1)
            act.wait_ge(O_filled, NC + 1)
            act.activation(k.gla[:, 4:8, SEQ:T], ps[:, 7, 0:H * NS].rearrange("p (h n) -> p h n", h=H), ACT.Copy)\
               .then_inc(O_drained, 1)

        def differences(v, i, n, levels, length, p, u):
            b, e = k.bcum[:, p, columns(i)], E[u][p]
            for l in range(levels):
                s = 1 << l
                bb = b.rearrange("p (m r) -> p m r", r=2 * s)
                v.tensor_tensor(e[:, l, 0:n].rearrange("p (m r) -> p m r", r=2 * s), bb,
                                bcast(bb[:, :, s - 1:s], n // (2 * s), 2 * s), ALU.subtract)
            for l in range(levels, LEVELS):
                if n < C:
                    v.memset(e[:, l, 0:n], 0.0)
            bb = b.rearrange("p (m r) -> p m r", r=length)
            v.tensor_copy(e[:, LEVELS + 1, 0:n], b)
            v.tensor_tensor(e[:, LEVELS, 0:n].rearrange("p (m r) -> p m r", r=length),
                            bcast(bb[:, :, length - 1:length], n // length, length), bb, ALU.subtract).then_inc(diff_ready, 1)

        def factored(v, i, n, p, u):
            v.wait_ge(exp_ready, 2 * i + p + 1)
            q, kk = k.gla[:, p, columns(i)], k.gla[:, 2 + p, columns(i)]
            v.tensor_tensor(Kf[p][:, :, 0:n], bcast(kk.unsqueeze(1), LEVELS + 1, n), E[u][p][:, 0:LEVELS + 1, 0:n], ALU.mult)
            v.tensor_tensor(Qs[u][p][:, 0:n], q, E[u][p][:, LEVELS + 1, 0:n], ALU.mult)
            v.tensor_tensor(Qf[p][:, 0:LEVELS, 0:n], bcast(q.unsqueeze(1), LEVELS, n), E[u][p][:, 0:LEVELS, 0:n], ALU.mult)\
             .then_inc(kq_ready, 1)

        def pair_products(v, i, n, levels, heads):
            for h in heads:
                v.wait_ge(L_filled, 4 * i + h + 1)
                out = level_bank(h, n)
                pr = prod[h % 2].rearrange("p a b -> p (a b)")[:, 0:(levels + 1) * n].rearrange("p (l n) -> p l n", n=n)
                o3 = out[:, 0:(levels + 1) * n].rearrange("p (l n) -> p l n", n=n)
                if levels == LEVELS:
                    v.tensor_tensor(pr[0:n], o3, k.pair[0:n, :, 0:n], ALU.mult).then_inc(L_drained, 1)
                else:
                    v.tensor_tensor(pr[0:n, 0:levels], o3[:, 0:levels], k.pair[0:n, 0:levels, 0:n], ALU.mult)
                    v.tensor_tensor(pr[0:n, levels], o3[:, levels], k.pair[0:n, LEVELS, 0:n], ALU.mult).then_inc(L_drained, 1)
                v.wait_ge(L_drained, 4 * i + h + 3)
                v.tensor_reduce(AT[h][0:n, 0:n], pr[0:n].rearrange("p l n -> p n l"), AX.X, ALU.add).then_inc(at_ready, 1)

        @block.vector
        def _(v):
            v.sem_inc(L_drained, 2)
            v.memset(S[0][:, :, :], 0.0)
            v.memset(S[1][:, :, :], 0.0).then_inc(S_drained, 1)
            for p in range(2):
                differences(v, 0, C, LEVELS, C, p, 0)

            for p in range(2):
                factored(v, 0, C, p, 0)

            def chunk(i, u, more):
                for p in range(2):
                    if more:
                        differences(v, i + 1, C, LEVELS, C, p, 1 - u)
                    pair_products(v, i, C, LEVELS, (2 * p, 2 * p + 1))
                for p in range(2):
                    if more:
                        v.wait_ge(T_filled, 2 * i + p + 1)
                        factored(v, i + 1, C, p, 1 - u)
                v.wait_ge(S_filled, i + 1)
                for p in range(2):
                    for hh in range(2):
                        r = slice(64 * hh, 64 * hh + 64)
                        ins = v.scalar_tensor_tensor(S[p][r, hh, :], S[p][r, hh, :], E[u][p][r, LEVELS + 1, C - 1:C],
                                                     ps[r, 6, p * 256 + hh * P:p * 256 + (hh + 1) * P], ALU.mult, ALU.add)
                ins.then_inc(S_drained, 1)
                v.wait_ge(S_drained, i + 2)
            with v.Fori(0, NC // 2 - 1) as g:
                for u in range(2):
                    chunk(g * 2 + u, u, True)
            chunk(NC - 2, 0, True)
            chunk(NC - 1, 1, False)
            for p in range(2):
                differences(v, NC, NS, 2, SL, p, 0)
            for p in range(2):
                factored(v, NC, NS, p, 0)
            pair_products(v, NC, NS, 2, range(H))
            for h in range(H):
                p, hh = divmod(h, 2)
                if h == 0:
                    v.wait_ge(shifted, 1)
                v.wait_ge(T_drained, 2 * NC + p + 3)
                v.tensor_tensor(vexp[h][0:NS, :].rearrange("p (b e) -> p b e", b=SB),
                                bcast(kdv[p][0:NS, 1 + hh, :].unsqueeze(1), SB, P),
                                bcast(k.inseq[0:NS, :].unsqueeze(2), SB, P), ALU.mult).then_inc(vexp_ready, 1)
            for n in range(2 * H):
                h, half = divmod(n, 2)
                v.wait_ge(S_filled, NC + n + 1)
                for b in range(4):
                    bb = 4 * half + b
                    ins = v.scalar_tensor_tensor(S0[h][:, bb, :], S0[h][:, bb, :],
                                                 head_f[0:GDK, h, bb * SL + SL - 1:bb * SL + SL],
                                                 ps[0:GDK, 6, b * P:(b + 1) * P], ALU.mult, ALU.add)
                ins.then_inc(S_drained, 1)

        @block.sync
        def _(sp):
            sp.wait_ge(L_filled, 4 * NC)
            for h in range(H):
                sp.dma_start(S0[h], a["state_gla"][0, :, h].rearrange("b d e -> d b e")).then_inc(s0_loaded[h], 16)
            sp.wait_ge(S_drained, NC + 1)
            for h in range(H):
                r = slice(64 * (h % 2), 64 * (h % 2) + 64)
                sp.dma_start(a["prompt_state_gla"][0, 0, h], S[h // 2][r, h % 2, :]).then_inc(stored, 16)
            sp.wait_ge(S_drained, NC + 1 + 2 * H)
            for h in range(H):
                sp.dma_start(a["sample_state_gla"][0, :, h].rearrange("b d e -> d b e"), S0[h]).then_inc(stored, 16)
            sp.wait_ge(stored, 16 * 2 * H)


def conformer_and_merge(k):
    nc, a, ps = k.nc, k.a, k.ps
    w = Area(k.work[:, :])
    k.merged = w.take(KT, T)
    ring_g, ring_v, sig = w.take(2, KT, P), w.take(2, KT, P), w.take(2, T)
    once = w.at
    cin, cs, before = w.take(CFK + T), w.take(SB, CFK + SL), w.take(CFC, SB * CFK)
    taps, tails, last = w.take(CFK + 1, CFC), w.take(CFC, CFK + NS), w.take(CFC * P)
    norm_w = Area(k.work[:, once:w.at])
    mean, sq = norm_w.take(T), norm_w.take(T)
    assert norm_w.at <= CFK + T + SB * (CFK + SL) + CFC * SB * CFK
    rstd = mean
    first = Area(k.work[:, once:])
    prev_in, taps_in = first.take(2, CFC * P), first.take(P)
    assert first.at <= CFK + T + SB * (CFK + SL)
    HR = SB // 2 * CFK
    y = k.oT[:, 8:12, :]
    win = a["w_in"][0].rearrange("(k p) n -> p k n", p=P)
    wb = a["w_branch"][0].rearrange("n (k p) c -> n p k c", p=P)
    ITEMS = []
    for j in range(CFC):
        ITEMS += [("glu", j, 0)] + [("merge", 2 * j + m, n) for m in range(2) for n in range(2)]
    NI = len(ITEMS)
    w_loaded = [k.sem(f"cm_w_loaded{s}") for s in range(2)]
    st_loaded, st_turned, st_copied = k.sem("cm_state_loaded"), k.sem("cm_state_turned"), k.sem("cm_state_copied")
    g_filled, v_filled, sig_done, v_drained, item_done = (
        k.sem("cm_" + x) for x in ("gate_filled", "value_filled", "sig_done", "value_drained", "item_done"))
    conv_done, tails_turned, tails_copied, last_stored, summed, squared, normed = (
        k.sem("cm_" + x) for x in ("conv_done", "tails_turned", "tails_copied", "last_stored", "summed", "squared", "normed"))
    by_dve, by_act, dstep, stored = (k.sem("cm_" + x) for x in ("by_dve", "by_act", "dve_step", "stored"))
    k.out_ring = Area(k.oT[:, 0:4, :].rearrange("p a b -> p (a b)")).take(2, KT, 256)
    k.out_loaded = [k.sem(f"po_w_loaded{s}") for s in range(2)]

    def load_merge(sp, q, m, n):
        s = q % 2
        sp.dma_start(ring_g[:, s], win[:, :, bass.ds(m * P + (COL["br"] + n * D), P)]).then_inc(w_loaded[s], 16)
        sp.dma_start(ring_v[:, s, 0:4], wb[n][:, :, bass.ds(m * P, P)]).then_inc(w_loaded[s], 16)

    def load_item(sp, q):
        kind, x, n = ITEMS[q]
        if kind == "merge":
            load_merge(sp, q, x, n)
            return
        for ring, c0 in ((ring_g, CFC * P), (ring_v, 0)):
            c0 += COL["conf"] + x * P
            sp.dma_start(ring[:, q % 2], win[:, :, c0:c0 + P]).then_inc(w_loaded[q % 2], 16)

    def first_loads(sp):
        rows = a["state_conv"][0].rearrange("b r c -> (b r) c")
        for m in range(2):
            sp.dma_start(prev_in[0:HR, m, :], rows[m * HR:(m + 1) * HR]).then_inc(st_loaded, 16)
        sp.dma_start(taps_in[0:(CFK + 1) * CFC, :], a["conf_dw_w"][0].rearrange("w (t p) -> (w t) p", p=P)).then_inc(st_loaded, 16)
        load_item(sp, 0)
        load_item(sp, 1)

    gated_norm(k, "gn", k.gla[:, 4:8, :], k.oT[:, 4:8, :], k.column("gla_norm_w"), Area(k.work[:, 0:4 * T]), first_loads)

    with nc.Block() as block:
        @block.sync
        def _(sp):
            for q in range(2, NI):
                sp.wait_ge(v_filled, q - 1)
                load_item(sp, q)
            sp.dma_start(a["sample_state_conv"][0, :, 0:CFK - SL, :], a["state_conv"][0, :, SL:CFK, :]).then_inc(stored, 16)
            for m in range(2):
                sp.wait_ge(v_filled, NI + m - 1)
                load_merge(sp, m, m, 2)
            sp.wait_ge(tails_copied, 1)
            sp.dma_start(a["prompt_state_conv"][0, 0], last[0:CFK, :]).then_inc(last_stored, 16)
            with sp.Fori(0, KT // 2 - 1) as i:
                for s in range(2):
                    sp.wait_ge(v_filled, i * 2 + (NI + 1 + s))
                    load_merge(sp, s, i * 2 + (2 + s), 2)
            for b in range(2):
                load_out(k, sp, b)
            sp.wait_ge(tails_copied, 2)
            for b in range(SB):
                sp.dma_start(a["sample_state_conv"][0, b, CFK - SL:CFK, :], last[b * SL:(b + 1) * SL, :]).then_inc(stored, 16)
            sp.wait_ge(stored, 16 * (1 + SB))

        @block.tensor
        def _(pe):
            def gate(s, wait_drained):
                if wait_drained is not None:
                    pe.wait_ge(sig_done, wait_drained)
                for c in range(NCH):
                    for j in range(KT):
                        ins = pe.matmul(ps[:, c, 0:CW], ring_g[:, s, j, :], k.hT[:, j, c * CW:(c + 1) * CW],
                                        start=(j == 0), stop=(j == KT - 1))
                ins.then_inc(g_filled, 1)

            def value(s, wait_drained, src, tiles):
                if wait_drained is not None:
                    pe.wait_ge(v_drained, wait_drained)
                for c in range(NCH):
                    for j in range(tiles):
                        ins = pe.matmul(ps[:, 3 + c, 0:CW], ring_v[:, s, j, :], src[:, j, c * CW:(c + 1) * CW],
                                        start=(j == 0), stop=(j == tiles - 1))
                ins.then_inc(v_filled, 1)

            pe.wait_ge(st_loaded, 48)
            for m in range(2):
                for t in range(CFC):
                    pe.transpose(ps[:, 6 + m, t * HR:(t + 1) * HR], prev_in[0:HR, m, t * P:(t + 1) * P], k.ident[0:HR, 0:HR])
            n = (CFK + 1) * CFC
            pe.transpose(ps[:, 0, 0:n], taps_in[0:n, :], k.ident[0:n, 0:n]).then_inc(st_turned, 1)
            pe.wait_ge(st_copied, 1)
            for q, (kind, x, n) in enumerate(ITEMS):
                pe.wait_ge(w_loaded[q % 2], 32 * (q // 2 + 1))
                gate(q % 2, q or None)
                value(q % 2, q or None, k.hT[:, :, :] if kind == "glu" else k.oT[:, 4 * n:4 * n + 4, :], KT if kind == "glu" else 4)
            pe.wait_ge(sig_done, NI)
            for t in range(CFC):
                pe.wait_ge(conv_done, t + 1)
                for c in range(NCH):
                    ins = pe.matmul(ps[:, c, 0:CW], k.ones[:, :], y[:, t, c * CW:(c + 1) * CW], start=(t == 0), stop=(t == CFC - 1))
            ins.then_inc(summed, 1)
            for t in range(CFC):
                pe.transpose(ps[0:CFK, 6, t * P:(t + 1) * P], tails[:, t, 0:CFK], k.ident[:, :])
                ins = pe.transpose(ps[0:NS, 7, t * P:(t + 1) * P], tails[:, t, CFK:], k.ident[:, :])
            ins.then_inc(tails_turned, 1)
            pe.wait_ge(by_dve, 1)
            pe.wait_ge(w_loaded[0], 32 * (NI // 2 + 1))
            gate(0, None)
            pe.wait_ge(v_drained, NI)
            for t in range(CFC):
                pe.wait_ge(squared, t + 1)
                for c in range(NCH):
                    ins = pe.matmul(ps[:, 3 + c, 0:CW], k.ones[:, :], sq[:, c * CW:(c + 1) * CW], start=(t == 0), stop=(t == CFC - 1))
                ins.then_inc(summed, 1)
            pe.wait_ge(w_loaded[1], 32 * (NI // 2 + 1))
            gate(1, NI + 1)
            pe.wait_ge(normed, CFC)
            value(0, None, y, 4)
            value(1, NI + 1, y, 4)
            with pe.Fori(0, KT // 2 - 1) as i:
                for s in range(2):
                    pe.wait_ge(w_loaded[s], i * 32 + 32 * (NI // 2 + 2))
                    gate(s, i * 2 + (NI + 2 + s))
                    value(s, i * 2 + (NI + 2 + s), y, 4)

        @block.scalar
        def _(act):
            def sigmoid(s, q):
                act.wait_ge(g_filled, q + 1)
                if not (isinstance(q, int) and q < 2):
                    act.wait_ge(item_done, q - 1)
                act.activation(chunks(sig[:, s, :]), ps[:, 0:3, 0:CW], ACT.Sigmoid).then_inc(sig_done, 1)
            for q in range(NI):
                sigmoid(q % 2, q)
            act.wait_ge(tails_turned, 1)
            act.activation(last[0:CFK, :], ps[0:CFK, 6, :], ACT.Copy).then_inc(tails_copied, 1)
            for t in range(CFC):
                act.wait_ge(by_dve, 1 + t + 1)
                if t:
                    act.wait_ge(summed, 1 + t)
                act.activation(sq[:, :], y[:, t, :], ACT.Square).then_inc(squared, 1)
                if t == 0:
                    sigmoid(0, NI)
            act.wait_ge(by_dve, 2 + CFC)
            act.activation(rstd[:, :], rstd[:, :], ACT.Sqrt).then_inc(by_act, 1)
            for t in range(CFC):
                act.wait_ge(by_dve, 3 + CFC + t)
                act.activation(y[:, t, :], y[:, t, :], ACT.Silu, bias=k.column("conf_ln_b", t), scale=k.column("conf_ln_w", t))\
                   .then_inc(normed, 1)
            sigmoid(1, NI + 1)
            act.wait_ge(last_stored, 16)
            act.activation(last[0:NS, :], ps[0:NS, 7, :], ACT.Copy).then_inc(tails_copied, 1)
            with act.Fori(0, KT // 2 - 1) as i:
                for s in range(2):
                    sigmoid(s, i * 2 + (NI + 2 + s))

        @block.vector
        def _(v):
            st = Steps(v, dstep)

            def merge_item(s, q, out, start):
                v.wait_ge(v_filled, q + 1)
                v.wait_ge(sig_done, q + 1)
                if start:
                    v.tensor_tensor(chunks(out), ps[:, 3:6, 0:CW], chunks(sig[:, s, :]), ALU.mult).then_inc(v_drained, 1)
                    v.wait_ge(v_drained, q + 1)
                    v.sem_inc(item_done, 1)
                    return
                v.tensor_tensor(chunks(sig[:, s, :]), ps[:, 3:6, 0:CW], chunks(sig[:, s, :]), ALU.mult).then_inc(v_drained, 1)
                v.wait_ge(v_drained, q + 1)
                v.tensor_tensor(out, out, sig[:, s, :], ALU.add).then_inc(item_done, 1)

            v.wait_ge(st_turned, 1)
            for m in range(2):
                v.tensor_copy(before[:, :, m * HR:(m + 1) * HR], ps[:, 6 + m, 0:CFC * HR].rearrange("p (t r) -> p t r", t=CFC))
            v.tensor_copy(taps[:, :, :].rearrange("p a b -> p (a b)"), ps[:, 0, 0:(CFK + 1) * CFC]).then_inc(st_copied, 1)
            st(v.memset(cin[:, 0:CFK], 0.0))
            v.wait_ge(st_copied, 1)
            for q, (kind, x, n) in enumerate(ITEMS):
                if kind == "merge":
                    merge_item(q % 2, q, k.merged[:, x, :], n == 0)
                else:
                    j = x
                    v.wait_ge(v_filled, q + 1)
                    v.wait_ge(sig_done, q + 1)
                    v.tensor_tensor(chunks(cin[:, CFK:]), ps[:, 3:6, 0:CW], chunks(sig[:, q % 2, :]), ALU.mult).then_inc(v_drained, 1)
                    v.wait_ge(v_drained, q + 1)
                    v.sem_inc(item_done, 1)
                    v.tensor_copy(cs[:, :, 0:CFK], before[:, j, :].rearrange("p (b r) -> p b r", b=SB))
                    v.tensor_copy(tails[:, j, 0:CFK], cin[:, SEQ:SEQ + CFK])
                    v.tensor_copy(tails[:, j, CFK:], cin[:, CFK + SEQ:CFK + T])
                    st(v.tensor_copy(cs[:, :, CFK:], cin[:, CFK + SEQ:CFK + T].rearrange("p (b r) -> p b r", b=SB)))
                part = q % 5
                for tap in range(*((0, 11), (11, 21), (21, CFK + 1), (0, 0), (0, 0))[part]):
                    f = taps[:, tap, j:j + 1]
                    x_in, o = cin[:, tap:tap + SEQ], y[:, j, 0:SEQ]
                    xs, os = cs[:, :, tap:tap + SL], samples(y[:, j, :])
                    if tap == 0:
                        v.tensor_scalar(o, x_in, f, k.column("conf_dw_b", j), ALU.mult, ALU.add)
                        ins = v.tensor_scalar(os, xs, f, k.column("conf_dw_b", j), ALU.mult, ALU.add)
                    else:
                        v.scalar_tensor_tensor(o, x_in, f, o, ALU.mult, ALU.add)
                        ins = v.scalar_tensor_tensor(os, xs, f, os, ALU.mult, ALU.add)
                    if tap < CFK:
                        st(ins)
                    else:
                        ins.then_inc(conv_done, 1)
                        v.wait_ge(conv_done, j + 1)
            v.wait_ge(summed, 1)
            v.tensor_scalar(chunks(mean), ps[:, 0:3, 0:CW], 1.0 / (CFC * P), None, ALU.mult).then_inc(by_dve, 1)
            v.wait_ge(by_dve, 1)
            for t in range(CFC):
                v.tensor_tensor(y[:, t, :], y[:, t, :], mean[:, :], ALU.subtract).then_inc(by_dve, 1)
            v.wait_ge(by_dve, 1 + CFC)
            v.wait_ge(summed, 1 + CFC)
            v.tensor_scalar(chunks(rstd), ps[:, 3:6, 0:CW], 1.0 / (CFC * P), EPS, ALU.mult, ALU.add).then_inc(by_dve, 1)
            v.wait_ge(by_act, 1)
            st(v.reciprocal(rstd[:, :], rstd[:, :]))
            for t in range(CFC):
                v.tensor_tensor(y[:, t, :], y[:, t, :], rstd[:, :], ALU.mult).then_inc(by_dve, 1)
            for m in range(2):
                merge_item(m, NI + m, k.merged[:, m, :], False)
            with v.Fori(0, KT // 2 - 1) as i:
                for s in range(2):
                    merge_item(s, i * 2 + (NI + 2 + s), k.merged[:, bass.ds(i * 2 + (2 + s), 1), :].rearrange("p a t -> p (a t)"), False)


def add_gated(v, k, m, slot, src):
    gate = k.mod[:, slot * KT + m, :]
    x = k.xT[:, m, :]
    tmp = k.gate_tmp
    n = SEQ - 2 * CW
    v.scalar_tensor_tensor(x[:, 0:2 * CW].rearrange("p (c w) -> p c w", c=2), src[:, 0:2, 0:CW], gate[:, 0:1],
                           x[:, 0:2 * CW].rearrange("p (c w) -> p c w", c=2), ALU.mult, ALU.add)
    v.scalar_tensor_tensor(x[:, 2 * CW:SEQ], src[:, 2, 0:n], gate[:, 0:1], x[:, 2 * CW:SEQ], ALU.mult, ALU.add)
    return v.tensor_tensor(tmp[:, m, :, :], src[:, 2, n:CW].rearrange("p (s l) -> p s l", l=SL),
                           bcast(gate[:, 1:NSEQ].unsqueeze(2), SB, SL), ALU.mult)


def load_out(k, sp, b):
    wo = k.a["w_out"][0].rearrange("(k p) n -> p k n", p=P)
    sp.dma_start(k.out_ring[:, b % 2], wo[:, :, b * 256:(b + 1) * 256]).then_inc(k.out_loaded[b % 2], 16)


def project_out(k):
    nc, ps = k.nc, k.ps
    w = Area(k.work[:, KT * T:])
    ring, w_loaded = k.out_ring, k.out_loaded
    k.gate_tmp = w.take(KT, SB, SL)
    filled, drained = k.sem("po_filled"), k.sem("po_drained")
    with nc.Block() as block:
        @block.sync
        def _(sp):
            for b in range(2, 4):
                sp.wait_ge(filled, 2 * (b - 1))
                load_out(k, sp, b)

        @block.tensor
        def _(pe):
            for m in range(KT):
                b, u = divmod(m, 2)
                pe.wait_ge(w_loaded[b % 2], 16 * (b // 2 + 1))
                if m >= 2:
                    pe.wait_ge(drained, m - 1)
                for c in range(NCH):
                    for j in range(KT):
                        ins = pe.matmul(ps[:, 3 * u + c, 0:CW], ring[:, b % 2, j, u * P:(u + 1) * P],
                                        k.merged[:, j, c * CW:(c + 1) * CW], start=(j == 0), stop=(j == KT - 1))
                ins.then_inc(filled, 1)

        @block.vector
        def _(v):
            for m in range(KT):
                v.wait_ge(filled, m + 1)
                add_gated(v, k, m, 2, ps[:, 3 * (m % 2):3 * (m % 2) + 3, :]).then_inc(drained, 1)
            v.wait_ge(drained, KT)
            for m in range(KT):
                s = samples(k.xT[:, m, :])
                v.tensor_tensor(s, s, k.gate_tmp[:, m], ALU.add)


NT = 9
NG, TOPG, EG, TOPK = 8, 4, 8, 8
NBLK = (E_N + (T * TOPK) // P + 1) // 2 * 2
assert NBLK * P >= T * TOPK and NBLK >= E_N + (T * TOPK - 1) // P
SLOT = 3 * KT * FF
NW = 3
RANGES = ((0, 3 * E_N // 2), (3 * E_N // 2, 7 * E_N // 4), (7 * E_N // 4, NBLK))
ROWS = T + P


def tokens_of(t):
    return P if t < 8 else NS


def plan_moe(k):
    k.ring = k.big[:, 0:NW * SLOT]
    w = Area(k.big[:, NW * SLOT:])
    k.token_idx = w.take(NBLK).bitcast(mybir.dt.int32)
    k.token_gate = w.take(NBLK)
    k.expert_tab = w.take(NBLK).bitcast(mybir.dt.int32)
    k.offset_tab = w.take(NBLK).bitcast(mybir.dt.int32)
    k.end_tab = w.take(E_N).bitcast(mybir.dt.int32)
    k.moe_rest = w.at
    k.u_rows = k.nc.dram_tensor("u_rows", (ROWS, D), F32, kind="Internal").ap()
    k.y_rows = k.nc.dram_tensor("y_rows", (ROWS, D), F32, kind="Internal").ap()


def route(k):
    nc, a, ps = k.nc, k.a, k.ps
    w = Area(k.ring[:, 0:2 * SLOT])
    gates = w.take(NT, E_N)
    rw, bias, brow = w.take(KT, E_N), w.take(E_N), w.take(E_N)
    s, sb, msk, sel = w.take(NT, E_N), w.take(NT, E_N), w.take(NT, E_N), w.take(NT, E_N)
    top2, grp = w.take(NT * NG, 8), w.take(NT, NG)
    gt, eq, before = w.take(NT, NG, NG), w.take(NT, NG, NG), w.take(NG, NG)
    rank, pen, top8, total = w.take(NT, NG), w.take(NT, NG), w.take(NT, 8), w.take(NT)
    prefix, cnt = w.take(NT + 1, E_N), w.take(E_N)
    nblk, bend, steps_row = w.take(E_N), w.take(E_N), w.take(E_N)
    place, slots, slot_gate = w.take(NT, E_N), w.take(NT, TOPK), w.take(NT, TOPK)
    slot_i, blk_i, lane_i = (w.take(NT, TOPK).bitcast(mybir.dt.int32) for _ in range(3))
    blk, lane = w.take(NT, TOPK), w.take(NT, TOPK)
    iota_i, iota_f = w.take(NBLK).bitcast(mybir.dt.int32), w.take(NBLK)
    tok_i, tok, empty = w.take(NT + 1).bitcast(mybir.dt.int32), w.take(NT + 1), w.take(NBLK)
    column, passed_end = w.take(2), w.take(NBLK)
    PW = TOPK * (P + 2 * NBLK)
    big = w.take(PW)
    tw = Area(k.big[:, NW * SLOT + k.moe_rest:])
    sg, su, hid = tw.take(T), tw.take(T), tw.take(2, T)
    rows = tw.take(2, D)
    match = big[:, 0:NT // 3 * TOPK * E_N].rearrange("p (t s e) -> p t s e", t=NT // 3, s=TOPK)
    logits_T = big[0:E_N, 0:T]
    at_lane, at_blk = [], []
    for place_w in (Area(big), Area(tw.take(PW))):
        at_lane.append(place_w.take(TOPK, P))
        at_blk.append(place_w.take(TOPK, 2, NBLK))
    sw = Area(k.ring[:, 2 * SLOT:3 * SLOT])
    wg, wu, wd = sw.take(KT, FF), sw.take(KT, FF), sw.take(2, D)
    zero = at_blk[1].rearrange("p s g n -> p (s g n)")[:, 0:D]

    names = ("logits_copied", "router_loaded", "shared_loaded", "logits", "scored", "bias_ready", "zeroed", "zeros_stored",
             "u_turned", "u_drained", "u_stored0", "u_stored1", "sh_filled", "sh_drained", "sh_hid_ready", "sel_ready", "counted",
             "column_ready", "column_turned", "steps_ready", "stepped", "lanes_ready", "placed", "route_step",
             "route_pool_step", "iota_ready")
    q = {n: k.sem("rt_" + n) for n in names}
    SH = [(n, f) for f in range(2) for n in "gu"] + [("d", m) for m in range(KT)]

    def first_loads(sp):
        sp.dma_start(rw[:, :, :], a["router_w"][0].rearrange("(k p) e -> p k e", p=P)).then_inc(q["router_loaded"], 16)
        sp.dma_start(brow[0:1, :], a["router_bias"]).then_inc(q["router_loaded"], 16)

    norm(k, "ffn", 3, first_loads)

    with nc.Block() as block:
        @block.sync
        def _(sp):
            sp.dma_start(wg[:, :, :], a["sh_w_gate"][0].rearrange("(k p) f -> p k f", p=P)).then_inc(q["shared_loaded"], 16)
            sp.dma_start(wu[:, :, :], a["sh_w_up"][0].rearrange("(k p) f -> p k f", p=P)).then_inc(q["shared_loaded"], 16)
            sp.dma_start(wd[:, :, :], a["sh_w_down"][0].rearrange("(k p) d -> p k d", p=P)).then_inc(q["shared_loaded"], 16)
            sp.wait_ge(q["zeroed"], 1)
            for t in range(8):
                sp.dma_start(k.y_rows[t * P:(t + 1) * P, :], zero[:, :]).then_inc(q["zeros_stored"], 16)
            sp.dma_start(k.y_rows[SEQ:T, :], zero[0:NS, :]).then_inc(q["zeros_stored"], 16)
            for rows_of in (k.y_rows, k.u_rows):
                sp.dma_start(rows_of[T:ROWS, :], zero[:, :]).then_inc(q["zeros_stored"], 16)
            for t in range(NT):
                n = tokens_of(t)
                sp.wait_ge(q["u_drained"], 2 * t + 2)
                sp.dma_start(k.u_rows[t * P:t * P + n, :], rows[0:n, t % 2, :]).then_inc(q[f"u_stored{t % 2}"], 16)
            sp.wait_ge(q["zeros_stored"], 16 * 11)
            sp.wait_ge(q["u_stored0"], 80)
            sp.wait_ge(q["u_stored1"], 64)

        @block.gpsimd
        def _(g):
            st = Steps(g, q["route_pool_step"])
            g.memset(zero[:, :], 0.0).then_inc(q["zeroed"], 1)
            g.iota(iota_i[:, :], pattern=[[1, NBLK]], base=0, channel_multiplier=0)
            g.iota(tok_i[:, 0:NT], pattern=[[P, NT]], base=1, channel_multiplier=1)
            g.iota(tok_i[:, NT:NT + 1], pattern=[[0, 1]], base=T + 1, channel_multiplier=1)
            st(g.memset(steps_row[0:1, :], float(SLOT)))
            g.tensor_copy(iota_f[:, :], iota_i[:, :])
            g.tensor_copy(tok[:, :], tok_i[:, :])
            g.memset(steps_row[0:1, NW - 1:E_N:NW], float(-(NW - 1) * SLOT)).then_inc(q["iota_ready"], 1)
            for f in range(2):
                g.wait_ge(q["sh_drained"], 2 * f + 2)
                g.tensor_tensor(hid[:, f, :], sg[:, :], su[:, :], ALU.mult).then_inc(q["sh_hid_ready"], 1)

        @block.tensor
        def _(pe):
            pe.wait_ge(q["router_loaded"], 32)
            for c in range(NCH):
                for j in range(KT):
                    ins = pe.matmul(ps[0:E_N, c, 0:CW], rw[:, j, :], k.hT[:, j, c * CW:(c + 1) * CW], start=(j == 0), stop=(j == KT - 1))
            ins.then_inc(q["logits"], 1)
            pe.matmul(ps[:, 7, E_N:2 * E_N], k.ones[0:1, :], brow[0:1, :], start=True, stop=True)
            pe.wait_ge(q["logits_copied"], 1)
            for t in range(NT):
                n = tokens_of(t)
                out = ps[0:n, 6, t * E_N:(t + 1) * E_N] if t < 8 else ps[0:n, 7, 0:E_N]
                ins = pe.transpose(out, logits_T[:, t * P:t * P + n], k.ident[0:E_N, 0:E_N])
            ins.then_inc(q["logits"], 1)
            for t in range(NT):
                n = tokens_of(t)
                for half in range(2):
                    if t >= 2:
                        pe.wait_ge(q["u_drained"], 2 * (t - 2) + half + 1)
                    for j in range(4):
                        ins = pe.transpose(ps[0:n, 2 * (t % 2) + half, j * P:(j + 1) * P],
                                           k.hT[:, 4 * half + j, t * P:t * P + n], k.ident[:, :])
                    ins.then_inc(q["u_turned"], 1)
            pe.wait_ge(q["shared_loaded"], 48)
            for i, (kind, x) in enumerate(SH):
                out = ps[:, 3 * (i % 2):3 * (i % 2) + 3, 0:CW]
                if i >= 2:
                    pe.wait_ge(q["sh_drained"], i - 1)
                else:
                    pe.wait_ge(q["u_drained"], 2 * NT)
                if kind == "d" and x == 0:
                    pe.wait_ge(q["sh_hid_ready"], 2)
                for c in range(NCH):
                    cc = slice(c * CW, (c + 1) * CW)
                    if kind in "gu":
                        ww = wg if kind == "g" else wu
                        for j in range(KT):
                            ins = pe.matmul(out[:, c, :], ww[:, j, x * P:(x + 1) * P], k.hT[:, j, cc],
                                            start=(j == 0), stop=(j == KT - 1))
                    else:
                        for j in range(2):
                            ins = pe.matmul(out[:, c, :], wd[:, j, x * P:(x + 1) * P], hid[:, j, cc],
                                            start=(j == 0), stop=(j == 1))
                ins.then_inc(q["sh_filled"], 1)
                if i == 0:
                    pe.wait_ge(q["sel_ready"], 1)
                    flat = lambda x: x.rearrange("p t e -> p (t e)")
                    pe.matmul(ps[:, 6, :], k.causal[:, :], flat(sel[:, 0:8, :]), start=True, stop=False)
                    pe.matmul(ps[:, 6, :], k.ones[:, :], flat(prefix[:, 0:8, :]), start=False, stop=True)
                    pe.matmul(ps[:, 7, 0:E_N], k.causal[:, :], sel[:, 8, :], start=True, stop=False)
                    pe.matmul(ps[:, 7, 0:E_N], k.ones[:, :], prefix[:, 8, :], start=False, stop=True)
                    pe.matmul(ps[:, 7, E_N:2 * E_N], k.ones[:, :], prefix[:, NT, :], start=True, stop=True).then_inc(q["counted"], 1)
                if i == 1:
                    pe.wait_ge(q["column_ready"], 1)
                    pe.wait_ge(q["iota_ready"], 1)
                    pe.matmul(ps[0:E_N, 7, 0:1], bend[0:1, :], k.ones[0:1, 0:1], start=True, stop=True)
                    pe.matmul(ps[0:E_N, 7, 1:2], steps_row[0:1, :], k.ones[0:1, 0:1], start=True, stop=True)\
                      .then_inc(q["column_turned"], 1)
                if i == 3:
                    pe.wait_ge(q["steps_ready"], 1)
                    pe.matmul(ps[0:1, 7, 0:NBLK], k.ones[0:E_N - 1, 0:1], passed_end[0:E_N - 1, :], start=True, stop=True)
                    pe.matmul(ps[0:1, 7, NBLK:2 * NBLK], column[0:E_N - 1, 1:2], passed_end[0:E_N - 1, :],
                              start=True, stop=True).then_inc(q["stepped"], 1)
                if i >= 3:
                    t = i - 3
                    pe.wait_ge(q["lanes_ready"], t + 1)
                    for n in range(TOPK):
                        ins = pe.matmul(ps[:, 6, 0:2 * NBLK], at_lane[t % 2][:, n, :],
                                        at_blk[t % 2][:, n, :, :].rearrange("p a b -> p (a b)"),
                                        start=(t == 0 and n == 0), stop=(t == NT - 1 and n == TOPK - 1))
                    ins.then_inc(q["placed"], 1)

        @block.scalar
        def _(act):
            act.wait_ge(q["bias_ready"], 1)
            act.wait_ge(q["logits"], 1)
            act.activation(chunks(logits_T), ps[0:E_N, 0:NCH, 0:CW], ACT.Copy).then_inc(q["logits_copied"], 1)
            act.wait_ge(q["logits"], 2)
            act.activation(bias[:, :], ps[:, 7, E_N:2 * E_N], ACT.Copy)
            act.activation(s[:, 0:8, :].rearrange("p t e -> p (t e)"), ps[:, 6, :], ACT.Sigmoid)
            act.activation(s[0:NS, 8, :], ps[0:NS, 7, 0:E_N], ACT.Sigmoid).then_inc(q["scored"], 1)
            for t in range(NT):
                n = tokens_of(t)
                for half in range(2):
                    act.wait_ge(q["u_turned"], 2 * t + half + 1)
                    if t >= 2:
                        act.wait_ge(q[f"u_stored{t % 2}"], 16 * (t // 2))
                    act.activation(rows[0:n, t % 2, half * 512:(half + 1) * 512], ps[0:n, 2 * (t % 2) + half, :],
                                   ACT.Copy).then_inc(q["u_drained"], 1)
            for i, (kind, x) in enumerate(SH):
                act.wait_ge(q["sh_filled"], i + 1)
                if kind in "gu" and x == 1:
                    act.wait_ge(q["sh_hid_ready"], 1)
                dst = {"g": sg, "u": su}[kind] if kind in "gu" else k.hT[:, x, :]
                act.activation(chunks(dst), ps[:, 3 * (i % 2):3 * (i % 2) + 3, 0:CW], ACT.Silu if kind == "g" else ACT.Copy)\
                   .then_inc(q["sh_drained"], 1)

        @block.vector
        def _(v):
            st = Steps(v, q["route_step"])
            v.memset(s[:, 8, :], 0.5).then_inc(q["bias_ready"], 1)
            st(v.memset(before[:, :, :], 0.0))
            for i in range(1, NG):
                v.memset(before[:, i, 0:i], 1.0)
            v.wait_ge(q["scored"], 1)
            st(v.tensor_tensor(sb[:, :, :], s[:, :, :], bcast(bias.unsqueeze(1), NT, E_N), ALU.add))
            for t in range(NT):
                for g in range(NG):
                    ins = v.max(top2[:, t * NG + g, :], sb[:, t, g * EG:(g + 1) * EG])
            st(ins)
            pair = top2.rearrange("p (t g) e -> p t g e", g=NG)
            st(v.tensor_tensor(grp[:, :, :], pair[:, :, :, 0], pair[:, :, :, 1], ALU.add))
            mine, other = bcast(grp.unsqueeze(3), NT, NG, NG), bcast(grp.unsqueeze(2), NT, NG, NG)
            v.tensor_tensor(gt[:, :, :, :], other, mine, ALU.is_gt)
            st(v.tensor_tensor(eq[:, :, :, :], other, mine, ALU.is_equal))
            st(v.tensor_tensor(eq[:, :, :, :], eq[:, :, :, :], bcast(before.unsqueeze(1), NT, NG, NG), ALU.mult))
            st(v.tensor_tensor(gt[:, :, :, :], gt[:, :, :, :], eq[:, :, :, :], ALU.add))
            st(v.tensor_reduce(rank[:, :, :], gt[:, :, :, :], AX.X, ALU.add))
            st(v.tensor_scalar(pen[:, :, :], rank[:, :, :], float(TOPG) - 0.5, -1e30, ALU.is_gt, ALU.mult))
            st(v.tensor_tensor(msk.rearrange("p t (g e) -> p t g e", g=NG), sb.rearrange("p t (g e) -> p t g e", g=NG),
                               bcast(pen.unsqueeze(3), NT, NG, EG), ALU.add))
            for t in range(NT):
                ins = v.max(top8[:, t, :], msk[:, t, :])
            st(ins)
            for t in range(NT):
                ins = v.match_replace(out=sel[:, t, :], in_to_replace=top8[:, t, :], in_values=msk[:, t, :], imm_value=-3e38)
            st(ins)
            st(v.tensor_tensor(sel[:, :, :], sel[:, :, :], msk[:, :, :], ALU.not_equal))
            v.memset(sel[NS:2 * NS, 8, :], 0.0)
            st(v.memset(sel[2 * NS:P, 8, :], 0.0))
            st(v.memset(prefix[:, 0, :], 0.0))
            for t in range(NT):
                st(v.tensor_tensor(prefix[:, t + 1, :], prefix[:, t, :], sel[:, t, :], ALU.add))
            v.sem_inc(q["sel_ready"], 1)
            st(v.tensor_tensor(gates[:, :, :], s[:, :, :], sel[:, :, :], ALU.mult))
            st(v.tensor_reduce(total[:, 0:8], gates[:, 0:8, :], AX.X, ALU.add))
            st(v.memset(total[:, 8:9], 1.0))
            st(v.tensor_reduce(total[0:NS, 8:9], gates[0:NS, 8:9, :], AX.X, ALU.add))
            st(v.reciprocal(total[:, :], total[:, :]))
            st(v.tensor_scalar(total[:, :], total[:, :], 2.5, None, ALU.mult))
            st(v.tensor_tensor(gates[:, :, :], gates[:, :, :], bcast(total.unsqueeze(2), NT, E_N), ALU.mult))

            v.wait_ge(q["counted"], 1)
            st(v.tensor_copy(cnt[:, :], ps[:, 7, E_N:2 * E_N]))
            st(v.tensor_scalar(nblk[:, :], cnt[:, :], float(P), 1.0, ALU.is_gt, ALU.add))
            for n in range(2, -(-T // P)):
                st(v.scalar_tensor_tensor(nblk[:, :], cnt[:, :], float(n * P), nblk[:, :], ALU.is_gt, ALU.add))
            st(v.tensor_tensor_scan(bend[:, :], k.ones[:, 0:E_N], nblk[:, :], 0.0, ALU.mult, ALU.add))
            st(v.tensor_tensor(nblk[:, :], bend[:, :], nblk[:, :], ALU.subtract))
            st(v.tensor_scalar(nblk[:, :], nblk[:, :], float(P), None, ALU.mult))
            v.tensor_tensor(place[:, 0:8, :], ps[:, 6, :].rearrange("p (t e) -> p t e", e=E_N), bcast(nblk.unsqueeze(1), 8, E_N), ALU.add)
            st(v.tensor_tensor(place[:, 8, :], ps[:, 7, 0:E_N], nblk[:, :], ALU.add))
            st(v.tensor_tensor(place[:, :, :], place[:, :, :], sel[:, :, :], ALU.mult))
            v.sem_inc(q["column_ready"], 1)
            for t in range(NT):
                ins = v.max(slots[:, t, :], place[:, t, :])
            st(ins)
            st(v.tensor_scalar(slot_i[:, :, :], slots[:, :, :], -1.0, None, ALU.add))
            v.tensor_scalar(blk_i[:, :, :], slot_i[:, :, :], 7, None, ALU.arith_shift_right)
            st(v.tensor_scalar(lane_i[:, :, :], slot_i[:, :, :], P - 1, None, ALU.bitwise_and))
            v.tensor_copy(blk[:, :, :], blk_i[:, :, :])
            st(v.tensor_copy(lane[:, :, :], lane_i[:, :, :]))
            for t in range(0, NT, 3):
                st(v.tensor_tensor(match[:, :, :, :], bcast(slots[:, t:t + 3, :].unsqueeze(3), 3, TOPK, E_N),
                                   bcast(place[:, t:t + 3, :].unsqueeze(2), 3, TOPK, E_N), ALU.is_equal))
                st(v.tensor_tensor(match[:, :, :, :], match[:, :, :, :], bcast(gates[:, t:t + 3, :].unsqueeze(2), 3, TOPK, E_N), ALU.mult))
                st(v.tensor_reduce(slot_gate[:, t:t + 3, :], match[:, :, :, :], AX.X, ALU.add))

            v.wait_ge(q["column_turned"], 1)
            st(v.tensor_copy(column[0:E_N, :], ps[0:E_N, 7, 0:2]))
            st(v.tensor_copy(k.end_tab[0:1, :], bend[0:1, :]))
            v.tensor_scalar(passed_end[0:E_N, :], iota_f[0:E_N, :], column[0:E_N, 0:1], None, ALU.is_ge).then_inc(q["steps_ready"], 1)
            v.wait_ge(q["zeros_stored"], 16 * 11)
            for t in range(NT):
                if t >= 2:
                    v.wait_ge(q["placed"], t - 1)
                lanes, blks = at_lane[t % 2], at_blk[t % 2]
                v.tensor_tensor(lanes[:, :, :], bcast(lane[:, t, :].unsqueeze(2), TOPK, P), bcast(iota_f[:, 0:P].unsqueeze(1), TOPK, P), ALU.is_equal)
                st(v.tensor_tensor(blks[:, :, 0, :], bcast(blk[:, t, :].unsqueeze(2), TOPK, NBLK), bcast(iota_f.unsqueeze(1), TOPK, NBLK), ALU.is_equal))
                v.tensor_tensor(blks[:, :, 1, :], blks[:, :, 0, :], bcast(slot_gate[:, t, :].unsqueeze(2), TOPK, NBLK), ALU.mult)
                st(v.tensor_scalar(blks[:, :, 0, :], blks[:, :, 0, :], tok[:, t:t + 1], None, ALU.mult))
                v.sem_inc(q["lanes_ready"], 1)
            v.wait_ge(q["stepped"], 1)
            v.tensor_copy(k.expert_tab[0:1, :], ps[0:1, 7, 0:NBLK])
            v.tensor_copy(k.offset_tab[0:1, :], ps[0:1, 7, NBLK:2 * NBLK])
            v.wait_ge(q["placed"], NT)
            st(v.tensor_scalar(empty[:, :], ps[:, 6, 0:NBLK], 0.0, tok[:, NT:NT + 1], ALU.is_equal, ALU.mult))
            v.scalar_tensor_tensor(k.token_idx[:, :], ps[:, 6, 0:NBLK], -1.0, empty[:, :], ALU.add, ALU.add)
            v.tensor_copy(k.token_gate[:, :], ps[:, 6, NBLK:2 * NBLK])


def experts(k):
    nc, a, ps = k.nc, k.a, k.ps
    w = Area(k.big[:, NW * SLOT + k.moe_rest:])
    x_rows, xT = w.take(2, D), w.take(2, KT, P)
    sg, hid, hidT = w.take(2, FF), w.take(2, FF), w.take(2, 2, P)
    y_out = w.take(2, D)
    idx_in, idx_out = w.take(2).bitcast(mybir.dt.int32), w.take(2).bitcast(mybir.dt.int32)
    DOWN = 2 * KT * FF
    weights_loaded = [k.sem(f"ex_weights_loaded{s}") for s in range(NW)]
    weights_ready = k.sem("ex_weights_ready")
    gathered = [k.sem(f"ex_gathered{u}") for u in range(2)]
    added = k.sem("ex_added")
    x_turned, x_by_act, x_by_dve, up_done, silu_done, hid_done, hid_turned, hid_copied, down_done, y_by_act, y_by_dve = (
        k.sem("ex_" + x) for x in ("x_turned", "x_by_act", "x_by_dve", "up_done", "silu_done", "hid_done", "hid_turned",
                                   "hid_copied", "down_done", "y_by_act", "y_by_dve"))
    idx_in_ready, idx_out_ready, passed, sp_passed = (k.sem("ex_" + x) for x in ("idx_in_ready", "idx_out_ready", "passed", "sp_passed"))

    def over_ranges(eng, run):
        total = eng.value_load(k.end_tab[0:1, E_N - 1:E_N], min_val=1, max_val=NBLK)
        run(*RANGES[0])
        for first, last in RANGES[1:]:
            with eng.If(total > first):
                run(first, last)

    with nc.Block() as block:
        @block.sync
        def _(sp):
            def load(e, s):
                w_s = k.ring[:, s * SLOT:(s + 1) * SLOT]
                up = w_s[:, 0:DOWN].rearrange("p (k g f) -> p k g f", g=2, f=FF)
                for g, name in enumerate(("exp_w_gate", "exp_w_up")):
                    sp.dma_start(up[:, :, g, :], a[name][0, bass.ds(e, 1)].rearrange("e (k p) f -> p (e k) f", p=P))\
                      .then_inc(weights_loaded[s], 16)
                sp.dma_start(w_s[:, DOWN:SLOT].rearrange("p (k d) -> p k d", d=D),
                             a["exp_w_down"][0, bass.ds(e, 1)].rearrange("e (k p) d -> p (e k) d", p=P))\
                  .then_inc(weights_loaded[s], 16)

            for e in range(NW):
                load(e, e)
            for e in range(NW - 1):
                sp.wait_ge(weights_loaded[e], 48)
                sp.sem_inc(weights_ready, 1)
            with sp.Fori(0, (E_N - NW) // NW) as i:
                for s in range(NW):
                    sp.wait_ge(weights_loaded[(s - 1) % NW], (i + (1 if s == 0 else 2)) * 48)
                    sp.sem_inc(weights_ready, 1)
                    before = sp.value_load(k.end_tab[0:1, bass.ds(i * NW + s, 1)], min_val=1, max_val=NBLK)
                    wait_before_addressed(sp, down_done, before, sp_passed)
                    load(i * NW + (NW + s), s)
            for e in range(NW + (E_N - NW) // NW * NW, E_N):
                sp.wait_ge(weights_loaded[(e - 1) % NW], ((e - 1) // NW + 1) * 48)
                sp.sem_inc(weights_ready, 1)
                before = sp.value_load(k.end_tab[0:1, e - NW:e - NW + 1], min_val=1, max_val=NBLK)
                wait_before_addressed(sp, down_done, before, sp_passed)
                load(e, e % NW)
            sp.wait_ge(weights_loaded[(E_N - 1) % NW], ((E_N - 1) // NW + 1) * 48)
            sp.sem_inc(weights_ready, 1)

        @block.gpsimd
        def _(g):
            def gather(n, u):
                if not (isinstance(n, int) and n < 2):
                    g.wait_ge(x_turned, n - 1)
                    g.sem_inc(passed, 1)
                g.tensor_copy(idx_in[:, u:u + 1], k.token_idx[:, bass.ds(n, 1)]).then_inc(idx_in_ready, 1)
                g.wait_ge(idx_in_ready, n + 1)
                g.sem_inc(passed, 1)
                g.indirect_dma_start(out=x_rows[:, u, :], out_offset=None, in_=k.u_rows,
                                     in_offset=bass.IndirectOffsetOnAxis(idx_in[:, u:u + 1], 0)).then_inc(gathered[u], 16)

            def add(n, u):
                if not (isinstance(n, int) and n == 0):
                    g.wait_ge(added, n * 16)
                    g.sem_inc(passed, 1)
                g.tensor_copy(idx_out[:, u:u + 1], k.token_idx[:, bass.ds(n, 1)]).then_inc(idx_out_ready, 1)
                g.wait_ge(idx_out_ready, n + 1)
                g.sem_inc(passed, 1)
                g.wait_ge(y_by_act, n + 2)
                g.sem_inc(passed, 1)
                g.wait_ge(y_by_dve, n + 2)
                g.sem_inc(passed, 1)
                g.indirect_dma_start(out=k.y_rows, out_offset=bass.IndirectOffsetOnAxis(idx_out[:, u:u + 1], 0),
                                     in_=y_out[:, u, :], in_offset=None, compute_op=ALU.add).then_inc(added, 16)

            def run(first, last):
                for n in range(3):
                    gather(first + n, n % 2)
                for n in range(2):
                    gather(first + n + 3, (n + 1) % 2)
                    add(first + n, n)
                with g.Fori(1, (last - first) // 2 - 2) as j:
                    for r in range(2):
                        gather(j * 2 + (first + 3 + r), (1 + r) % 2)
                        add(j * 2 + (first + r), r)
                gather(last - 1, 1)
                for n in range(last - 4, last):
                    add(n, n % 2)
                g.wait_ge(added, 16 * last)
            over_ranges(g, run)

        def offset_of(pe, n):
            return pe.value_load(k.offset_tab[0:1, bass.ds(n, 1)], min_val=0, max_val=(NW - 1) * SLOT)

        @block.tensor
        def _(pe):
            def turn_x(n, u, half):
                pe.wait_ge(gathered[u], (half + 1) * 16)
                if not (isinstance(n, int) and n == 0):
                    pe.wait_ge(x_by_act, n)
                    pe.wait_ge(x_by_dve, n)
                for j in range(KT):
                    ins = pe.transpose(ps[:, j // 4, (j % 4) * P:(j % 4 + 1) * P], x_rows[:, u, j * P:(j + 1) * P], k.ident[:, :])
                ins.then_inc(x_turned, 1)

            def up(n, u):
                e = pe.value_load(k.expert_tab[0:1, bass.ds(n, 1)], min_val=0, max_val=E_N - 1)
                off = offset_of(pe, n)
                pe.wait_ge(x_by_act, n + 1)
                pe.wait_ge(x_by_dve, n + 1)
                pe.wait_ge(weights_ready, e + 1)
                for j in range(KT):
                    ins = pe.matmul(ps[:, 2 + u, :], xT[:, u, j, :], k.big[:, bass.ds(off + j * (2 * FF), 2 * FF)],
                                    start=(j == 0), stop=(j == KT - 1))
                ins.then_inc(up_done, 1)

            def down(n, u):
                off = offset_of(pe, n)
                pe.wait_ge(hid_copied, n + 1)
                pe.wait_ge(y_by_act, n + 1)
                pe.wait_ge(y_by_dve, n + 1)
                for half in range(2):
                    for j in range(2):
                        ins = pe.matmul(ps[:, 5 + half, :], hidT[:, u, j, :], k.big[:, bass.ds(off + (DOWN + j * D + half * 512), 512)],
                                        start=(j == 0), stop=(j == 1))
                ins.then_inc(down_done, 1)

            def turn_hid(n, u):
                pe.wait_ge(hid_done, n + 1)
                if not (isinstance(n, int) and n == 0):
                    pe.wait_ge(hid_copied, n)
                for j in range(2):
                    ins = pe.transpose(ps[:, 4, j * P:(j + 1) * P], hid[:, u, j * P:(j + 1) * P], k.ident[:, :])
                ins.then_inc(hid_turned, 1)

            def run(first, last):
                turn_x(first, 0, first // 2)
                up(first, 0)
                turn_x(first + 1, 1, first // 2)
                turn_hid(first, 0)
                with pe.Fori(0, (last - first) // 2 - 1) as j:
                    for r in range(2):
                        n, u = j * 2 + (first + 1 + r), (1 + r) % 2
                        up(n, u)
                        turn_x(j * 2 + (first + 2 + r), 1 - u, j + (first // 2 + 1))
                        down(j * 2 + (first + r), 1 - u)
                        turn_hid(n, u)
                up(last - 1, 1)
                down(last - 2, 0)
                turn_hid(last - 1, 1)
                down(last - 1, 1)
            over_ranges(pe, run)

        @block.scalar
        def _(act):
            def copy_x(n, u):
                act.wait_ge(x_turned, n + 1)
                act.activation(xT[:, u, 0:4, :].rearrange("p a b -> p (a b)"), ps[:, 0, :], ACT.Copy).then_inc(x_by_act, 1)

            def silu(n, u):
                act.wait_ge(up_done, n + 1)
                act.activation(sg[:, u, :], ps[:, 2 + u, 0:FF], ACT.Silu).then_inc(silu_done, 1)

            def copy_y(n, u):
                act.wait_ge(down_done, n + 1)
                if not (isinstance(n, int) and n < 2):
                    act.wait_ge(added, (n - 1) * 16)
                act.activation(y_out[:, u, 0:512], ps[:, 5, :], ACT.Copy).then_inc(y_by_act, 1)

            def copy_hid(n, u):
                act.wait_ge(hid_turned, n + 1)
                act.activation(hidT[:, u, :, :].rearrange("p a b -> p (a b)"), ps[:, 4, 0:FF], ACT.Copy).then_inc(hid_copied, 1)

            act.sem_inc(y_by_act, 1)

            def run(first, last):
                copy_x(first, 0)
                silu(first, 0)
                copy_x(first + 1, 1)
                copy_hid(first, 0)

                def step(n, u):
                    silu(n, u)
                    copy_x(n + 1, 1 - u)
                    copy_y(n - 1, 1 - u)
                    copy_hid(n, u)
                step(first + 1, 1)
                step(first + 2, 0)
                with act.Fori(1, (last - first) // 2 - 1) as j:
                    for r in range(2):
                        step(j * 2 + (first + 1 + r), (1 + r) % 2)
                silu(last - 1, 1)
                copy_y(last - 2, 0)
                copy_hid(last - 1, 1)
                copy_y(last - 1, 1)
            over_ranges(act, run)

        @block.vector
        def _(v):
            def copy_x(n, u):
                v.wait_ge(x_turned, n + 1)
                v.tensor_copy(xT[:, u, 4:8, :].rearrange("p a b -> p (a b)"), ps[:, 1, :]).then_inc(x_by_dve, 1)

            def hidden(n, u):
                v.wait_ge(silu_done, n + 1)
                v.scalar_tensor_tensor(hid[:, u, :], sg[:, u, :], k.token_gate[:, bass.ds(n, 1)], ps[:, 2 + u, FF:2 * FF],
                                       ALU.mult, ALU.mult).then_inc(hid_done, 1)

            def copy_y(n, u):
                v.wait_ge(down_done, n + 1)
                if not (isinstance(n, int) and n < 2):
                    v.wait_ge(added, (n - 1) * 16)
                v.tensor_copy(y_out[:, u, 512:D], ps[:, 6, :]).then_inc(y_by_dve, 1)

            add_shared(v, k, Steps(v, k.sem("ex_shared_step")))
            v.sem_inc(y_by_dve, 1)

            def run(first, last):
                copy_x(first, 0)
                hidden(first, 0)
                copy_x(first + 1, 1)

                def step(n, u):
                    hidden(n, u)
                    copy_x(n + 1, 1 - u)
                    copy_y(n - 1, 1 - u)
                step(first + 1, 1)
                step(first + 2, 0)
                with v.Fori(1, (last - first) // 2 - 1) as j:
                    for r in range(2):
                        step(j * 2 + (first + 1 + r), (1 + r) % 2)
                hidden(last - 1, 1)
                copy_y(last - 2, 0)
                copy_y(last - 1, 1)
            over_ranges(v, run)


def add_shared(v, k, st):
    for m in range(KT):
        gate = k.mod[:, 5 * KT + m, :]
        x = k.xT[:, m, :]
        v.scalar_tensor_tensor(x[:, 0:SEQ], k.hT[:, m, 0:SEQ], gate[:, 0:1], x[:, 0:SEQ], ALU.mult, ALU.add)
    ys, xs = (z[:, :, SEQ:T].rearrange("p k (s l) -> p k s l", l=SL) for z in (k.hT, k.xT))
    st(v.tensor_tensor(ys, ys, bcast(k.mod[:, 5 * KT:6 * KT, 1:NSEQ].unsqueeze(3), KT, SB, SL), ALU.mult))
    st(v.tensor_tensor(xs, xs, ys, ALU.add))


def finish(k):
    nc, a, ps = k.nc, k.a, k.ps
    w = Area(k.big[:, :])
    rows, out, squares = w.take(NT, D), w.take(3, D), w.take(2, D)
    rows_of = w.take(3, D)
    spread = [w.take(KT, P), w.take(KT, NS), w.take(KT, P)]
    total, eps = w.take(NT), w.take(1)
    loaded, stored = [k.sem(f"fi_loaded{t}") for t in range(NT)], [k.sem(f"fi_stored{u}") for u in range(3)]
    spread_ready, spread_turned, rows_ready, turned, summed, scaled, rooted, finished, eps_ready, dstep = (
        k.sem("fi_" + x) for x in ("spread_ready", "spread_turned", "rows_ready", "turned", "summed", "scaled", "rooted",
                                   "finished", "eps_ready", "dve_step"))

    def banks(t):
        return 6 if t % 2 == 0 else 0

    with nc.Block() as block:
        @block.sync
        def _(sp):
            for t in range(NT):
                n = tokens_of(t)
                sp.dma_start(rows[0:n, t, :], k.y_rows[t * P:t * P + n, :]).then_inc(loaded[t], 16)
            for t in range(NT):
                sp.wait_ge(finished, t + 1)
                if t < 8:
                    sp.dma_start(a["y_prompt"][0, t * P:(t + 1) * P, :], out[:, t % 3, :]).then_inc(stored[t % 3], 16)
                else:
                    sp.dma_start(a["y_sample"].rearrange("s l d -> (s l) d"), out[0:NS, t % 3, :]).then_inc(stored[t % 3], 16)
            for u in range(3):
                sp.wait_ge(stored[u], 16 * (NT // 3))

        @block.gpsimd
        def _(g):
            g.memset(eps[:, :], EPS).then_inc(eps_ready, 1)
            g.tensor_copy(spread[0][:, :, :], bcast(k.mod[:, 5 * KT:6 * KT, 0:1], KT, P)).then_inc(spread_ready, 1)
            g.tensor_copy(spread[1].rearrange("p k (s l) -> p k s l", l=SL),
                          bcast(k.mod[:, 5 * KT:6 * KT, 1:NSEQ].unsqueeze(3), KT, SB, SL)).then_inc(spread_ready, 1)
            c0 = PRM["final_norm_w"]
            g.tensor_copy(spread[2][:, :, :], bcast(k.prm[:, c0:c0 + KT].unsqueeze(2), KT, P)).then_inc(spread_ready, 1)

        @block.tensor
        def _(pe):
            for x in range(3):
                n = NS if x == 1 else P
                pe.wait_ge(spread_ready, x + 1)
                for j in range(KT):
                    ins = pe.transpose(ps[0:n, 2 * x + j // 4, (j % 4) * P:(j % 4 + 1) * P], spread[x][:, j, :], k.ident[:, :])
                ins.then_inc(spread_turned, 1)
            for t in range(NT):
                n = tokens_of(t)
                if t == 1:
                    pe.wait_ge(rows_ready, 1)
                if t >= 2:
                    pe.wait_ge(summed, t - 1)
                for j in range(KT):
                    ins = pe.transpose(ps[0:n, banks(t) + j // 4, (j % 4) * P:(j % 4 + 1) * P],
                                       k.xT[:, j, t * P:t * P + n], k.ident[:, :])
                ins.then_inc(turned, 1)

        @block.scalar
        def _(act):
            for x in range(3):
                n = NS if x == 1 else P
                act.wait_ge(spread_turned, x + 1)
                act.activation(rows_of[0:n, x, :].rearrange("p (b c) -> p b c", b=2), ps[0:n, 2 * x:2 * x + 2, :], ACT.Copy)\
                   .then_inc(rows_ready, 1)
            act.wait_ge(eps_ready, 1)
            for t in range(NT):
                n = tokens_of(t)
                act.wait_ge(summed, t + 1)
                act.activation(squares[0:n, t % 2, :], rows[0:n, t, :], ACT.Square, accum_out=total[0:n, t:t + 1]).then_inc(scaled, 1)
                act.wait_ge(scaled, t + 1)
                act.activation(total[0:n, t:t + 1], total[0:n, t:t + 1], ACT.Sqrt, scale=1.0 / D, bias=eps[0:n, :]).then_inc(rooted, 1)

        @block.vector
        def _(v):
            st = Steps(v, dstep)

            def normalise(t):
                n = tokens_of(t)
                v.wait_ge(rooted, t + 1)
                st(v.reciprocal(total[0:n, t:t + 1], total[0:n, t:t + 1]))
                if t >= 3:
                    v.wait_ge(stored[t % 3], 16 * (t // 3))
                v.scalar_tensor_tensor(out[0:n, t % 3, :], rows[0:n, t, :], total[0:n, t:t + 1], rows_of[0:n, 2, :],
                                       ALU.mult, ALU.mult).then_inc(finished, 1)
            for t in range(NT):
                n = tokens_of(t)
                v.wait_ge(loaded[t], 16)
                v.wait_ge(rows_ready, 1 if t < 8 else 2)
                st(v.tensor_tensor(rows[0:n, t, :], rows[0:n, t, :], rows_of[0:n, t // 8, :], ALU.mult))
                v.wait_ge(turned, t + 1)
                r = rows[0:n, t, :].rearrange("p (b c) -> p b c", b=2)
                v.tensor_tensor(r, r, ps[0:n, banks(t):banks(t) + 2, :], ALU.add).then_inc(summed, 1)
                if t == 1:
                    v.wait_ge(rows_ready, 3)
                if t:
                    normalise(t - 1)
            normalise(NT - 1)


def step_program(nc, a):
    with ExitStack() as ctx:
        k = Core(nc, ctx, a)
        setup(k)
        delta_project(k)
        delta_rows(k)
        delta_rule(k)
        gated_norm(k, "dn", k.qkv[:, 2 * H:3 * H, :], k.oT[:, 0:H, :], k.column("dn_norm_w"), Area(k.work[:, 0:2 * H * T]))
        gla_project(k)
        gla_rule(k)
        k.fresh_semaphores()
        conformer_and_merge(k)
        project_out(k)
        k.fresh_semaphores()
        plan_moe(k)
        route(k)
        experts(k)
        finish(k)
        k.fresh_semaphores()


INS = ["x_prompt", "x_sample", "state_delta", "state_delta_conv", "state_gla", "state_conv", "c_prompt", "c_sample",
       "ada_w", "ada_b", "norm_mix_w", "w_in", "dn_conv_w", "dn_A_log", "dn_dt_bias", "dn_norm_w", "gla_gate_w",
       "gla_gate_b", "gla_norm_w", "conf_dw_w", "conf_dw_b", "conf_ln_w", "conf_ln_b", "w_branch", "w_out",
       "norm_ffn_w", "router_w", "router_bias", "exp_w_gate", "exp_w_up", "exp_w_down", "sh_w_gate", "sh_w_up",
       "sh_w_down", "final_norm_w"]


def kernel(**inputs):
    import numpy as np
    import concourse.bacc as bacc
    from concourse.bass_utils import run_bass_kernel_spmd

    nc = bacc.Bacc("TRN2", target_bir_lowering=False, num_devices=1)
    arrays, a = {}, {}
    for name in INS:
        x = np.ascontiguousarray(inputs[name])
        arrays[f"in_{name}"] = x
        a[name] = nc.dram_tensor(f"in_{name}", x.shape, mybir.dt.from_np(x.dtype), kind="ExternalInput").ap()
    for name, shape in OUTS:
        a[name] = nc.dram_tensor(f"out_{name}", shape, F32, kind="ExternalOutput").ap()
    step_program(nc, a)
    r = run_bass_kernel_spmd(nc, [arrays], core_ids=[0])
    return tuple(r.results[0][f"out_{name}"] for name, _ in OUTS)
```
